# Optimizing a Trainium2 kernel written in Bass

```python
import math
import jax, jax.numpy as jnp
from jax import lax
import numpy as np

D_MODEL = 1024
BATCH = 1
SEQ = 512
DEPTH = 2
DEC_BATCH = 8
DEC_SEQ = 8
PAST_LEN = 256
PAGE_SIZE = 128

N_EVEN = (DEPTH + 1) // 2
N_ODD = DEPTH // 2
A_WIDTH = D_MODEL // 2
A_GROUP = 16
A_GROUPS = A_WIDTH // A_GROUP
A_STATE = 64
B_WIDTH = D_MODEL // 2
B_DK = 128
B_HEADS = B_WIDTH // B_DK
B_CHUNK = 64
D_MIX_AB = A_WIDTH + B_WIDTH
AB_COLS = A_WIDTH + 4 * B_WIDTH
C_HEADS = 8
C_HEAD_DIM = D_MODEL // C_HEADS // 2
C_VDIM = 2 * C_HEAD_DIM
C_COLS = 3 * C_HEADS * C_VDIM
Q_BLOCK = 128
REL_BUCKETS = 32
REL_MAX_DIST = 128
PEER_HEADS = 8
N_KEYS = 128
N_EXPERTS = N_KEYS * N_KEYS
PEER_TOPK = 16
PEER_QDIM = 256
PEER_BLOCK = 256
PLE_DIM = 256
EPS = 1e-6

kernel_name = 'hybrid_s5_hgrn2_diffattn_peer_step'

def rmsnorm(x, g):
    xf = x.astype(jnp.float32)
    y = xf * lax.rsqrt(jnp.mean(xf * xf, axis=-1, keepdims=True) + EPS)
    return (y * g.astype(jnp.float32)).astype(x.dtype)

def _cplx_combine(e1, e2):
    a1r, a1i, b1r, b1i = e1
    a2r, a2i, b2r, b2i = e2
    return (a1r * a2r - a1i * a2i,
            a1r * a2i + a1i * a2r,
            a2r * b1r - a2i * b1i + b2r,
            a2r * b1i + a2i * b1r + b2i)

def s5_mixer(u, h0_re, h0_im, a_re, a_im, log_dt, b_re, b_im, c_re, c_im, d, glu_w, glu_b):
    f32 = jnp.float32
    Bn, T, _ = u.shape
    uf = u.astype(f32).reshape(Bn, T, A_GROUPS, A_GROUP)
    a_re = a_re.astype(f32)
    a_im = a_im.astype(f32)
    b_re = b_re.astype(f32)
    b_im = b_im.astype(f32)
    dt = jnp.exp(log_dt.astype(f32))[:, None]
    mag = jnp.exp(a_re * dt)
    lb_re = mag * jnp.cos(a_im * dt)
    lb_im = mag * jnp.sin(a_im * dt)
    den = a_re * a_re + a_im * a_im
    coef_re = ((lb_re - 1.0) * a_re + lb_im * a_im) / den
    coef_im = (lb_im * a_re - (lb_re - 1.0) * a_im) / den
    bb_re = coef_re[..., None] * b_re - coef_im[..., None] * b_im
    bb_im = coef_re[..., None] * b_im + coef_im[..., None] * b_re
    x_re = jnp.einsum('gpc,btgc->btgp', bb_re, uf)
    x_im = jnp.einsum('gpc,btgc->btgp', bb_im, uf)
    ar = jnp.broadcast_to(lb_re, x_re.shape)
    ai = jnp.broadcast_to(lb_im, x_re.shape)
    cum_re, cum_im, s_re, s_im = lax.associative_scan(_cplx_combine, (ar, ai, x_re, x_im), axis=1)
    h0r = h0_re.astype(f32)[:, None]
    h0i = h0_im.astype(f32)[:, None]
    h_re = s_re + cum_re * h0r - cum_im * h0i
    h_im = s_im + cum_re * h0i + cum_im * h0r
    y = (jnp.einsum('gcp,btgp->btgc', c_re.astype(f32), h_re)
         - jnp.einsum('gcp,btgp->btgc', c_im.astype(f32), h_im)
         + d.astype(f32).reshape(A_GROUPS, A_GROUP) * uf)
    y = jax.nn.gelu(y.reshape(Bn, T, A_WIDTH))
    out = y * jax.nn.sigmoid(y @ glu_w.astype(f32) + glu_b.astype(f32))
    return out.astype(u.dtype), h_re[:, -1].astype(h0_re.dtype), h_im[:, -1].astype(h0_im.dtype)

def hgrn2_mixer(q, fpre, i, g, S0, lb, norm_g):
    f32 = jnp.float32
    Bn, T, _ = q.shape
    heads = lambda z: z.astype(f32).reshape(Bn, T, B_HEADS, B_DK)
    lbh = lb.astype(f32).reshape(B_HEADS, B_DK)
    f = lbh + (1.0 - lbh) * jax.nn.sigmoid(heads(fpre))
    logf = jnp.log(f)
    k = 1.0 - f
    qh = heads(q)
    vh = heads(i)
    L = math.gcd(T, B_CHUNK)
    nc = T // L
    to_chunks = lambda z: z.reshape(Bn, nc, L, B_HEADS, B_DK).transpose(1, 0, 3, 2, 4)
    causal = jnp.tril(jnp.ones((L, L), dtype=bool))

    def step(S, inp):
        qc, lfc, kc, vc = inp
        b = jnp.cumsum(lfc, axis=2)
        inter = jnp.einsum('bhtd,bhde->bhte', qc * jnp.exp(b), S)
        diff = b[:, :, :, None, :] - b[:, :, None, :, :]
        decay = jnp.exp(jnp.where(causal[:, :, None], diff, -jnp.inf))
        attn = jnp.einsum('bhtd,bhsd,bhtsd->bhts', qc, kc, decay)
        o = inter + jnp.einsum('bhts,bhse->bhte', attn, vc)
        bl = b[:, :, -1]
        S = jnp.exp(bl)[..., None] * S + jnp.einsum('bhsd,bhse->bhde', kc * jnp.exp(bl[:, :, None] - b), vc)
        return S, o

    S_T, o = lax.scan(step, S0.astype(f32), (to_chunks(qh), to_chunks(logf), to_chunks(k), to_chunks(vh)))
    o = o.transpose(1, 0, 3, 2, 4).reshape(Bn, T, B_HEADS, B_DK)
    o = rmsnorm(o, norm_g) * jax.nn.silu(heads(g))
    return o.reshape(Bn, T, B_WIDTH).astype(q.dtype), S_T.astype(S0.dtype)

def even_mixer(xn, j, s5_re0, s5_im0, S0, w):
    proj = xn @ w['w_in_ab'][j]
    u = proj[..., :A_WIDTH]
    q, fpre, i, g = jnp.split(proj[..., A_WIDTH:], 4, axis=-1)
    ya, hr, hi = s5_mixer(u, s5_re0, s5_im0, w['s5_a_re'][j], w['s5_a_im'][j], w['s5_log_dt'][j],
                          w['s5_b_re'][j], w['s5_b_im'][j], w['s5_c_re'][j], w['s5_c_im'][j],
                          w['s5_d'][j], w['s5_glu_w'][j], w['s5_glu_b'][j])
    lb = jnp.cumsum(jax.nn.softmax(w['hgrn_lower_bounds'].astype(jnp.float32), axis=0), axis=0)[j]
    yb, S = hgrn2_mixer(q, fpre, i, g, S0, lb, w['hgrn_norm'][j])
    out = jnp.concatenate([ya, yb.astype(ya.dtype)], axis=-1) @ w['w_out_ab'][j]
    return out, hr, hi, S

def rel_bucket(n):
    max_exact = REL_BUCKETS // 2
    nf = jnp.maximum(n, 1).astype(jnp.float32)
    large = max_exact + (jnp.log(nf / max_exact) / math.log(REL_MAX_DIST / max_exact)
                         * (REL_BUCKETS - max_exact)).astype(jnp.int32)
    large = jnp.minimum(large, REL_BUCKETS - 1)
    return jnp.where(n < max_exact, n, large)

def diff_attention(q, q_pos, segs, lam, rel_bias):
    f32 = jnp.float32
    Bn, Tq = q.shape[:2]
    blk = math.gcd(Tq, Q_BLOCK)
    nb = Tq // blk
    scale = C_HEAD_DIM ** -0.5
    qb = jnp.moveaxis(q.reshape(Bn, nb, blk, C_HEADS, 2, C_HEAD_DIM), 1, 0)
    pb = q_pos.reshape(nb, blk)
    k_pos = jnp.concatenate([pos for _, _, pos in segs])
    split_at = np.cumsum([pos.shape[0] for _, _, pos in segs])[:-1].tolist()
    bias_tab = rel_bias.astype(f32)

    def one(args):
        qi, pi = args
        s = jnp.concatenate([jnp.einsum('bqhcd,bkhcd->bhcqk', qi, kk) for kk, _, _ in segs], axis=-1)
        s = s.astype(f32) * scale
        dist = pi[:, None] - k_pos[None, :]
        bias = jnp.take(bias_tab, rel_bucket(jnp.maximum(dist, 0)), axis=0)
        s = s + jnp.transpose(bias, (2, 0, 1))[:, None]
        s = jnp.where(dist >= 0, s, -jnp.inf)
        pr = jax.nn.softmax(s, axis=-1)
        a = pr[:, :, 0] - lam * pr[:, :, 1]
        parts = jnp.split(a, split_at, axis=-1)
        return sum(jnp.einsum('bhqk,bkhe->bqhe', ap.astype(vv.dtype), vv) for ap, (_, vv, _) in zip(parts, segs))

    o = lax.map(one, (qb, pb))
    return jnp.moveaxis(o, 0, 1).reshape(Bn, Tq, C_HEADS, C_VDIM)

def odd_mixer(xn, j, layer, cache_k, cache_v, page_table, w):
    f32 = jnp.float32
    Bn, T, _ = xn.shape
    proj = xn @ w['w_in_c'][j]
    qz, kz, vz = jnp.split(proj, 3, axis=-1)
    q = rmsnorm(qz.reshape(Bn, T, C_HEADS, 2, C_HEAD_DIM), w['c_q_norm'][j])
    k = rmsnorm(kz.reshape(Bn, T, C_HEADS, 2, C_HEAD_DIM), w['c_k_norm'][j])
    v = vz.reshape(Bn, T, C_HEADS, C_VDIM)
    if page_table is None:
        past_len = 0
        segs = []
    else:
        pk = cache_k[j, page_table]
        past_len = pk.shape[1] * pk.shape[2]
        pk = pk.reshape(Bn, past_len, C_HEADS, 2, C_HEAD_DIM)
        pv = cache_v[j, page_table].reshape(Bn, past_len, C_HEADS, C_VDIM)
        segs = [(pk, pv, jnp.arange(past_len))]
    q_pos = past_len + jnp.arange(T)
    segs = segs + [(k, v, q_pos)]
    lam_init = 0.8 - 0.6 * math.exp(-0.3 * layer)
    lam = (jnp.exp(jnp.sum(w['c_lam_q1'][j].astype(f32) * w['c_lam_k1'][j].astype(f32)))
           - jnp.exp(jnp.sum(w['c_lam_q2'][j].astype(f32) * w['c_lam_k2'][j].astype(f32))) + lam_init)
    o = diff_attention(q, q_pos, segs, lam, w['rel_bias'])
    o = rmsnorm(o, w['c_subln'][j]) * (1.0 - lam_init)
    out = o.reshape(Bn, T, C_HEADS * C_VDIM) @ w['w_out_c'][j]
    return out, k.reshape(Bn, T, C_HEADS, 2 * C_HEAD_DIM), v

def peer(xn, wq, keys, u_tab, v_tab):
    Bn, T, D = xn.shape
    N = Bn * T
    blk = math.gcd(N, PEER_BLOCK)
    xb = xn.reshape(N // blk, blk, D)

    def one(xi):
        q = (xi @ wq).reshape(blk, PEER_HEADS, 2, PEER_QDIM // 2)
        s = jnp.einsum('nhcd,hckd->nhck', q, keys).astype(jnp.float32)
        top_s, top_i = lax.top_k(s, PEER_TOPK)
        cand_s = (top_s[:, :, 0, :, None] + top_s[:, :, 1, None, :]).reshape(blk, PEER_HEADS, PEER_TOPK * PEER_TOPK)
        cand_i = (top_i[:, :, 0, :, None] * N_KEYS + top_i[:, :, 1, None, :]).reshape(blk, PEER_HEADS, PEER_TOPK * PEER_TOPK)
        sel_s, sel_pos = lax.top_k(cand_s, PEER_TOPK)
        idx = jnp.take_along_axis(cand_i, sel_pos, axis=-1)
        gate = jax.nn.softmax(sel_s, axis=-1)
        u = jnp.take(u_tab, idx, axis=0)
        act = jax.nn.gelu(jnp.einsum('nhkd,nd->nhk', u, xi).astype(jnp.float32))
        wgt = (gate * act).astype(xi.dtype)
        return jnp.einsum('nhk,nhkd->nd', wgt, jnp.take(v_tab, idx, axis=0))

    return lax.map(one, xb).reshape(Bn, T, D)

def run_group(x, p, s5_re0, s5_im0, hgrn0, cache_k, cache_v, page_table, w):
    h = x
    s5_re, s5_im, hg, ks, vs = [], [], [], [], []
    for layer in range(DEPTH):
        j = layer // 2
        xn = rmsnorm(h, w['norm_mix'][layer])
        if layer % 2 == 0:
            mix, hr, hi, S = even_mixer(xn, j, s5_re0[j], s5_im0[j], hgrn0[j], w)
            s5_re.append(hr)
            s5_im.append(hi)
            hg.append(S)
        else:
            mix, kr, vr = odd_mixer(xn, j, layer, cache_k, cache_v, page_table, w)
            ks.append(kr)
            vs.append(vr)
        h = h + mix
        h = h + peer(rmsnorm(h, w['norm_ffn'][layer]), w['peer_wq'][layer], w['peer_keys'][layer],
                     w['peer_u'][layer], w['peer_v'][layer])
        gate = jax.nn.sigmoid(rmsnorm(h, w['norm_ple'][layer]) @ w['ple_gate'][layer])
        h = h + (p[layer] @ w['ple_proj'][layer]) * gate
    return h, jnp.stack(s5_re), jnp.stack(s5_im), jnp.stack(hg), jnp.stack(ks), jnp.stack(vs)

def setup_inputs(seed: int = 0) -> dict:
    key = jax.random.key(seed)
    keys = iter(jax.random.split(key, 64))
    f32 = jnp.float32

    def nrm(shape, scale):
        return jax.random.normal(next(keys), shape, f32) * scale

    def gain(shape):
        return 1.0 + nrm(shape, 0.02)

    n_pages = PAST_LEN // PAGE_SIZE
    n_used = DEC_BATCH * n_pages
    n_pool = n_used + n_used // 4
    page_table = jax.random.permutation(next(keys), n_pool)[:n_used].reshape(DEC_BATCH, n_pages).astype(jnp.int32)
    n_idx = jnp.arange(A_STATE, dtype=f32)
    log_dt = jax.random.uniform(next(keys), (N_EVEN, A_GROUPS), f32, math.log(1e-3), math.log(1e-1))
    return {
        'x_prompt': nrm((BATCH, SEQ, D_MODEL), 1.0),
        'x_sample': nrm((DEC_BATCH, DEC_SEQ, D_MODEL), 1.0),
        'p_prompt': nrm((DEPTH, BATCH, SEQ, PLE_DIM), 1.0),
        'p_sample': nrm((DEPTH, DEC_BATCH, DEC_SEQ, PLE_DIM), 1.0),
        'state_s5_re': nrm((N_EVEN, DEC_BATCH, A_GROUPS, A_STATE), 0.5),
        'state_s5_im': nrm((N_EVEN, DEC_BATCH, A_GROUPS, A_STATE), 0.5),
        'state_hgrn': nrm((N_EVEN, DEC_BATCH, B_HEADS, B_DK, B_DK), 0.5),
        'cache_k': nrm((N_ODD, n_pool, PAGE_SIZE, C_HEADS, 2 * C_HEAD_DIM), 1.0),
        'cache_v': nrm((N_ODD, n_pool, PAGE_SIZE, C_HEADS, C_VDIM), 1.0),
        'page_table': page_table,
        'norm_mix': gain((DEPTH, D_MODEL)),
        'norm_ffn': gain((DEPTH, D_MODEL)),
        'norm_ple': gain((DEPTH, D_MODEL)),
        'w_in_ab': nrm((N_EVEN, D_MODEL, AB_COLS), D_MODEL ** -0.5),
        'w_out_ab': nrm((N_EVEN, D_MIX_AB, D_MODEL), D_MIX_AB ** -0.5),
        's5_a_re': -0.5 + nrm((N_EVEN, A_GROUPS, A_STATE), 0.01),
        's5_a_im': math.pi * n_idx + nrm((N_EVEN, A_GROUPS, A_STATE), 0.01),
        's5_log_dt': log_dt,
        's5_b_re': nrm((N_EVEN, A_GROUPS, A_STATE, A_GROUP), (2 * A_GROUP) ** -0.5),
        's5_b_im': nrm((N_EVEN, A_GROUPS, A_STATE, A_GROUP), (2 * A_GROUP) ** -0.5),
        's5_c_re': nrm((N_EVEN, A_GROUPS, A_GROUP, A_STATE), A_STATE ** -0.5),
        's5_c_im': nrm((N_EVEN, A_GROUPS, A_GROUP, A_STATE), A_STATE ** -0.5),
        's5_d': nrm((N_EVEN, A_WIDTH), 0.5),
        's5_glu_w': nrm((N_EVEN, A_WIDTH, A_WIDTH), A_WIDTH ** -0.5),
        's5_glu_b': nrm((N_EVEN, A_WIDTH), 0.01),
        'hgrn_lower_bounds': nrm((N_EVEN + 1, B_WIDTH), 0.1),
        'hgrn_norm': gain((N_EVEN, B_DK)),
        'w_in_c': nrm((N_ODD, D_MODEL, C_COLS), D_MODEL ** -0.5),
        'w_out_c': nrm((N_ODD, C_HEADS * C_VDIM, D_MODEL), (C_HEADS * C_VDIM) ** -0.5),
        'c_q_norm': gain((N_ODD, 2, C_HEAD_DIM)),
        'c_k_norm': gain((N_ODD, 2, C_HEAD_DIM)),
        'c_lam_q1': nrm((N_ODD, C_HEAD_DIM), 0.1),
        'c_lam_k1': nrm((N_ODD, C_HEAD_DIM), 0.1),
        'c_lam_q2': nrm((N_ODD, C_HEAD_DIM), 0.1),
        'c_lam_k2': nrm((N_ODD, C_HEAD_DIM), 0.1),
        'c_subln': gain((N_ODD, C_VDIM)),
        'rel_bias': nrm((REL_BUCKETS, C_HEADS), 0.5),
        'peer_wq': nrm((DEPTH, D_MODEL, PEER_HEADS * PEER_QDIM), D_MODEL ** -0.5),
        'peer_keys': nrm((DEPTH, PEER_HEADS, 2, N_KEYS, PEER_QDIM // 2), (PEER_QDIM // 2) ** -0.5),
        'peer_u': nrm((DEPTH, N_EXPERTS, D_MODEL), D_MODEL ** -0.5),
        'peer_v': nrm((DEPTH, N_EXPERTS, D_MODEL), 0.3),
        'ple_proj': nrm((DEPTH, PLE_DIM, D_MODEL), PLE_DIM ** -0.5),
        'ple_gate': nrm((DEPTH, D_MODEL, D_MODEL), D_MODEL ** -0.5),
    }

def reference(x_prompt, x_sample, p_prompt, p_sample, state_s5_re, state_s5_im, state_hgrn, cache_k, cache_v,
              page_table, norm_mix, norm_ffn, norm_ple, w_in_ab, w_out_ab, s5_a_re, s5_a_im, s5_log_dt,
              s5_b_re, s5_b_im, s5_c_re, s5_c_im, s5_d, s5_glu_w, s5_glu_b, hgrn_lower_bounds, hgrn_norm,
              w_in_c, w_out_c, c_q_norm, c_k_norm, c_lam_q1, c_lam_k1, c_lam_q2, c_lam_k2, c_subln, rel_bias,
              peer_wq, peer_keys, peer_u, peer_v, ple_proj, ple_gate):
    w = dict(norm_mix=norm_mix, norm_ffn=norm_ffn, norm_ple=norm_ple, w_in_ab=w_in_ab, w_out_ab=w_out_ab,
             s5_a_re=s5_a_re, s5_a_im=s5_a_im, s5_log_dt=s5_log_dt, s5_b_re=s5_b_re, s5_b_im=s5_b_im,
             s5_c_re=s5_c_re, s5_c_im=s5_c_im, s5_d=s5_d, s5_glu_w=s5_glu_w, s5_glu_b=s5_glu_b,
             hgrn_lower_bounds=hgrn_lower_bounds, hgrn_norm=hgrn_norm, w_in_c=w_in_c, w_out_c=w_out_c,
             c_q_norm=c_q_norm, c_k_norm=c_k_norm, c_lam_q1=c_lam_q1, c_lam_k1=c_lam_k1, c_lam_q2=c_lam_q2,
             c_lam_k2=c_lam_k2, c_subln=c_subln, rel_bias=rel_bias, peer_wq=peer_wq, peer_keys=peer_keys,
             peer_u=peer_u, peer_v=peer_v, ple_proj=ple_proj, ple_gate=ple_gate)
    Bp = x_prompt.shape[0]
    z_s5 = jnp.zeros((N_EVEN, Bp, A_GROUPS, A_STATE), x_prompt.dtype)
    z_hg = jnp.zeros((N_EVEN, Bp, B_HEADS, B_DK, B_DK), x_prompt.dtype)
    y_prompt, s5r_p, s5i_p, hg_p, k_p, v_p = run_group(x_prompt, p_prompt, z_s5, z_s5, z_hg, None, None, None, w)
    y_sample, s5r_s, s5i_s, hg_s, k_s, v_s = run_group(x_sample, p_sample, state_s5_re, state_s5_im, state_hgrn,
                                                       cache_k, cache_v, page_table, w)
    return (y_prompt, y_sample, s5r_p, s5i_p, hg_p, k_p, v_p, s5r_s, s5i_s, hg_s, k_s, v_s)


_drawn_inputs = setup_inputs


def setup_inputs(seed=0):
    import zlib

    import numpy as np

    out = dict(_drawn_inputs(seed))
    spreads = {}
    factors = {'norm_ple': 6.675,
     's5_a_re': 4.194,
     's5_glu_b': 7.354,
     'hgrn_norm': 2.855,
     'c_q_norm': 3.658,
     'c_k_norm': 2.823,
     'c_lam_q1': 4.724,
     'c_lam_k1': 3.348,
     'c_subln': 4.148}
    for name, (base, spread) in spreads.items():
        noise = np.random.default_rng([zlib.crc32(name.encode()), seed]).standard_normal(out[name].shape)
        drawn = base * np.exp(spread * noise) if base else spread * noise
        out[name] = __import__('jax').numpy.asarray(drawn.astype(out[name].dtype))
    for name, factor in factors.items():
        out[name] = (out[name] * factor).astype(out[name].dtype)
    return out
```

```python
import math
from contextlib import ExitStack

import concourse.bass as bass
import concourse.mybir as mybir
import numpy as np

P = 128
D = 1024
DC = D // P
TP = 512
NB, TS = 8, 8
T = TP + NB * TS
HALF = T // 2
TPAD = 640
NT = TPAD // P
EPS = 1e-6
NEG = -1e30

F32 = mybir.dt.float32
U32 = mybir.dt.uint32
I32 = mybir.dt.int32
ALU = mybir.AluOpType
ACT = mybir.ActivationFunctionType
AX = mybir.AxisListType.X

S5_TILES = 16
SEG = TS + 1
L5 = TP + NB * SEG
BH = 4
CH = 64
NCH = TP // CH
CHD = 64
H = 8
PAST = 256
PAGE = 128
LAM_INIT = 0.8 - 0.6 * math.exp(-0.3 * 1)
BW = 640
PH = 8
PK = 16
TB = 32
NTB = T // TB
JB = 4
NJB = P // JB
N_SEL = 2 * NT
N_PRE = N_SEL + NTB * 2 // JB
BIG_ROUND = 1.5 * 2.0 ** 23


class Stage:

    def __init__(self, nc, name):
        self.nc, self.name, self.sems = nc, name, []
        self.ctx = ExitStack()

    def __enter__(self):
        self.ctx.__enter__()
        return self

    def __exit__(self, *exc):
        self.ctx.__exit__(*exc)
        if exc[0] is None and self.sems:
            self.nc.clear_and_free_semaphores(self.sems)
            self.nc.all_engine_barrier()

    def sem(self, name):
        self.sems.append(self.nc.alloc_semaphore(f"{self.name}_{name}"))
        return self.sems[-1]

    def sb(self, name, shape, dt=F32):
        return self.ctx.enter_context(self.nc.sbuf_tensor(f"{self.name}_{name}", shape, dt))

    def ps(self, name, shape, dt=F32):
        return self.ctx.enter_context(self.nc.psum_tensor(f"{self.name}_{name}", shape, dt))

    def block(self):
        return self.nc.Block()


def store(eng, dr, dst, src):
    dr["n_stored"] += 1
    return eng.dma_start(dst, src).then_inc(dr["stored"], 16)


def wait_apart(eng, sem, value, column):
    eng.wait_ge(sem, value)
    eng.tensor_tensor(column, column, column, ALU.mult)


def halves(ap, n=T):
    return ap.rearrange("p (a n) -> p a n", a=2)


def at(ap, i):
    return ap[:, bass.ds(i, 1)].rearrange("p a n -> p (a n)")


def paired(eng, count, body):
    for k in range(2):
        body(0, k, True)
    if count > 2:
        with eng.Fori(1, count // 2) as i:
            for k in range(2):
                body(i, k, False)


def looped(eng, count, body):
    body(0, True)
    with eng.Fori(1, count) as t:
        body(t, False)


def linear(nc, name, w_dram, n_in, n_out, rhs, evac_on, evac):
    with Stage(nc, name) as st:
        w = st.sb("w", [P, 2, n_in * P])
        acc = st.ps("acc", [P, 2, 2, 512])
        w_landed = [st.sem(f"w_landed{k}") for k in range(2)]
        multiplied = st.sem("multiplied")
        evacuated = st.sem("evacuated")
        with st.block() as block:

            @block.sync
            def _(sp):
                def load(i, k, first):
                    src = w_dram[bass.ds(i * 2 + k if first else sp.snap(i * 2 + k), 1)]
                    if not first:
                        sp.wait_ge(multiplied, i * 2 + k - 1)
                    sp.dma_start(w[:, k, :], src.rearrange("a p n -> p (a n)")).then_inc(w_landed[k], 16)

                paired(sp, n_out, load)

            @block.tensor
            def _(pe):
                def multiply(i, k, first):
                    pe.wait_ge(w_landed[k], i * 16 + 16)
                    if not first:
                        pe.wait_ge(evacuated, i * 2 + k - 1)
                    for c in range(n_in):
                        for a in range(2):
                            last = pe.matmul(acc[:, k, a, 0:HALF], w[:, k, c * P:(c + 1) * P],
                                             rhs[:, c, a * HALF:(a + 1) * HALF],
                                             start=(c == 0), stop=(c == n_in - 1))
                    last.then_inc(multiplied, 1)

                paired(pe, n_out, multiply)

            def take(eng):
                def one(i, k, first):
                    eng.wait_ge(multiplied, i * 2 + k + 1)
                    evac(eng, i * 2 + k, acc[:, k, :, 0:HALF]).then_inc(evacuated, 1)

                paired(eng, n_out, one)

            if evac_on == "act":
                block.scalar(take)
            else:
                block.vector(take)


def to_buffer(buf, first=0, func=ACT.Copy):
    def evac(eng, o, res):
        return eng.activation(halves(at(buf, o + first)), res, func)
    return evac


def add_to(buf):
    def evac(eng, o, res):
        dst = halves(at(buf, o))
        return eng.tensor_tensor(dst, dst, res, ALU.add)
    return evac


def rmsnorm(nc, name, x, out, gain, ones, eps):
    with Stage(nc, name) as st:
        sq = st.sb("sq", [P, DC, T])
        rstd = st.sb("rstd", [P, T])
        tot = st.ps("tot", [P, 2, 512])
        squared = st.sem("squared")
        summed = st.sem("summed")
        rooted = st.sem("rooted")
        with st.block() as block:

            @block.scalar
            def _(act):
                for c in range(DC):
                    act.activation(sq[:, c, :], x[:, c, :], ACT.Square).then_inc(squared, 1)
                act.wait_ge(summed, 1)
                act.activation(halves(rstd[:]), tot[:, :, 0:HALF], ACT.Sqrt, bias=eps, scale=1.0 / D)\
                   .then_inc(rooted, 1)

            @block.tensor
            def _(pe):
                for c in range(DC):
                    pe.wait_ge(squared, c + 1)
                    for a in range(2):
                        last = pe.matmul(tot[:, a, 0:HALF], ones, sq[:, c, a * HALF:(a + 1) * HALF],
                                         start=(c == 0), stop=(c == DC - 1))
                last.then_inc(summed, 1)

            @block.vector
            def _(dve):
                dve.wait_ge(rooted, 1)
                dve.reciprocal(rstd[:], rstd[:])
                dve.drain()
                for c in range(DC):
                    dve.scalar_tensor_tensor(out=out[:, c, :], in0=x[:, c, :], scalar=gain[:, c:c + 1],
                                             in1=rstd[:], op0=ALU.mult, op1=ALU.mult)


def headnorm(nc, name, buf, n, ones, count, gain, eps):
    with Stage(nc, name) as st:
        sq = st.sb("sq", [P, 2, T])
        rstd = st.sb("rstd", [P, 2, T])
        tot = st.ps("tot", [P, 2, 2, 512])
        squared = st.sem("squared")
        summed = st.sem("summed")
        rooted = st.sem("rooted")
        scaled = st.sem("scaled")
        with st.block() as block:

            @block.scalar
            def _(act):
                def one(i, k, first):
                    if not first:
                        act.wait_ge(scaled, i * 2 + k - 1)
                    act.activation(sq[:, k, :], at(buf, i * 2 + k), ACT.Square).then_inc(squared, 1)
                    act.wait_ge(summed, i * 2 + k + 1)
                    act.activation(halves(rstd[:, k, :]), tot[:, k, :, 0:HALF], ACT.Sqrt, bias=eps,
                                   scale=1.0 / count).then_inc(rooted, 1)

                paired(act, n, one)

            @block.tensor
            def _(pe):
                def one(i, k, first):
                    pe.wait_ge(squared, i * 2 + k + 1)
                    for a in range(2):
                        last = pe.matmul(tot[:, k, a, 0:HALF], ones, sq[:, k, a * HALF:(a + 1) * HALF],
                                         start=True, stop=True)
                    last.then_inc(summed, 1)

                paired(pe, n, one)

            @block.vector
            def _(dve):
                def one(i, k, first):
                    dve.wait_ge(rooted, i * 2 + k + 1)
                    dve.reciprocal(rstd[:, k, :], rstd[:, k, :])
                    dve.drain()
                    chunk = at(buf, i * 2 + k)
                    dve.scalar_tensor_tensor(out=chunk, in0=chunk, scalar=gain, in1=rstd[:, k, :],
                                             op0=ALU.mult, op1=ALU.mult).then_inc(scaled, 1)

                paired(dve, n, one)


def linear_by_token(nc, name, w_dram, n_cols, x, out, tile, n_tiles):
    n_half = n_cols // 512
    with Stage(nc, name) as st:
        w = st.sb("w", [P, DC, n_cols])
        acc = st.ps("acc", [P, 2, n_half, 512])
        w_landed = st.sem("w_landed")
        multiplied = st.sem("multiplied")
        evacuated = st.sem("evacuated")
        rows = [min(tile, T - t * tile) for t in range(n_tiles)]
        with st.block() as block:

            @block.sync
            def _(sp):
                sp.dma_start(w[:], w_dram).then_inc(w_landed, 16)

            @block.tensor
            def _(pe):
                pe.wait_ge(w_landed, 16)
                for t, m in enumerate(rows):
                    if t >= 2:
                        pe.wait_ge(evacuated, t - 1)
                    for c in range(DC):
                        for a in range(n_half):
                            last = pe.matmul(acc[0:m, t % 2, a, :], x[:, c, t * tile:t * tile + m],
                                             w[:, c, a * 512:(a + 1) * 512],
                                             start=(c == 0), stop=(c == DC - 1))
                    last.then_inc(multiplied, 1)

            @block.scalar
            def _(act):
                for t, m in enumerate(rows):
                    act.wait_ge(multiplied, t + 1)
                    act.activation(out[0:m, t, :].rearrange("p (a n) -> p a n", a=n_half),
                                   acc[0:m, t % 2, :, :], ACT.Copy).then_inc(evacuated, 1)



def s5(nc, dr, cst, u, cat):
    with ExitStack() as outer:
        def sb(name, shape):
            return outer.enter_context(nc.sbuf_tensor(f"s5_{name}", shape, F32))

        ct = sb("ct", [P, 2, S5_TILES, P])
        bt = sb("bt", [P, 2, S5_TILES, P])
        mag = sb("mag", [P, S5_TILES])
        h0 = sb("h0", [P, 2, S5_TILES, NB])
        ends = sb("ends", [P, 2, S5_TILES, 1 + NB])
        rot1 = sb("rot1", [P, 2, S5_TILES])
        with Stage(nc, "s5b") as st:
            braw = st.sb("braw", [P, 2, S5_TILES, P])
            bb = st.sb("bb", [P, 2, 4, P])
            par = st.sb("par", [P, 3, S5_TILES])
            dt = st.sb("dt", [P, S5_TILES])
            ang = st.sb("ang", [P, 2, S5_TILES])
            rnd = st.sb("rnd", [P, 2, S5_TILES])
            lbre = st.sb("lbre", [P, 2, S5_TILES])
            den = st.sb("den", [P, S5_TILES])
            tmp = st.sb("tmp", [P, S5_TILES])
            coef = st.sb("coef", [P, 2, S5_TILES])
            bp = st.sb("bp", [P, 4, P])
            tr = st.ps("tr", [P, 2, 2, 4, P])
            landed = st.sem("landed")
            b_landed = st.sem("b_landed")
            c_landed = st.sem("c_landed")
            dt_ready = st.sem("dt_ready")
            arg_ready = st.sem("arg_ready")
            trig_ready = st.sem("trig_ready")
            bb_ready = st.sem("bb_ready")
            turned = st.sem("turned")
            copied = st.sem("copied")
            with st.block() as block:

                @block.sync
                def _(sp):
                    sp.dma_start(par[:], dr["s5_par"]).then_inc(landed, 16)
                    sp.dma_start(braw[:], dr["s5_b"]).then_inc(b_landed, 16)
                    sp.dma_start(ct[:], dr["s5_c"]).then_inc(c_landed, 16)
                    sp.dma_start(h0[:], dr["s5_h0"]).then_inc(landed, 16)
                    sp.wait_ge(landed, 32)

                @block.scalar
                def _(act):
                    act.wait_ge(landed, 32)
                    act.activation(dt[:], par[:, 2, :], ACT.Exp).then_inc(dt_ready, 1)
                    act.wait_ge(arg_ready, 1)
                    act.activation(mag[:], mag[:], ACT.Exp)
                    act.activation(rot1[:], ang[:], ACT.Sin).then_inc(trig_ready, 1)
                    for q in range(4):
                        for r in range(2):
                            act.wait_ge(turned, 2 * q + r + 1)
                            act.activation(bt[:, r, 4 * q:4 * q + 4, :], tr[:, q % 2, r, :, :], ACT.Copy)\
                               .then_inc(copied, 1)

                @block.vector
                def _(dve):
                    are, aim = par[:, 0, :], par[:, 1, :]
                    dve.wait_ge(dt_ready, 1)
                    dve.tensor_tensor(mag[:], are, dt[:], ALU.mult)
                    dve.tensor_tensor(ang[:, 1, :], aim, dt[:], ALU.mult)
                    dve.drain()
                    dve.tensor_scalar(ang[:, 0, :], ang[:, 1, :], math.pi / 2, None, ALU.add)
                    dve.drain()
                    dve.tensor_scalar(rnd[:], ang[:], 1.0 / (2 * math.pi), BIG_ROUND, ALU.mult, ALU.add)
                    dve.drain()
                    dve.tensor_scalar(rnd[:], rnd[:], BIG_ROUND, None, ALU.subtract)
                    dve.drain()
                    two_pi_hi = 6.28125
                    dve.scalar_tensor_tensor(out=ang[:], in0=rnd[:], scalar=-two_pi_hi, in1=ang[:],
                                             op0=ALU.mult, op1=ALU.add)
                    dve.drain()
                    dve.scalar_tensor_tensor(out=ang[:], in0=rnd[:], scalar=-(2 * math.pi - two_pi_hi),
                                             in1=ang[:], op0=ALU.mult, op1=ALU.add)
                    dve.drain()
                    dve.tensor_scalar(ang[:], ang[:], 3.1415925, -3.1415925, ALU.min, ALU.max)
                    dve.tensor_tensor(den[:], are, are, ALU.mult)
                    dve.tensor_tensor(tmp[:], aim, aim, ALU.mult)
                    dve.drain()
                    dve.tensor_tensor(den[:], den[:], tmp[:], ALU.add).then_inc(arg_ready, 1)
                    dve.drain()
                    dve.reciprocal(den[:], den[:])
                    dve.wait_ge(trig_ready, 1)
                    for r in range(2):
                        dve.tensor_tensor(lbre[:, r, :], rot1[:, r, :], mag[:], ALU.mult)
                    dve.drain()
                    dve.tensor_scalar(lbre[:, 0, :], lbre[:, 0, :], 1.0, None, ALU.subtract)
                    dve.drain()
                    dve.tensor_tensor(coef[:, 0, :], lbre[:, 0, :], are, ALU.mult)
                    dve.tensor_tensor(tmp[:], lbre[:, 1, :], aim, ALU.mult)
                    dve.tensor_tensor(coef[:, 1, :], lbre[:, 1, :], are, ALU.mult)
                    dve.tensor_tensor(dt[:], lbre[:, 0, :], aim, ALU.mult)
                    dve.drain()
                    dve.tensor_tensor(coef[:, 0, :], coef[:, 0, :], tmp[:], ALU.add)
                    dve.tensor_tensor(coef[:, 1, :], coef[:, 1, :], dt[:], ALU.subtract)
                    dve.drain()
                    for r in range(2):
                        dve.tensor_tensor(coef[:, r, :], coef[:, r, :], den[:], ALU.mult)
                    dve.wait_ge(b_landed, 16)
                    dve.wait_ge(c_landed, 16)
                    dve.drain()
                    dve.tensor_scalar(ct[:, 1, :, :], ct[:, 1, :, :], -1.0, None, ALU.mult)
                    for q in range(4):
                        s = slice(4 * q, 4 * q + 4)
                        cr = coef[:, 0, s].unsqueeze(2).to_broadcast([P, 4, P])
                        ci = coef[:, 1, s].unsqueeze(2).to_broadcast([P, 4, P])
                        if q:
                            dve.wait_ge(turned, 2 * q)
                        dve.tensor_tensor(bb[:, 0, :, :], braw[:, 0, s, :], cr, ALU.mult)
                        dve.tensor_tensor(bp[:], braw[:, 1, s, :], ci, ALU.mult)
                        dve.drain()
                        dve.tensor_tensor(bb[:, 0, :, :], bb[:, 0, :, :], bp[:], ALU.subtract)
                        dve.drain()
                        dve.tensor_tensor(bb[:, 1, :, :], braw[:, 1, s, :], cr, ALU.mult)
                        dve.tensor_tensor(bp[:], braw[:, 0, s, :], ci, ALU.mult)
                        dve.drain()
                        dve.tensor_tensor(bb[:, 1, :, :], bb[:, 1, :, :], bp[:], ALU.add).then_inc(bb_ready, 1)

                @block.tensor
                def _(pe):
                    for q in range(4):
                        pe.wait_ge(bb_ready, q + 1)
                        if q >= 2:
                            pe.wait_ge(copied, 2 * (q - 1))
                        for r in range(2):
                            for j in range(4):
                                last = pe.transpose(tr[:, q % 2, r, j, :], bb[:, r, j, :], cst["ident"])
                            last.then_inc(turned, 1)

        rot = sb("rot", [P, 2, S5_TILES, L5])
        with Stage(nc, "s5p") as st:
            t = [st.sb(f"t{k}", [P, S5_TILES, TP // 2]) for k in range(2)]
            wk = st.sb("wk", [P, 2, S5_TILES])
            wt = st.sb("wt", [P, 3, S5_TILES])
            half_done = st.sem("half_done")
            with st.block() as block:

                @block.vector
                def _(dve):
                    dve.memset(rot[:, 0, :, 0:1], 1.0)
                    dve.memset(rot[:, 1, :, 0:1], 0.0)
                    dve.tensor_copy(wk[:], rot1[:])
                    dve.drain()
                    k = 1
                    while k < TP:
                        c, s = rot[:, 0, :, 0:k], rot[:, 1, :, 0:k]
                        nc_, ns = rot[:, 0, :, k:2 * k], rot[:, 1, :, k:2 * k]
                        wr = wk[:, 0, :].unsqueeze(2).to_broadcast([P, S5_TILES, k])
                        wi = wk[:, 1, :].unsqueeze(2).to_broadcast([P, S5_TILES, k])
                        dve.tensor_tensor(t[0][:, :, 0:k], s, wi, ALU.mult)
                        dve.tensor_tensor(t[1][:, :, 0:k], s, wr, ALU.mult)
                        dve.tensor_tensor(nc_, c, wr, ALU.mult)
                        dve.tensor_tensor(ns, c, wi, ALU.mult)
                        dve.tensor_tensor(wt[:, 0, :], wk[:, 0, :], wk[:, 0, :], ALU.mult)
                        dve.tensor_tensor(wt[:, 1, :], wk[:, 1, :], wk[:, 1, :], ALU.mult)
                        dve.tensor_tensor(wt[:, 2, :], wk[:, 0, :], wk[:, 1, :], ALU.mult)
                        dve.drain()
                        dve.tensor_tensor(nc_, nc_, t[0][:, :, 0:k], ALU.subtract)
                        dve.tensor_tensor(ns, ns, t[1][:, :, 0:k], ALU.add)
                        dve.tensor_tensor(wk[:, 0, :], wt[:, 0, :], wt[:, 1, :], ALU.subtract)
                        dve.tensor_scalar(wk[:, 1, :], wt[:, 2, :], 2.0, None, ALU.mult)
                        dve.drain()
                        k *= 2
                    for r in range(2):
                        for b in range(NB):
                            dve.tensor_copy(rot[:, r, :, TP + SEG * b:TP + SEG * (b + 1)], rot[:, r, :, 0:SEG])

        y = cat[:, 0:4, :]
        with Stage(nc, "s5s") as st:
            x = st.sb("x", [P, 2, 2, L5])
            g = st.sb("g", [P, 2, L5])
            v = st.sb("v", [P, 2, L5])
            hh = st.sb("hh", [P, 2, 2, L5])
            decay = st.sb("decay", [P, 2, L5])
            bu = st.ps("bu", [P, 2, 2, 512])
            cy = st.ps("cy", [P, 2, 2, 512])
            bu_ready = st.sem("bu_ready")
            x_ready = st.sem("x_ready")
            x_used = st.sem("x_used")
            h_ready = st.sem("h_ready")
            h_used = st.sem("h_used")
            y_taken = st.sem("y_taken")
            LH = L5 // 2
            with st.block() as block:

                @block.tensor
                def _(pe):
                    def read_in(s):
                        if s:
                            pe.wait_ge(x_ready, s)
                        for r in range(2):
                            for a in range(2):
                                last = pe.matmul(bu[:, r, a, 0:HALF], bt[:, r, s, :],
                                                 u[:, s // 4, a * HALF:(a + 1) * HALF], start=True, stop=True)
                        last.then_inc(bu_ready, 1)

                    def read_out(s):
                        pe.wait_ge(h_ready, s + 1)
                        if s % 4 == 0 and s >= 8:
                            pe.wait_ge(y_taken, s // 4 - 1)
                        for r in range(2):
                            for a in range(2):
                                last = pe.matmul(cy[:, (s // 4) % 2, a, 0:LH], ct[:, r, s, :],
                                                 hh[:, s % 2, r, a * LH:(a + 1) * LH],
                                                 start=(s % 4 == 0 and r == 0), stop=(s % 4 == 3 and r == 1))
                        last.then_inc(h_used, 1)

                    read_in(0)
                    for s in range(S5_TILES):
                        if s + 1 < S5_TILES:
                            read_in(s + 1)
                        read_out(s)

                @block.scalar
                def _(act):
                    for s in range(S5_TILES):
                        k = s % 2
                        if s >= 2:
                            act.wait_ge(x_used, s - 1)
                        act.activation(decay[:, k, :], cst["seg_mask"], ACT.Copy, scale=mag[:, s:s + 1])
                        for r in range(2):
                            act.activation(x[:, k, r, TP:L5].rearrange("p (b e) -> p b e", e=SEG)[:, :, 0:1],
                                           h0[:, r, s, :].unsqueeze(2), ACT.Copy)
                        act.wait_ge(bu_ready, s + 1)
                        for r in range(2):
                            act.activation(x[:, k, r, 0:HALF], bu[:, r, 0, 0:HALF], ACT.Copy)
                            act.activation(x[:, k, r, HALF:TP], bu[:, r, 1, 0:TP - HALF], ACT.Copy)
                            last = act.activation(
                                x[:, k, r, TP:L5].rearrange("p (b e) -> p b e", e=SEG)[:, :, 1:SEG],
                                bu[:, r, 1, TP - HALF:HALF].rearrange("p (b e) -> p b e", e=TS), ACT.Copy)
                        last.then_inc(x_ready, 1)

                @block.vector
                def _(dve):
                    def take_y(q):
                        dve.wait_ge(h_used, 4 * q + 4)
                        res = cy[:, q % 2, :, :]
                        uq, yq, dq = u[:, q, :], y[:, q, :], cst["s5_d"][:, q:q + 1]
                        dve.scalar_tensor_tensor(out=yq[:, 0:LH], in0=uq[:, 0:LH], scalar=dq,
                                                 in1=res[:, 0, 0:LH], op0=ALU.mult, op1=ALU.add)
                        dve.scalar_tensor_tensor(out=yq[:, LH:TP], in0=uq[:, LH:TP], scalar=dq,
                                                 in1=res[:, 1, 0:TP - LH], op0=ALU.mult, op1=ALU.add)
                        dve.scalar_tensor_tensor(
                            out=yq[:, TP:T].rearrange("p (b e) -> p b e", e=TS),
                            in0=uq[:, TP:T].rearrange("p (b e) -> p b e", e=TS), scalar=dq,
                            in1=res[:, 1, TP - LH:LH].rearrange("p (b e) -> p b e", e=SEG)[:, :, 1:SEG],
                            op0=ALU.mult, op1=ALU.add).then_inc(y_taken, 1)

                    for s in range(S5_TILES):
                        k = s % 2
                        c, sn = rot[:, 0, s, :], rot[:, 1, s, :]
                        dve.wait_ge(x_ready, s + 1)
                        xr, xi = x[:, k, 0, :], x[:, k, 1, :]
                        gr, gi, vr, vi = g[:, 0, :], g[:, 1, :], v[:, 0, :], v[:, 1, :]
                        dve.tensor_tensor(gr, xr, c, ALU.mult)
                        dve.tensor_tensor(vr, xi, sn, ALU.mult)
                        dve.tensor_tensor(gi, xi, c, ALU.mult)
                        dve.tensor_tensor(vi, xr, sn, ALU.mult)
                        dve.drain()
                        dve.tensor_tensor(gr, gr, vr, ALU.add)
                        dve.tensor_tensor(gi, gi, vi, ALU.subtract)
                        dve.drain()
                        dve.tensor_tensor_scan(vr, decay[:, k, :], gr, 0.0, ALU.mult, ALU.add)
                        dve.tensor_tensor_scan(vi, decay[:, k, :], gi, 0.0, ALU.mult, ALU.add).then_inc(x_used, 1)
                        dve.drain()
                        if s >= 2:
                            dve.wait_ge(h_used, s - 1)
                        hr, hi = hh[:, k, 0, :], hh[:, k, 1, :]
                        dve.tensor_tensor(hr, vr, c, ALU.mult)
                        dve.tensor_tensor(gr, vi, sn, ALU.mult)
                        dve.tensor_tensor(hi, vi, c, ALU.mult)
                        dve.tensor_tensor(gi, vr, sn, ALU.mult)
                        dve.drain()
                        dve.tensor_tensor(hr, hr, gr, ALU.subtract)
                        dve.tensor_tensor(hi, hi, gi, ALU.add).then_inc(h_ready, 1)
                        dve.drain()
                        for r in range(2):
                            dve.tensor_copy(ends[:, r, s, 0:1], hh[:, k, r, TP - 1:TP])
                            dve.tensor_copy(ends[:, r, s, 1:1 + NB].unsqueeze(2),
                                            hh[:, k, r, TP:L5].rearrange("p (b e) -> p b e", e=SEG)[:, :, TS:SEG])
                        if s % 4 == 3 and s > 3:
                            take_y(s // 4 - 1)
                    take_y(3)

        with Stage(nc, "s5g") as st:
            yg = st.sb("yg", [P, 4, T])
            gelued = st.sem("gelued")
            with st.block() as block:

                @block.scalar
                def _(act):
                    act.activation(yg[:], y, ACT.Gelu_apprx_tanh).then_inc(gelued, 1)

                @block.sync
                def _(sp):
                    store(sp, dr, dr["out_s5"], ends[:])
                    sp.wait_ge(dr["stored"], 16 * dr["n_stored"])

            def gate(eng, o, res):
                return eng.activation(halves(at(y, o)), res, ACT.Sigmoid, bias=cst["s5_glu_b"][:, bass.ds(o, 1)])

            linear(nc, "glu", dr["w_glu"], 4, 4, yg, "act", gate)
            with st.block() as block:

                @block.vector
                def _(dve):
                    dve.tensor_tensor(y, yg[:], y, ALU.mult)



def hgrn(nc, dr, cst, q, f, g, v, cat):
    NC9 = NCH + 1
    with Stage(nc, "hg") as st:
        k = st.sb("k", [P, BH, T])
        b = st.sb("b", [P, BH, T])
        e = st.sb("e", [P, BH, T])
        x = st.sb("x", [P, BH, T])
        A = st.sb("A", [CH, BH, NC9, CH])
        part = st.sb("part", [CH, 2, NC9, CH])
        lbs = st.sb("lbs", [P, BH, 2])
        lb = st.sb("lb", [P, BH])
        sumlb = st.sb("sumlb", [P, BH])
        omlb = st.sb("omlb", [P, BH])
        lb_in = st.sem("lb_in")
        lb_exp = st.sem("lb_exp")
        lb_max = st.sem("lb_max")
        sig = st.sem("sig")
        f_ready = st.sem("f_ready")
        logged = st.sem("logged")
        b_ready = st.sem("b_ready")
        d_ready = st.sem("d_ready")
        e_ready = st.sem("e_ready")
        x_ready = st.sem("x_ready")
        scored = st.sem("scored")
        taken = st.sem("taken")
        sps = st.ps("sps", [CH, 2, 2, 512])
        flat = lambda t: t[:].rearrange("p h n -> p (h n)")
        LEVELS = [32, 16, 8, 4, 2, 1]

        def spans(buf, m):
            if m >= 8:
                return buf[:, :, 0:TP].rearrange("p h (a m) -> p h a m", m=2 * m)
            return flat(buf).rearrange("p (a m) -> p a m", m=2 * m)

        def part_of(ap, lo, hi):
            return ap[:, :, :, lo:hi] if len(ap.shape) == 4 else ap[:, :, lo:hi]

        with st.block() as block:

            @block.sync
            def _(sp):
                sp.dma_start(lbs[:], dr["hgrn_lb"]).then_inc(lb_in, 16)
                sp.wait_ge(lb_in, 16)

            @block.scalar
            def _(act):
                act.wait_ge(lb_max, 1)
                act.activation(lbs[:], lbs[:], ACT.Exp).then_inc(lb_exp, 1)
                act.activation(f[:], f[:], ACT.Sigmoid).then_inc(sig, 1)
                act.activation(g[:], g[:], ACT.Silu)
                act.wait_ge(f_ready, 1)
                act.activation(f[:], f[:], ACT.Ln).then_inc(logged, 1)
                for n, m in enumerate(LEVELS):
                    act.wait_ge(d_ready, n + 1)
                    act.activation(part_of(spans(e, m), m, 2 * m), part_of(spans(e, m), m, 2 * m), ACT.Exp)
                    act.activation(part_of(spans(e, m), 0, m), part_of(spans(e, m), 0, m), ACT.Exp, scale=-1.0)\
                       .then_inc(e_ready, 1)

            @block.vector
            def _(dve):
                dve.wait_ge(lb_in, 16)
                dve.tensor_tensor(sumlb[:], lbs[:, :, 0], lbs[:, :, 1], ALU.max)
                dve.drain()
                dve.tensor_tensor(lbs[:], lbs[:], sumlb[:].unsqueeze(2).to_broadcast([P, BH, 2]), ALU.subtract)\
                   .then_inc(lb_max, 1)
                dve.wait_ge(lb_exp, 1)
                dve.tensor_tensor(sumlb[:], lbs[:, :, 0], lbs[:, :, 1], ALU.add)
                dve.drain()
                dve.reciprocal(sumlb[:], sumlb[:])
                dve.drain()
                dve.tensor_tensor(lb[:], lbs[:, :, 0], sumlb[:], ALU.mult)
                dve.drain()
                dve.tensor_scalar(omlb[:], lb[:], -1.0, 1.0, ALU.mult, ALU.add)
                dve.drain()
                dve.wait_ge(sig, 1)
                for h in range(BH):
                    dve.tensor_scalar(f[:, h, :], f[:, h, :], omlb[:, h:h + 1], lb[:, h:h + 1], ALU.mult, ALU.add)
                dve.drain()
                dve.tensor_scalar(k[:], f[:], -1.0, 1.0, ALU.mult, ALU.add).then_inc(f_ready, 1)
                dve.drain()
                dve.wait_ge(logged, 1)
                dve.tensor_tensor_scan(flat(b), cst["chunk_mask"], flat(f), 0.0, ALU.mult, ALU.add)
                dve.drain()

                def collect(n, h):
                    i = n * BH + h
                    dve.wait_ge(scored, i + 1)
                    mask = cst["level_mask"][:, n, :]
                    lots = [(0, NCH, 0)] + ([] if 0 < n <= 3 and n != 0 else [(NCH, 1, 1)])
                    for c0, cn, bank in lots:
                        src = sps[:, i % 2, bank, 0:cn * CH].rearrange("p (c t) -> p c t", t=CH)
                        mk = mask.unsqueeze(1).to_broadcast([CH, cn, CH])
                        dst = A[:, h, c0:c0 + cn, :]
                        if n == 0:
                            last = dve.tensor_tensor(dst, src, mk, ALU.mult)
                        else:
                            last = dve.tensor_tensor(part[:, i % 2, c0:c0 + cn, :], src, mk, ALU.mult)
                    last.then_inc(taken, 1)
                    dve.drain()
                    if n:
                        hi = lots[-1][0] + lots[-1][1]
                        dve.tensor_tensor(A[:, h, 0:hi, :], A[:, h, 0:hi, :], part[:, i % 2, 0:hi, :], ALU.add)

                for h in range(BH):
                    collect(0, h)
                for n, m in enumerate(LEVELS):
                    ref = part_of(spans(b, m), m - 1, m)
                    dve.tensor_tensor(spans(e, m), spans(b, m), ref.to_broadcast(spans(b, m).shape), ALU.subtract)\
                       .then_inc(d_ready, 1)
                    dve.wait_ge(e_ready, n + 1)
                    if n:
                        dve.wait_ge(scored, BH * (n + 1))
                    dve.tensor_tensor(part_of(spans(x, m), m, 2 * m), part_of(spans(e, m), m, 2 * m),
                                      part_of(spans(q, m), m, 2 * m), ALU.mult)
                    dve.tensor_tensor(part_of(spans(x, m), 0, m), part_of(spans(e, m), 0, m),
                                      part_of(spans(k, m), 0, m), ALU.mult).then_inc(x_ready, 1)
                    for h in range(BH):
                        collect(n + 1, h)

            @block.tensor
            def _(pe):
                def score(n, h, left, right, chunks):
                    i = n * BH + h
                    if i >= 2:
                        pe.wait_ge(taken, i - 1)
                    for c in range(chunks):
                        s = slice(c * CH, (c + 1) * CH)
                        last = pe.matmul(sps[:, i % 2, c // NCH, (c % NCH) * CH:(c % NCH + 1) * CH],
                                         left[:, h, s], right[:, h, s], start=True, stop=True)
                    last.then_inc(scored, 1)

                pe.wait_ge(f_ready, 1)
                for h in range(BH):
                    score(0, h, k, q, NC9)
                for n, m in enumerate(LEVELS):
                    pe.wait_ge(x_ready, n + 1)
                    for h in range(BH):
                        score(n + 1, h, x, x, NCH if m >= 8 else NC9)

        S = st.sb("S", [P, BH, P])
        S0 = st.sb("S0", [P, NB, BH, P])
        vm = st.sb("vm", [CH, 2, NB, P])
        kt = st.sb("kt", [CH, 2, BH, P])
        o_in = st.ps("o_in", [P, 2, 512])
        kps = st.ps("kps", [P, 1, 512])
        eb_ready = st.sem("eb_ready")
        dk_ready = st.sem("dk_ready")
        dk_exp = st.sem("dk_exp")
        kd_ready = st.sem("kd_ready")
        turned = st.sem("turned")
        kt_ready = st.sem("kt_ready")
        s_done = st.sem("s_done")
        dS_ready = st.sem("dS_ready")
        o_ready = st.sem("o_ready")
        o_taken = st.sem("o_taken")
        s0_in = st.sem("s0_in")
        vm_ready = st.sem("vm_ready")
        d = st.sb("d", [P, BH, T])
        dps = st.ps("dps", [P, 1, 512])
        vm_used = [st.sem("dS_taken0"), st.sem("dS_taken1")]
        with st.block() as block:

            @block.sync
            def _(sp):
                sp.dma_start(S0[:], dr["hgrn_s0"]).then_inc(s0_in, 16)
                sp.wait_ge(s_done, NCH)
                store(sp, dr, dr["out_hgrn_p"], S[:])
                sp.wait_ge(s_done, NCH + BH)
                store(sp, dr, dr["out_hgrn_s"], S0[:])
                sp.wait_ge(dr["stored"], 16 * dr["n_stored"])

            @block.scalar
            def _(act):
                act.activation(e[:], b[:], ACT.Exp).then_inc(eb_ready, 1)
                act.wait_ge(dk_ready, 1)
                act.activation(d[:], d[:], ACT.Exp).then_inc(dk_exp, 1)
                for c in range(NC9):
                    act.wait_ge(turned, c + 1)
                    if c >= 2:
                        act.wait_ge(dS_ready, c - 1)
                    act.activation(kt[:, c % 2, :, :], kps[0:CH, 0, :].rearrange("p (h n) -> p h n", h=BH), ACT.Copy)\
                       .then_inc(kt_ready, 1)
                    act.wait_ge(o_ready, c + 1)
                    act.activation(cat[:, 4:8, c * CH:(c + 1) * CH],
                                   o_in[:, c % 2, 0:BH * CH].rearrange("p (h n) -> p h n", h=BH), ACT.Copy)\
                       .then_inc(o_taken, 1)

            @block.vector
            def _(dve):
                last = b[:, :, 0:TP].rearrange("p h (c t) -> p h c t", t=CH)
                dve.tensor_tensor(d[:, :, 0:TP].rearrange("p h (c t) -> p h c t", t=CH),
                                  last[:, :, :, CH - 1:CH].to_broadcast([P, BH, NCH, CH]), last, ALU.subtract)
                last = b[:, :, TP:T].rearrange("p h (c t) -> p h c t", t=TS)
                dve.tensor_tensor(d[:, :, TP:T].rearrange("p h (c t) -> p h c t", t=TS),
                                  last[:, :, :, TS - 1:TS].to_broadcast([P, BH, NB, TS]), last, ALU.subtract)\
                   .then_inc(dk_ready, 1)
                dve.wait_ge(eb_ready, 1)
                dve.tensor_tensor(x[:], q[:], e[:], ALU.mult)
                dve.wait_ge(dk_exp, 1)
                dve.tensor_tensor(k[:], k[:], d[:], ALU.mult).then_inc(kd_ready, 1)
                for c in range(NCH):
                    dve.wait_ge(dS_ready, c + 1)
                    if c:
                        dve.wait_ge(o_ready, c + 1)
                    new = dps[:, 0, :].rearrange("p (h n) -> p h n", h=BH)
                    for h in range(BH):
                        if c == 0:
                            op = dve.tensor_copy(S[:, h, :], new[:, h, :])
                        else:
                            op = dve.scalar_tensor_tensor(
                                out=S[:, h, :], in0=S[:, h, :], scalar=e[:, h, (c + 1) * CH - 1:(c + 1) * CH],
                                in1=new[:, h, :], op0=ALU.mult, op1=ALU.add)
                    op.then_inc(s_done, 1)
                dve.wait_ge(s0_in, 16)
                for h in range(BH):
                    if h >= 2:
                        dve.wait_ge(dS_ready, NCH + 2 * (h - 1))
                    dve.tensor_tensor(vm[:, h % 2, :, :],
                                      v[:, NCH, h * P:(h + 1) * P].unsqueeze(1).to_broadcast([CH, NB, P]),
                                      cst["seq_mask"].unsqueeze(2).to_broadcast([CH, NB, P]), ALU.mult)\
                       .then_inc(vm_ready, 1)
                    if h == 0:
                        dve.wait_ge(o_ready, NC9)
                    ebl = e[:, h, TP:T].rearrange("p (b t) -> p b t", t=TS)[:, :, TS - 1:TS]
                    dve.tensor_tensor(S0[:, :, h, :], S0[:, :, h, :], ebl.to_broadcast([P, NB, P]), ALU.mult)
                    dve.drain()
                    for a in range(2):
                        dve.wait_ge(dS_ready, NCH + 2 * h + a + 1)
                        dst = S0[:, 4 * a:4 * a + 4, h, :]
                        op = dve.tensor_tensor(dst, dst, dps[:, 0, :].rearrange("p (b n) -> p b n", n=P), ALU.add)
                        op.then_inc(vm_used[a], 1)
                    dve.drain().then_inc(s_done, 1)

            @block.tensor
            def _(pe):
                pe.wait_ge(kd_ready, 1)
                pe.wait_ge(s0_in, 16)
                for c in range(NC9):
                    cols = slice(c * CH, (c + 1) * CH)
                    if c:
                        pe.wait_ge(kt_ready, c)
                    for h in range(BH):
                        last_t = pe.transpose(kps[0:CH, 0, h * P:(h + 1) * P], k[:, h, cols], cst["ident"])
                    last_t.then_inc(turned, 1)
                    if c >= 2:
                        pe.wait_ge(o_taken, c - 1)
                    if c:
                        pe.wait_ge(s_done, c)
                    for h in range(BH):
                        o = o_in[:, c % 2, h * CH:(h + 1) * CH]
                        last_o = pe.matmul(o, v[:, c, h * P:(h + 1) * P], A[:, h, c, :], start=True,
                                           stop=(c in (0, NCH)))
                        if 0 < c < NCH:
                            last_o = pe.matmul(o, S[:, h, :], x[:, h, cols], start=False, stop=True)
                        if c == NCH:
                            for bb in range(NB):
                                last_o = pe.matmul(o[:, bb * TS:(bb + 1) * TS], S0[:, bb, h, :],
                                                   x[:, h, TP + bb * TS:TP + (bb + 1) * TS],
                                                   start=False, stop=True, skip_group_check=True)
                    last_o.then_inc(o_ready, 1)
                    pe.wait_ge(kt_ready, c + 1)
                    if c < NCH:
                        for h in range(BH):
                            last_s = pe.matmul(dps[:, 0, h * P:(h + 1) * P], kt[:, c % 2, h, :],
                                               v[:, c, h * P:(h + 1) * P], start=True, stop=True)
                        last_s.then_inc(dS_ready, 1)
                for h in range(BH):
                    pe.wait_ge(vm_ready, h + 1)
                    for a in range(2):
                        if a:
                            pe.wait_ge(vm_used[0], h + 1)
                        elif h:
                            pe.wait_ge(vm_used[1], h)
                        pe.matmul(dps[:, 0, :], kt[:, NCH % 2, h, :],
                                  vm[:, h % 2, 4 * a:4 * a + 4, :].rearrange("p b n -> p (b n)"),
                                  start=True, stop=True).then_inc(dS_ready, 1)

    headnorm(nc, "hgn", cat[:, 4:8, :], BH, cst["ones"], P, cst["hgrn_norm"], cst["eps"])
    with Stage(nc, "hgg") as st:
        with st.block() as block:

            @block.vector
            def _(dve):
                dve.tensor_tensor(cat[:, 4:8, :], cat[:, 4:8, :], g[:], ALU.mult)



class Activities:

    def __init__(self, nc, st, dr, layer, xn, keys, first_unit, n_units):
        self.nc, self.keys, self.xn = nc, keys, xn
        self.at0, self.n = first_unit, n_units
        per = JB // keys
        self.src = dr["peer_ut"][layer].rearrange("b p (c h n) -> b h p c n", c=DC, h=per)
        self.dst = dr["activities"].rearrange("b p (h n) -> b h p n", h=per)
        self.per = per
        self.ut = st.sb("ut", [P, 2, DC, keys * P])
        self.s = st.sb("s", [P, 2, keys, T])
        self.ps = st.ps("s_ps", [P, 2, 2, 512])
        self.u_in = [st.sem(f"u_in{k}") for k in range(2)]
        self.s_ready = st.sem("s_ready")
        self.gelued = st.sem("gelued")
        self.s_out = [st.sem(f"s_out{k}") for k in range(2)]

    def _unit(self, sp, ap, i, k, first):
        if self.per == 1:
            n = self.at0 + i * 2 + k
            return ap[bass.ds(n if first else sp.snap(n), 1), 0]
        n = self.at0 // 2 + i
        return ap[bass.ds(n if first else sp.snap(n), 1), k]

    def load(self, sp, i, k, first):
        src = self._unit(sp, self.src, i, k, first)
        if not first:
            sp.wait_ge(self.s_ready, (i * 2 + k - 1) * self.keys)
        sp.dma_start(self.ut[:, k, :, :], src.rearrange("a p c n -> p (a c) n")).then_inc(self.u_in[k], 16)

    def store(self, sp, i, k, first):
        dst = self._unit(sp, self.dst, i, k, first)
        sp.wait_ge(self.gelued, (i * 2 + k + 1) * self.keys)
        sp.dma_start(dst.rearrange("a p n -> p (a n)"), self.s[:, k, :, :].rearrange("p j n -> p (j n)"))\
          .then_inc(self.s_out[k], 16)

    def stored(self, sp):
        for k in range(2):
            sp.wait_ge(self.s_out[k], self.n // 2 * 16)

    def score(self, pe, i, k, j, first):
        if j == 0:
            pe.wait_ge(self.u_in[k], i * 16 + 16)
        if not (first and k == 0 and j < 2):
            pe.wait_ge(self.gelued, (i * 2 + k) * self.keys + j - 1)
        for c in range(DC):
            for a in range(2):
                last = pe.matmul(self.ps[:, j % 2, a, 0:HALF], self.ut[:, k, c, j * P:(j + 1) * P],
                                 self.xn[:, c, a * HALF:(a + 1) * HALF], start=(c == 0), stop=(c == DC - 1))
        last.then_inc(self.s_ready, 1)

    def gelu(self, act, i, k, j, first):
        if not first and j == 0:
            act.wait_ge(self.s_out[k], i * 16)
        act.wait_ge(self.s_ready, (i * 2 + k) * self.keys + j + 1)
        act.activation(halves(self.s[:, k, j, :]), self.ps[:, j % 2, :, 0:HALF], ACT.Gelu_apprx_tanh)\
           .then_inc(self.gelued, 1)


def peer(nc, dr, cst, layer, xn, h):
    nm = f"p{layer}"
    with ExitStack() as outer:
        sel = outer.enter_context(nc.sbuf_tensor(f"{nm}_sel", [P, 3, TPAD], F32))
        with ExitStack() as inner:
            q = inner.enter_context(nc.sbuf_tensor(f"{nm}_q", [P, 2 * PH, TPAD], F32))
            linear(nc, f"{nm}q", dr["w_peer_q"][layer], DC, 2 * PH, xn, "act",
                   lambda eng, o, res: eng.activation(
                       q[:, bass.ds(o, 1), 0:T].rearrange("p a (b n) -> p (a b) n", b=2), res, ACT.Copy))
            select_experts(nc, dr, cst, layer, nm, q, sel, xn)
        spread_gates(nc, dr, cst, layer, nm, sel, xn)
    all_experts(nc, dr, cst, layer, nm, xn, h)


def select_experts(nc, dr, cst, layer, nm, q, sel, xn):
    NQ = 2 * PH
    with Stage(nc, f"{nm}s") as st:
        keys = st.sb("keys", [P, NQ, P])
        qs = st.sb("qs", [P, NQ, P])
        work = st.sb("work", [P, NQ, P])
        top = st.sb("top", [P, NQ, PK])
        topi = st.sb("topi", [P, NQ, PK], U32)
        topf = st.sb("topf", [P, NQ, PK])
        cand = st.sb("cand", [P, PH, PK * PK])
        work2 = work[:].rearrange("p (h c) n -> p h (c n)", c=2)
        sv = st.sb("sv", [P, PH, PK])
        pos = st.sb("pos", [P, PH, PK], U32)
        ab = st.sb("ab", [P, 2, PH, PK], U32)
        abf = st.sb("abf", [P, 2, PH, PK])
        eq = cand[:].rearrange("p h (k a) -> p h k a", a=PK)
        res = st.sb("res", [P, 3, PH, PK])
        sm = st.sb("sm", [P, PH])
        sc = st.ps("sc", [P, NQ, P])
        tr = sc[:, 0:3, :]
        acts = Activities(nc, st, dr, layer, xn, JB, 0, 2 * NT)
        keys_in = st.sem("keys_in")
        padded = st.sem("padded")
        staged = st.sem("staged")
        scored = st.sem("scored")
        spare = st.sb("spare", [P, 1])
        sc_read = st.sem("sc_read")
        sv_ready = st.sem("sv_ready")
        gates_exp = st.sem("gates_exp")
        res_ready = st.sem("res_ready")
        turned = st.sem("turned")
        kept = st.sem("kept")
        with st.block() as block:

            @block.sync
            def _(sp):
                sp.dma_start(keys[:], dr["peer_keys"][layer]).then_inc(keys_in, 16)

                def unit(i, k, first):
                    acts.load(sp, i, k, first)
                    if k:
                        acts.store(sp, i, 0, first)
                    elif not first:
                        acts.store(sp, i - 1, 1, first)

                paired(sp, acts.n, unit)
                acts.store(sp, NT - 1, 1, True)
                acts.stored(sp)

            @block.gpsimd
            def _(pool):
                pool.memset(q[:, :, T:TPAD], 0.0).then_inc(padded, 1)

            @block.scalar
            def _(act):
                act.wait_ge(padded, 1)

                def tile(t, first):
                    if not first:
                        act.wait_ge(scored, t)
                    act.activation(qs[:], q[:, :, bass.ds(t * P, P)], ACT.Copy).then_inc(staged, 1)
                    for n in range(2 * JB):
                        if n == 6:
                            act.wait_ge(sv_ready, t + 1)
                            act.activation(res[:, 2, :, :], sv[:], ACT.Exp).then_inc(gates_exp, 1)
                        acts.gelu(act, t, n // JB, n % JB, first)
                    act.wait_ge(turned, t + 1)
                    act.activation(sel[:, :, bass.ds(t * P, P)], tr, ACT.Copy).then_inc(kept, 1)

                looped(act, NT, tile)

            @block.tensor
            def _(pe):
                pe.wait_ge(keys_in, 16)

                def tile(t, first):
                    pe.wait_ge(staged, t + 1)
                    if not first:
                        pe.wait_ge(kept, t)
                    for n in range(NQ):
                        last = pe.matmul(sc[:, n, :], qs[:, n, :], keys[:, n, :], start=True, stop=True)
                    last.then_inc(scored, 1)
                    for n in range(2 * JB):
                        acts.score(pe, t, n // JB, n % JB, first)
                    pe.wait_ge(res_ready, t + 1)
                    for n in range(3):
                        last = pe.transpose(tr[:, n, :], res[:, n, :, :].rearrange("p h k -> p (h k)"), cst["ident"])
                    last.then_inc(turned, 1)

                looped(pe, NT, tile)

            @block.vector
            def _(dve):
                dve.memset(spare[:], 0.0)
                dve.drain()

                def tile(t, first):
                    wait_apart(dve, scored, t + 1, spare[:])
                    for n in range(NQ):
                        dve.max(top[:, n, 0:8], sc[:, n, :])
                    dve.drain()
                    for n in range(NQ):
                        dve.max_index(topi[:, n, 0:8], top[:, n, 0:8], sc[:, n, :])
                        last = dve.match_replace(work[:, n, :], top[:, n, 0:8], sc[:, n, :], -3e38)
                    last.then_inc(sc_read, 1)
                    dve.drain()
                    for n in range(NQ):
                        dve.max(top[:, n, 8:16], work[:, n, :])
                    dve.drain()
                    for n in range(NQ):
                        dve.max_index(topi[:, n, 8:16], top[:, n, 8:16], work[:, n, :])
                    dve.drain()
                    dve.tensor_copy(topf[:], topi[:])
                    pair = top[:].rearrange("p (h c) k -> p h c k", c=2)
                    dve.tensor_tensor(cand[:].rearrange("p h (a b) -> p h a b", b=PK),
                                      pair[:, :, 0, :].unsqueeze(3).to_broadcast([P, PH, PK, PK]),
                                      pair[:, :, 1, :].unsqueeze(2).to_broadcast([P, PH, PK, PK]), ALU.add)
                    dve.drain()
                    for n in range(PH):
                        dve.max(sv[:, n, 0:8], cand[:, n, :])
                    dve.drain()
                    for n in range(PH):
                        dve.max_index(pos[:, n, 0:8], sv[:, n, 0:8], cand[:, n, :])
                        dve.match_replace(work2[:, n, :], sv[:, n, 0:8], cand[:, n, :], -3e38)
                    dve.drain()
                    for n in range(PH):
                        dve.max(sv[:, n, 8:16], work2[:, n, :])
                    dve.drain()
                    for n in range(PH):
                        dve.max_index(pos[:, n, 8:16], sv[:, n, 8:16], work2[:, n, :])
                    dve.drain()
                    if not first:
                        dve.wait_ge(turned, t)
                    dve.tensor_tensor(sm[:].unsqueeze(2), sv[:, :, 0:1], sv[:, :, 0:1], ALU.max)
                    dve.tensor_scalar(ab[:, 0, :, :], pos[:], 4, None, ALU.logical_shift_right)
                    dve.tensor_scalar(ab[:, 1, :, :], pos[:], 15, None, ALU.bitwise_and)
                    dve.drain()
                    dve.tensor_tensor(sv[:], sv[:], sm[:].unsqueeze(2).to_broadcast([P, PH, PK]), ALU.subtract)\
                       .then_inc(sv_ready, 1)
                    dve.tensor_copy(abf[:], ab[:])
                    dve.drain()
                    iota = cst["iota"][:, 0:PK].unsqueeze(1).unsqueeze(1).to_broadcast([P, PH, PK, PK])
                    idx = topf[:].rearrange("p (h c) k -> p h c k", c=2)
                    for c in range(2):
                        dve.tensor_tensor(eq, iota, abf[:, c, :, :].unsqueeze(3).to_broadcast([P, PH, PK, PK]),
                                          ALU.is_equal)
                        dve.drain()
                        dve.tensor_tensor(eq, eq, idx[:, :, c, :].unsqueeze(2).to_broadcast([P, PH, PK, PK]), ALU.mult)
                        dve.drain()
                        dve.tensor_reduce(res[:, c, :, :], eq, AX, ALU.add)
                        dve.drain()
                    dve.wait_ge(gates_exp, t + 1)
                    dve.tensor_reduce(sm[:], res[:, 2, :, :], AX, ALU.add)
                    dve.drain()
                    dve.reciprocal(sm[:], sm[:])
                    dve.drain()
                    dve.tensor_tensor(res[:, 2, :, :], res[:, 2, :, :],
                                      sm[:].unsqueeze(2).to_broadcast([P, PH, PK]), ALU.mult)
                    dve.drain().then_inc(res_ready, 1)

                looped(dve, NT, tile)


def spread_gates(nc, dr, cst, layer, nm, sel, xn):
    NQ4 = TB // 4
    DEPTH = 4
    with Stage(nc, f"{nm}g") as st:
        cols = st.sb("cols", [P, 2, 3, TB])
        cols_p = st.sb("cols_p", [P, TB])
        spare = st.sb("spare", [P, NQ4])
        one_i = st.sb("one_i", [P, DEPTH, 4, P])
        one_j = st.sb("one_j", [P, DEPTH, 4, P])
        grid = st.sb("grid", [P, 2, P, TB])
        gp = st.ps("gp", [P, 2, 4, P])
        acts = Activities(nc, st, dr, layer, xn, 2, 2 * N_SEL, NTB)
        i_ready = st.sem("i_ready")
        j_ready = st.sem("j_ready")
        multiplied = st.sem("multiplied")
        taken = st.sem("taken")
        grid_out = [st.sem(f"grid_out{k}") for k in range(2)]
        with st.block() as block:

            def hot_j(eng, c, r, w):
                return eng.tensor_scalar(one_j[:, r % DEPTH, w, :], cst["iota"], c[:, 4 * r + w:4 * r + w + 1],
                                         None, ALU.is_equal)

            @block.vector
            def _(dve):
                def batch(i, k, first):
                    tb = i * 2 + k
                    dve.tensor_copy(cols[:, k, :, :], sel[:, :, bass.ds(tb * TB, TB)])
                    dve.drain()
                    for r in range(NQ4):
                        if not (first and k == 0 and r < DEPTH):
                            dve.wait_ge(multiplied, tb * NQ4 + r + 1 - DEPTH)
                        for w in range(4):
                            dve.tensor_scalar(one_i[:, r % DEPTH, w, :], cst["iota"],
                                              cols[:, k, 0, 4 * r + w:4 * r + w + 1],
                                              cols[:, k, 2, 4 * r + w:4 * r + w + 1], ALU.is_equal, ALU.mult)
                        for w in range(2):
                            last = hot_j(dve, cols[:, k, 1, :], r, w)
                        last.then_inc(i_ready, 1)

                paired(dve, NTB, batch)

            @block.gpsimd
            def _(pool):
                def batch(i, k, first):
                    tb = i * 2 + k
                    if first and k == 0:
                        pool.memset(spare[:], 0.0)
                    pool.tensor_copy(cols_p[:], sel[:, 1, bass.ds(tb * TB, TB)])
                    pool.drain()
                    for r in range(NQ4):
                        if not (first and k == 0 and r < DEPTH):
                            wait_apart(pool, multiplied, tb * NQ4 + r + 1 - DEPTH, spare[:, r:r + 1])
                        for w in range(2, 4):
                            last = hot_j(pool, cols_p, r, w)
                        last.then_inc(j_ready, 1)
                    pool.drain()

                paired(pool, NTB, batch)

            @block.tensor
            def _(pe):
                def batch(i, k, first):
                    tb = i * 2 + k
                    for r in range(NQ4):
                        if r % (NQ4 // 2) == 0:
                            acts.score(pe, i, k, r // (NQ4 // 2), first)
                        n = tb * NQ4 + r
                        pe.wait_ge(i_ready, n + 1)
                        pe.wait_ge(j_ready, n + 1)
                        if not (first and k == 0 and r < 2):
                            pe.wait_ge(taken, n - 1)
                        for w in range(4):
                            last = pe.matmul(gp[:, r % 2, w, :], one_i[:, r % DEPTH, w, :], one_j[:, r % DEPTH, w, :],
                                             start=True, stop=True)
                        last.then_inc(multiplied, 1)

                paired(pe, NTB, batch)

            @block.scalar
            def _(act):
                def batch(i, k, first):
                    tb = i * 2 + k
                    for r in range(NQ4):
                        if r % (NQ4 // 2) == 0:
                            acts.gelu(act, i, k, r // (NQ4 // 2), first)
                        if r == 0 and not first:
                            act.wait_ge(grid_out[k], i * 16)
                        act.wait_ge(multiplied, tb * NQ4 + r + 1)
                        act.activation(grid[:, k, :, 4 * r:4 * r + 4].rearrange("p j w -> p w j"), gp[:, r % 2, :, :],
                                       ACT.Copy).then_inc(taken, 1)

                paired(act, NTB, batch)

            @block.sync
            def _(sp):
                def grid_store(i, k, first):
                    tb = i * 2 + k
                    dst = dr["gates"][bass.ds(tb if first else sp.snap(tb), 1)]
                    sp.wait_ge(taken, tb * NQ4 + NQ4)
                    sp.dma_start(dst.rearrange("a p n -> p (a n)"), grid[:, k, :, :].rearrange("p j w -> p (j w)"))\
                      .then_inc(grid_out[k], 16)

                def batch(i, k, first):
                    acts.load(sp, i, k, first)
                    if k:
                        acts.store(sp, i, 0, first)
                        grid_store(i, 0, first)
                    elif not first:
                        acts.store(sp, i - 1, 1, first)
                        grid_store(i - 1, 1, first)

                paired(sp, NTB, batch)
                acts.store(sp, NTB // 2 - 1, 1, True)
                grid_store(NTB // 2 - 1, 1, True)
                acts.stored(sp)
                for k in range(2):
                    sp.wait_ge(grid_out[k], NTB // 2 * 16)


def all_experts(nc, dr, cst, layer, nm, xn, h):
    with Stage(nc, f"{nm}e") as st:
        ut = st.sb("ut", [P, 2, DC, JB * P])
        vt = st.sb("vt", [P, 2, JB, D])
        gt = st.sb("gt", [P, 2, NTB, JB * TB])
        act_s = st.sb("act_s", [P, 2, T])
        w = st.sb("w", [P, 2, JB, T])
        s_ps = st.ps("s_ps", [P, 2, 2, 512])
        y_ps = st.ps("y_ps", [P, 2, 2, 512])
        u_in = [st.sem(f"u_in{k}") for k in range(2)]
        s_in = [st.sem(f"s_in{k}") for k in range(2)]
        v_in = [st.sem(f"v_in{k}") for k in range(2)]
        g_in = [st.sem(f"g_in{k}") for k in range(2)]
        s_ready = st.sem("s_ready")
        gelued = st.sem("gelued")
        act_used = st.sem("act_used")
        w_ready = st.sem("w_ready")
        y_ready = st.sem("y_ready")
        y_added = st.sem("y_added")
        A_PAIRS = N_PRE // 2
        B_PAIRS = (N_PRE + 2) // 2
        NEW = N_PRE
        assert N_PRE % 2 == 1
        with st.block() as block:

            @block.sync
            def _(sp):
                def load(i, k, first, fresh):
                    n = i * 2 + k
                    static = isinstance(n, int)
                    m = n if static else sp.snap(n)
                    us, vs = dr["peer_ut"][layer][bass.ds(m, 1)], dr["peer_v"][layer][bass.ds(m, 1)]
                    ss = dr["activities"][bass.ds(m, 1)]
                    gs = dr["gates"][:, :, bass.ds(m * (JB * TB), JB * TB)]
                    if fresh:
                        if not static or n >= NEW + 2:
                            sp.wait_ge(s_ready, (n - NEW - 1) * JB)
                        sp.dma_start(ut[:, k, :, :].rearrange("p c n -> p (c n)"), us.rearrange("a p n -> p (a n)"))\
                          .then_inc(u_in[k], 16)
                    if not first:
                        sp.wait_ge(w_ready, n - 1)
                    sp.dma_start(gt[:, k, :, :], gs.rearrange("b p n -> p b n")).then_inc(g_in[k], 16)
                    if not first:
                        sp.wait_ge(y_ready, n * DC - DC)
                    if not fresh:
                        sp.dma_start(w[:, k, :, :].rearrange("p j n -> p (j n)"), ss.rearrange("a p n -> p (a n)"))\
                          .then_inc(s_in[k], 16)
                    sp.dma_start(vt[:, k, :, :].rearrange("p c n -> p (c n)"), vs.rearrange("a p n -> p (a n)"))\
                      .then_inc(v_in[k], 16)

                for k in range(2):
                    load(0, k, True, False)
                with sp.Fori(1, A_PAIRS) as i:
                    for k in range(2):
                        load(i, k, False, False)
                load(A_PAIRS, 0, False, False)
                load(A_PAIRS, 1, False, True)
                with sp.Fori(B_PAIRS, NJB // 2) as i:
                    for k in range(2):
                        load(i, k, False, True)

            @block.tensor
            def _(pe):
                def score(i, k, first):
                    m = i * 2 + k - NEW
                    pe.wait_ge(u_in[k], (i - A_PAIRS if k else i - B_PAIRS) * 16 + 16)
                    for j in range(JB):
                        if not (first and j < 2):
                            pe.wait_ge(gelued, m * JB + j - 1)
                        for c in range(DC):
                            for a in range(2):
                                last = pe.matmul(s_ps[:, j % 2, a, 0:HALF], ut[:, k, c, j * P:(j + 1) * P],
                                                 xn[:, c, a * HALF:(a + 1) * HALF],
                                                 start=(c == 0), stop=(c == DC - 1))
                        last.then_inc(s_ready, 1)

                def combine(i, k, first):
                    pe.wait_ge(v_in[k], i * 16 + 16)
                    pe.wait_ge(w_ready, i * 2 + k + 1)
                    for c in range(DC):
                        if not (first and c < 2):
                            pe.wait_ge(y_added, (i * 2 + k) * DC + c - 1)
                        for j in range(JB):
                            for a in range(2):
                                last = pe.matmul(y_ps[:, c % 2, a, 0:HALF], vt[:, k, j, c * P:(c + 1) * P],
                                                 w[:, k, j, a * HALF:(a + 1) * HALF],
                                                 start=(j == 0), stop=(j == JB - 1))
                        last.then_inc(y_ready, 1)

                combine(0, 0, True)
                combine(0, 1, False)
                with pe.Fori(1, A_PAIRS) as i:
                    for k in range(2):
                        combine(i, k, False)
                score(A_PAIRS, 1, True)
                combine(A_PAIRS, 0, False)
                with pe.Fori(B_PAIRS, NJB // 2) as i:
                    score(i, 0, False)
                    combine(i - 1, 1, False)
                    score(i, 1, False)
                    combine(i, 0, False)
                combine(NJB // 2 - 1, 1, False)

            @block.scalar
            def _(act):
                def one(i, k, first):
                    for j in range(JB):
                        n = (i * 2 + k - NEW) * JB + j
                        act.wait_ge(s_ready, n + 1)
                        if not (first and j < 2):
                            act.wait_ge(act_used, n - 1)
                        act.activation(halves(act_s[:, j % 2, :]), s_ps[:, j % 2, :, 0:HALF], ACT.Gelu_apprx_tanh)\
                           .then_inc(gelued, 1)

                one(A_PAIRS, 1, True)
                with act.Fori(B_PAIRS, NJB // 2) as i:
                    for k in range(2):
                        one(i, k, False)

            @block.vector
            def _(dve):
                def gate(k):
                    return gt[:, k, :, :].rearrange("p b (j n) -> p j b n", j=JB)

                def weigh_stored(i, k):
                    dve.wait_ge(g_in[k], i * 16 + 16)
                    dve.wait_ge(s_in[k], i * 16 + 16)
                    a = w[:, k, :, :].rearrange("p j (b n) -> p j b n", n=TB)
                    dve.tensor_tensor(a, a, gate(k), ALU.mult).then_inc(w_ready, 1)

                def weigh(i, k):
                    dve.wait_ge(g_in[k], i * 16 + 16)
                    dve.wait_ge(y_ready, (i * 2 + k - 1) * DC)
                    for j in range(JB):
                        dve.wait_ge(gelued, (i * 2 + k - NEW) * JB + j + 1)
                        dve.tensor_tensor(w[:, k, j, :].rearrange("p (b n) -> p b n", n=TB),
                                          act_s[:, j % 2, :].rearrange("p (b n) -> p b n", n=TB),
                                          gate(k)[:, j], ALU.mult).then_inc(act_used, 1)
                    dve.drain().then_inc(w_ready, 1)

                def add(i, k):
                    for c in range(DC):
                        dve.wait_ge(y_ready, (i * 2 + k) * DC + c + 1)
                        dst = halves(h[:, c, :])
                        dve.tensor_tensor(dst, dst, y_ps[:, c % 2, :, 0:HALF], ALU.add).then_inc(y_added, 1)
                    dve.drain()

                weigh_stored(0, 0)
                weigh_stored(0, 1)
                add(0, 0)
                with dve.Fori(1, A_PAIRS) as i:
                    weigh_stored(i, 0)
                    add(i - 1, 1)
                    weigh_stored(i, 1)
                    add(i, 0)
                weigh_stored(A_PAIRS, 0)
                add(A_PAIRS - 1, 1)
                weigh(A_PAIRS, 1)
                add(A_PAIRS, 0)
                with dve.Fori(B_PAIRS, NJB // 2) as i:
                    weigh(i, 0)
                    add(i - 1, 1)
                    weigh(i, 1)
                    add(i, 0)
                add(NJB // 2 - 1, 1)



def ple(nc, dr, cst, layer, xn, h):
    with ExitStack() as ctx:
        gate = ctx.enter_context(nc.sbuf_tensor(f"ple{layer}_gate", [P, DC, T], F32))
        emb = ctx.enter_context(nc.sbuf_tensor(f"ple{layer}_emb", [P, 2, T], F32))
        with Stage(nc, f"ple{layer}i") as st:
            landed = st.sem("landed")
            with st.block() as block:

                @block.sync
                def _(sp):
                    sp.dma_start(emb[:], dr["pT"][layer]).then_inc(landed, 16)
                    sp.wait_ge(landed, 16)

        linear(nc, f"ple{layer}g", dr["w_ple_g"][layer], DC, DC, xn, "act", to_buffer(gate, func=ACT.Sigmoid))

        def evac(eng, o, res):
            buf = halves(at(gate, o))
            eng.tensor_tensor(buf, buf, res, ALU.mult)
            eng.drain()
            dst = at(h, o)
            return eng.tensor_tensor(dst, dst, at(gate, o), ALU.add)

        linear(nc, f"ple{layer}p", dr["w_ple_p"][layer], 2, DC, emb, "dve", evac)



def bias_lines(nc, dr, cst):
    with Stage(nc, "bl") as st:
        rb = st.sb("rb", [33, H])
        rep = st.sb("rep", [33, H, P])
        hot = st.sb("hot", [33, BW])
        line = st.sb("line", [P, 2, BW])
        ps = st.ps("ps", [P, 2, 2, 512])
        landed = st.sem("landed")
        spread = st.sem("spread")
        multiplied = st.sem("multiplied")
        copied = st.sem("copied")
        written = [st.sem(f"written{k}") for k in range(2)]
        with st.block() as block:

            @block.sync
            def _(sp):
                sp.dma_start(rb[:], dr["rel_bias"]).then_inc(landed, 16)
                sp.dma_start(hot[:], dr["bucket_hot"]).then_inc(landed, 16)
                for n in range(H):
                    sp.wait_ge(copied, n + 1)
                    sp.dma_start(dr["bias_rows"][n], line[:, n % 2, :]).then_inc(written[n % 2], 16)
                for k in range(2):
                    sp.wait_ge(written[k], 16 * H // 2)

            @block.vector
            def _(dve):
                dve.wait_ge(landed, 32)
                dve.tensor_copy(rep[:], rb[:].unsqueeze(2).to_broadcast([33, H, P])).then_inc(spread, 1)

            @block.tensor
            def _(pe):
                pe.wait_ge(spread, 1)
                for n in range(H):
                    if n >= 2:
                        pe.wait_ge(copied, n - 1)
                    for a in range(2):
                        last = pe.matmul(ps[:, n % 2, a, 0:BW // 2], rep[:, n, :], hot[:, a * BW // 2:(a + 1) * BW // 2],
                                         start=True, stop=True)
                    last.then_inc(multiplied, 1)

            @block.scalar
            def _(act):
                for n in range(H):
                    act.wait_ge(multiplied, n + 1)
                    if n >= 2:
                        act.wait_ge(written[n % 2], 16 * (n // 2))
                    act.activation(line[:, n % 2, :].rearrange("p (a n) -> p a n", a=2), ps[:, n % 2, :, 0:BW // 2], ACT.Copy)\
                       .then_inc(copied, 1)


def attention(nc, dr, cst, qk, v, out):
    with ExitStack() as outer:
        lam = outer.enter_context(nc.sbuf_tensor("at_lam", [P, 4], F32))
        with Stage(nc, "al") as st:
            lv = st.sb("lv", [P, 4, CHD])
            pr = st.sb("pr", [P, 2, CHD])
            s2 = st.sb("s2", [P, 2])
            landed = st.sem("landed")
            summed = st.sem("summed")
            exped = st.sem("exped")
            with st.block() as block:

                @block.sync
                def _(sp):
                    sp.dma_start(lv[:], dr["c_lam"]).then_inc(landed, 16)
                    sp.wait_ge(landed, 16)

                @block.vector
                def _(dve):
                    dve.wait_ge(landed, 16)
                    dve.tensor_tensor(pr[:], lv[:, 0:2, :], lv[:, 2:4, :], ALU.mult)
                    dve.drain()
                    dve.tensor_reduce(s2[:], pr[:], AX, ALU.add).then_inc(summed, 1)
                    dve.wait_ge(exped, 1)
                    dve.tensor_tensor(lam[:, 0:1], s2[:, 0:1], s2[:, 1:2], ALU.subtract)
                    dve.drain()
                    dve.tensor_scalar(lam[:, 0:1], lam[:, 0:1], LAM_INIT, None, ALU.add)
                    dve.drain()
                    dve.tensor_scalar(lam[:, 1:2], lam[:, 0:1], -1.0, None, ALU.mult)
                    dve.drain()
                    dve.scalar_tensor_tensor(out=lam[:, 2:3], in0=cst["map_rows"][:, 1:2], scalar=lam[:, 1:2],
                                             in1=cst["map_rows"][:, 0:1], op0=ALU.mult, op1=ALU.add)

                @block.scalar
                def _(act):
                    act.wait_ge(summed, 1)
                    act.activation(s2[:], s2[:], ACT.Exp).then_inc(exped, 1)

        prompt_attention(nc, dr, cst, qk, v, out, lam)
        sample_attention(nc, dr, cst, qk, v, out, lam)


def prompt_attention(nc, dr, cst, qk, v, out, lam):
    NQB = TP // P
    with Stage(nc, "pa") as st:
        qs = st.sb("qs", [P, 2, TP])
        ks = st.sb("ks", [P, 2, TP])
        vs = st.sb("vs", [P, 2, NQB, P])
        bias = st.sb("bias", [P, 2, TP])
        sc = st.sb("sc", [P, 2, 2, TP])
        mx = st.sb("mx", [P, 2, 2])
        sm = st.sb("sm", [P, 2, 2])
        a = st.sb("a", [P, 2, TP])
        at_ = st.sb("at", [P, 2, TP])
        s_ps = st.ps("s_ps", [P, 2, 512])
        t_ps = st.ps("t_ps", [P, 2, 512])
        o_ps = st.ps("o_ps", [P, 2, 512])
        bias_in = [st.sem(f"bias_in{k}") for k in range(2)]
        staged = st.sem("staged")
        scored = st.sem("scored")
        sc_read = st.sem("sc_read")
        mx_ready = st.sem("mx_ready")
        exped = st.sem("exped")
        a_ready = st.sem("a_ready")
        turned = st.sem("turned")
        at_ready = st.sem("at_ready")
        o_ready = st.sem("o_ready")
        o_taken = st.sem("o_taken")
        with st.block() as block:

            @block.sync
            def _(sp):
                def load(i, k, first):
                    n = i * 2 + k
                    src = dr["bias_skew"][bass.ds(n if first else sp.snap(n), 1)]
                    if not first:
                        sp.wait_ge(sc_read, (n - 1) * NQB)
                    sp.dma_start(bias[:, k, :], src.rearrange("a p n -> p (a n)")).then_inc(bias_in[k], 16)

                paired(sp, H, load)

            @block.gpsimd
            def _(pool):
                def stage(i, k, first):
                    n = i * 2 + k
                    if not first:
                        pool.wait_ge(o_ready, (n - 1) * NQB)
                    pool.tensor_copy(qs[:, k, :], qk[:, bass.ds(n, 1), 0:TP].rearrange("p a n -> p (a n)"))
                    pool.tensor_copy(ks[:, k, :], qk[:, bass.ds(n + H, 1), 0:TP].rearrange("p a n -> p (a n)"))
                    pool.tensor_copy(vs[:, k, :, :], v[:, 0:NQB, bass.ds(n * P, P)]).then_inc(staged, 1)

                paired(pool, H, stage)

            @block.tensor
            def _(pe):
                def head(i, k, first):
                    n = i * 2 + k
                    pe.wait_ge(staged, n + 1)

                    def score(qb):
                        m = n * NQB + qb
                        if not (first and k == 0 and qb == 0):
                            pe.wait_ge(sc_read, m)
                        for c in range(2):
                            rows = slice(c * CHD, (c + 1) * CHD)
                            last = pe.matmul(s_ps[:, c, 0:(qb + 1) * P], qs[rows, k, qb * P:(qb + 1) * P],
                                             ks[rows, k, 0:(qb + 1) * P],
                                             start=True, stop=True)
                        last.then_inc(scored, 1)

                    def combine(qb):
                        m = n * NQB + qb
                        pe.wait_ge(a_ready, m + 1)
                        if not (first and k == 0 and qb < 2):
                            pe.wait_ge(at_ready, m - 1)
                        for kb in range(qb + 1):
                            last = pe.transpose(t_ps[:, qb % 2, kb * P:(kb + 1) * P], a[:, qb % 2, kb * P:(kb + 1) * P],
                                                cst["ident"])
                        last.then_inc(turned, 1)
                        pe.wait_ge(at_ready, m + 1)
                        if not (first and k == 0 and qb < 2):
                            pe.wait_ge(o_taken, m - 1)
                        for kb in range(qb + 1):
                            last = pe.matmul(o_ps[:, qb % 2, 0:P], vs[:, k, kb, :], at_[:, qb % 2, kb * P:(kb + 1) * P],
                                             start=(kb == 0), stop=(kb == qb))
                        last.then_inc(o_ready, 1)

                    score(0)
                    for qb in range(NQB):
                        if qb + 1 < NQB:
                            score(qb + 1)
                        combine(qb)

                paired(pe, H, head)

            @block.vector
            def _(dve):
                def head(i, k, first):
                    n = i * 2 + k
                    dve.wait_ge(bias_in[k], i * 16 + 16)
                    for qb in range(NQB):
                        m = n * NQB + qb
                        w = (qb + 1) * P
                        s, z = sc[:, qb % 2, :, 0:w], qb % 2
                        dve.wait_ge(scored, m + 1)
                        for c in range(2):
                            last = dve.scalar_tensor_tensor(out=sc[:, z, c, 0:w], in0=s_ps[:, c, 0:w], scalar=CHD ** -0.5,
                                                            in1=bias[:, k, TP - w:TP], op0=ALU.mult, op1=ALU.add)
                        last.then_inc(sc_read, 1)
                        dve.drain()
                        dve.tensor_reduce(mx[:, z, :], s, AX, ALU.max, negate=True).then_inc(mx_ready, 1)
                        dve.wait_ge(exped, m + 1)
                        dve.reciprocal(sm[:, z, :], sm[:, z, :])
                        dve.drain()
                        dve.tensor_scalar(sm[:, z, 1:2], sm[:, z, 1:2], lam[:, 1:2], None, ALU.mult)
                        if not (first and k == 0 and qb < 2):
                            dve.wait_ge(turned, m - 1)
                        dve.tensor_scalar(a[:, z, 0:w], sc[:, z, 0, 0:w], sm[:, z, 0:1], None, ALU.mult)
                        dve.drain()
                        dve.scalar_tensor_tensor(out=a[:, z, 0:w], in0=sc[:, z, 1, 0:w], scalar=sm[:, z, 1:2],
                                                 in1=a[:, z, 0:w], op0=ALU.mult, op1=ALU.add).then_inc(a_ready, 1)

                paired(dve, H, head)

            @block.scalar
            def _(act):
                def head(i, k, first):
                    n = i * 2 + k

                    def take(qb):
                        m = n * NQB + qb
                        act.wait_ge(turned, m + 1)
                        act.activation(at_[:, qb % 2, 0:(qb + 1) * P], t_ps[:, qb % 2, 0:(qb + 1) * P], ACT.Copy)\
                           .then_inc(at_ready, 1)
                        act.wait_ge(o_ready, m + 1)
                        act.activation(out[:, bass.ds(n, 1), qb * P:(qb + 1) * P].rearrange("p a n -> p (a n)"),
                                       o_ps[:, qb % 2, 0:P], ACT.Copy).then_inc(o_taken, 1)

                    for qb in range(NQB):
                        m = n * NQB + qb
                        w = (qb + 1) * P
                        act.wait_ge(mx_ready, m + 1)
                        for c in range(2):
                            last = act.activation(sc[:, qb % 2, c, 0:w], sc[:, qb % 2, c, 0:w], ACT.Exp,
                                                  bias=mx[:, qb % 2, c:c + 1], accum_out=sm[:, qb % 2, c:c + 1])
                        last.then_inc(exped, 1)
                        take(qb)

                paired(act, H, head)


def sample_attention(nc, dr, cst, qk, v, out, lam):
    NP = PAST // PAGE
    with Stage(nc, "sa") as st:
        pages = st.sb("pages", [P, NB * NP], I32)
        pagef = st.sb("pagef", [P, NB * NP])
        rows = st.sb("rows", [P, NB * NP], U32)
        kc = st.sb("kc", [P, 2, NP, D])
        vc = st.sb("vc", [P, 2, NP, D])
        kt = st.sb("kt", [P, H, PAST])
        qd = st.sb("qd", [P, H * (P + 16)])
        bpast = st.sb("bpast", [P, PAST + TS])
        bnew = st.sb("bnew", [P, NB * (NB * TS + TS)])
        sc = st.sb("sc", [P, PAST + NB * TS])
        mx = st.sb("mx", [P, 1])
        sm = st.sb("sm", [P, 1])
        a = st.sb("a", [P, PAST + NB * TS])
        at_ = st.sb("at", [P, 3, P])
        osb = st.sb("osb", [P, H, 2, TS])
        k_ps = st.ps("k_ps", [P, 2, 4, P])
        s_ps = st.ps("s_ps", [P, 2, 512])
        t_ps = st.ps("t_ps", [P, 3, P])
        o_ps = st.ps("o_ps", [P, H, 2, TS])
        landed = st.sem("landed")
        rows_ready = st.sem("rows_ready")
        qd_zero = st.sem("qd_zero")
        qd_ready = st.sem("qd_ready")
        k_turned = st.sem("k_turned")
        kt_ready = st.sem("kt_ready")
        scored = st.sem("scored")
        mx_ready = st.sem("mx_ready")
        exped = st.sem("exped")
        a_ready = st.sem("a_ready")
        turned = st.sem("turned")
        at_ready = st.sem("at_ready")
        o_ready = st.sem("o_ready")
        o_copied = st.sem("o_copied")
        o_taken = st.sem("o_taken")
        kv_in = dr["kv_in"]
        NG = NP * H // 4
        with st.block() as block:

            @block.sync
            def _(sp):
                sp.dma_start(pages[:], dr["pages"]).then_inc(landed, 16)
                for n in range(H):
                    for c in range(2):
                        sp.dma_start(bpast[n * 16 + c * TS:n * 16 + (c + 1) * TS, :], dr["bias_past"][n])\
                          .then_inc(landed, 16)
                sp.wait_ge(landed, 16 * (1 + 2 * H))

            @block.gpsimd
            def _(pool):
                pool.memset(qd[:], 0.0).then_inc(qd_zero, 1)
                pool.memset(bnew[:], NEG).then_inc(qd_zero, 1)
                pool.wait_ge(rows_ready, 1)
                for b in range(NB):
                    if b >= 2:
                        pool.wait_ge(o_ready, b - 1)
                    for g in range(NP):
                        for dst, src in ((kc, "cache_k"), (vc, "cache_v")):
                            pool.indirect_dma_start(
                                dst[:, b % 2, g, :], None, dr[src],
                                bass.IndirectOffsetOnAxis(ap=rows[:, b * NP + g:b * NP + g + 1], axis=0))\
                                .then_inc(kv_in[b % 2], 16)

            @block.vector
            def _(dve):
                dve.wait_ge(landed, 16 * (1 + 2 * H))
                dve.tensor_copy(pagef[:], pages[:])
                dve.drain()
                dve.tensor_scalar(pagef[:], pagef[:], float(PAGE), cst["part"], ALU.mult, ALU.add)
                dve.drain()
                dve.tensor_copy(rows[:], pagef[:]).then_inc(rows_ready, 1)
                dve.wait_ge(qd_zero, 2)
                dve.tensor_copy(
                    bnew[:].rearrange("p (b n) -> p b n", b=NB)[:, :, 0:TS],
                    bpast[:, PAST:PAST + TS].unsqueeze(1).to_broadcast([P, NB, TS]))
                dve.drain()
                for b in range(NB):
                    if b:
                        dve.wait_ge(scored, b)
                    for c in range(2):
                        r = slice(c * CHD, (c + 1) * CHD)
                        last = dve.tensor_copy(
                            qd[r, :].rearrange("p (h n) -> p h n", h=H)[:, :, c * TS:(c + 1) * TS],
                            qk[r, 0:H, TP + b * TS:TP + (b + 1) * TS])
                    last.then_inc(qd_ready, 1)
                    dve.wait_ge(scored, b + 1)
                    dve.scalar_tensor_tensor(out=sc[:, 0:PAST], in0=s_ps[:, 0, 0:PAST], scalar=CHD ** -0.5,
                                             in1=bpast[:, 0:PAST], op0=ALU.mult, op1=ALU.add)
                    dve.scalar_tensor_tensor(out=sc[:, PAST:], in0=s_ps[:, 1, 0:NB * TS], scalar=CHD ** -0.5,
                                             in1=bnew[:, b * NB * TS:(b + 1) * NB * TS], op0=ALU.mult, op1=ALU.add)
                    dve.drain()
                    dve.tensor_reduce(mx[:], sc[:], AX, ALU.max, negate=True).then_inc(mx_ready, 1)
                    dve.wait_ge(exped, b + 1)
                    dve.reciprocal(sm[:], sm[:])
                    dve.drain()
                    dve.tensor_scalar(sm[:], sm[:], lam[:, 2:3], None, ALU.mult)
                    dve.drain()
                    dve.tensor_scalar(a[:], sc[:], sm[:], None, ALU.mult).then_inc(a_ready, 1)
                    dve.wait_ge(o_copied, b + 1)
                    dve.tensor_tensor(out[:, :, TP + b * TS:TP + (b + 1) * TS], osb[:, :, 0, :], osb[:, :, 1, :], ALU.add)\
                       .then_inc(o_taken, 1)

            @block.scalar
            def _(act):
                for b in range(NB):
                    for g in range(NG):
                        act.wait_ge(k_turned, b * NG + g + 1)
                        if b and g == 0:
                            act.wait_ge(scored, b)
                        page, h0 = g // 2, (g % 2) * 4
                        act.activation(kt[:, h0:h0 + 4, page * PAGE:(page + 1) * PAGE], k_ps[:, g % 2, :, :], ACT.Copy)\
                           .then_inc(kt_ready, 1)
                    act.wait_ge(mx_ready, b + 1)
                    act.activation(sc[:], sc[:], ACT.Exp, bias=mx[:], accum_out=sm[:]).then_inc(exped, 1)
                    act.wait_ge(turned, b + 1)
                    act.activation(at_[:, 0:2, :], t_ps[:, 0:2, :], ACT.Copy)
                    act.activation(at_[0:NB * TS, 2, :], t_ps[0:NB * TS, 2, :], ACT.Copy).then_inc(at_ready, 1)
                    act.wait_ge(o_ready, b + 1)
                    if b:
                        act.wait_ge(o_taken, b)
                    act.activation(osb[:], o_ps[:], ACT.Copy).then_inc(o_copied, 1)

            @block.tensor
            def _(pe):
                NK = NB * TS
                for b in range(NB):
                    pe.wait_ge(kv_in[b % 2], 16 * 2 * NP * (b // 2 + 1))
                    for g in range(NG):
                        n = b * NG + g
                        if n >= 2:
                            pe.wait_ge(kt_ready, n - 1)
                        for j in range(4):
                            hh = (g % 2) * 4 + j
                            last = pe.transpose(k_ps[:, g % 2, j, :], kc[:, b % 2, g // 2, hh * P:(hh + 1) * P], cst["ident"])
                        last.then_inc(k_turned, 1)
                    pe.wait_ge(kt_ready, (b + 1) * NG)
                    pe.wait_ge(qd_ready, b + 1)
                    if b:
                        pe.wait_ge(a_ready, b)
                    for n in range(H):
                        pe.matmul(s_ps[:, 0, 0:PAST], qd[:, n * P:(n + 1) * P], kt[:, n, :],
                                  start=(n == 0), stop=(n == H - 1))
                    for n in range(H):
                        last = pe.matmul(s_ps[:, 1, 0:NK], qd[:, n * P:(n + 1) * P], qk[:, H + n, TP:T],
                                         start=(n == 0), stop=(n == H - 1))
                    last.then_inc(scored, 1)
                    pe.wait_ge(a_ready, b + 1)
                    for n in range(2):
                        pe.transpose(t_ps[:, n, :], a[:, n * P:(n + 1) * P], cst["ident"])
                    pe.transpose(t_ps[0:NK, 2, :], a[:, PAST:PAST + NK], cst["ident"]).then_inc(turned, 1)
                    pe.wait_ge(at_ready, b + 1)
                    if b:
                        pe.wait_ge(o_copied, b)
                    for n in range(H):
                        cols = slice(n * 16, (n + 1) * 16)
                        o = o_ps[:, n, :, :].rearrange("p c t -> p (c t)")
                        for g in range(NP):
                            pe.matmul(o, vc[:, b % 2, g, n * P:(n + 1) * P], at_[:, g, cols], start=(g == 0), stop=False)
                        last = pe.matmul(o, v[0:NK, TP // P, n * P:(n + 1) * P], at_[0:NK, 2, cols], start=False, stop=True)
                    last.then_inc(o_ready, 1)



CONST_COLS = dict(gains=48, s5_d=4, s5_glu_b=4, hgrn_norm=1, qk_norm=2, subln=1)


def program(nc, dr, upto=99, dumps=None):
    with ExitStack() as ctx:
        def sb(name, shape, dt=F32):
            return ctx.enter_context(nc.sbuf_tensor(name, shape, dt))

        h = sb("h", [P, DC, T])
        xn = sb("xn", [P, DC, T])
        small = sb("small", [P, sum(CONST_COLS.values())])
        ident = sb("ident", [P, P])
        ones = sb("ones", [P, P])
        ones2 = sb("ones2", [P, P])
        iota = sb("iota", [P, P])
        part = sb("part", [P, 1])
        map_rows = sb("map_rows", [P, 2])
        eps = sb("eps", [P, 1])
        cst = dict(ident=ident[:], ones=ones[:], ones2=ones2[:], iota=iota[:], part=part[:], eps=eps[:],
                   map_rows=map_rows[:])
        col = 0
        for name, n in CONST_COLS.items():
            cst[name] = small[:, col:col + n]
            col += n
        dr["stored"] = nc.alloc_semaphore("stored")
        dr["n_stored"] = 0
        dr["kv_in"] = [nc.alloc_semaphore(f"kv_in{k}") for k in range(2)]

        with Stage(nc, "init") as st:
            landed = st.sem("landed")
            with st.block() as block:

                @block.sync
                def _(sp):
                    sp.dma_start(h[:], dr["xT"]).then_inc(landed, 16)
                    for dst, src in ((small, "small"), (ident, "ident"), (ones2, "ones2"), (map_rows, "map_rows"),
                                     (iota, "iota"), (part, "part")):
                        sp.dma_start(dst[:], dr[src]).then_inc(landed, 16)
                    sp.wait_ge(landed, 7 * 16)

                @block.vector
                def _(dve):
                    dve.memset(ones[:], 1.0)
                    dve.memset(eps[:], EPS)
                    dve.wait_ge(landed, 7 * 16)
                    dve.tensor_scalar(cst["subln"], cst["subln"], 1.0 - LAM_INIT, None, ALU.mult)

        def gain(kind, layer):
            n = (kind * 2 + layer) * DC
            return cst["gains"][:, n:n + DC]

        def norm(kind, layer):
            rmsnorm(nc, f"n{kind}{layer}", h, xn, gain(kind, layer), cst["ones"], cst["eps"])

        def dump(name, buf):
            if dumps is not None and name in dumps:
                with Stage(nc, "d" + name) as st:
                    with st.block() as block:

                        @block.sync
                        def _(sp):
                            store(sp, dr, dumps[name], buf[:])
                            sp.wait_ge(dr["stored"], 16 * dr["n_stored"])

        norm(0, 0)
        if upto >= 1:
            with ExitStack() as c0:
                cat = c0.enter_context(nc.sbuf_tensor("cat", [P, DC, T], F32))
                with ExitStack() as c1:
                    u = c1.enter_context(nc.sbuf_tensor("u", [P, 4, T], F32))
                    seg = c1.enter_context(nc.sbuf_tensor("seg_mask", [P, L5], F32))
                    cst["seg_mask"] = seg[:]
                    with Stage(nc, "seg") as st:
                        with st.block() as block:

                            @block.vector
                            def _(dve):
                                dve.memset(seg[:], 1.0)
                                dve.drain()
                                dve.memset(seg[:, TP:L5].rearrange("p (b e) -> p b e", e=SEG)[:, :, 0:1], 0.0)

                    linear(nc, "inu", dr["w_in_u"], DC, 4, xn, "act", to_buffer(u))
                    s5(nc, dr, cst, u, cat)
                with ExitStack() as c1:
                    q, f, g = [c1.enter_context(nc.sbuf_tensor(f"hg_{n}", [P, BH, T], F32)) for n in "qfg"]
                    v = c1.enter_context(nc.sbuf_tensor("hg_v", [CH, NCH + 1, BH * P], F32))
                    chunk_mask = c1.enter_context(nc.sbuf_tensor("chunk_mask", [P, BH * T], F32))
                    level_mask = c1.enter_context(nc.sbuf_tensor("level_mask", [CH, 7, CH], F32))
                    seq_mask = c1.enter_context(nc.sbuf_tensor("seq_mask", [CH, NB], F32))
                    cst.update(chunk_mask=chunk_mask[:], level_mask=level_mask[:], seq_mask=seq_mask[:])
                    with Stage(nc, "hgm") as st:
                        landed = st.sem("landed")
                        with st.block() as block:

                            @block.sync
                            def _(sp):
                                sp.dma_start(level_mask[:], dr["level_mask"]).then_inc(landed, 16)
                                sp.dma_start(seq_mask[:], dr["seq_mask"]).then_inc(landed, 16)
                                sp.wait_ge(landed, 32)

                            @block.vector
                            def _(dve):
                                dve.memset(chunk_mask[:], 1.0)
                                dve.drain()
                                m = chunk_mask[:].rearrange("p (h n) -> p h n", h=BH)
                                dve.memset(m[:, :, 0:TP].rearrange("p h (c t) -> p h c t", t=CH)[:, :, :, 0:1], 0.0)
                                dve.memset(m[:, :, TP:T].rearrange("p h (c t) -> p h c t", t=TS)[:, :, :, 0:1], 0.0)

                    for name, buf in (("q", q), ("f", f), ("g", g)):
                        linear(nc, f"in{name}", dr[f"w_in_{name}"], DC, BH, xn, "act", to_buffer(buf))
                    linear_by_token(nc, "inv", dr["w_in_i"], BH * P, xn, v, CH, NCH + 1)
                    if upto >= 2:
                        hgrn(nc, dr, cst, q, f, g, v, cat)
                if upto >= 2:
                    dump("cat", cat)
                if upto >= 3:
                    linear(nc, "outab", dr["w_out_ab"], DC, DC, cat, "dve", add_to(h))
        dump("h0", h)
        if upto >= 4:
            norm(1, 0)
            peer(nc, dr, cst, 0, xn, h)
            dump("h1", h)
        if upto >= 5:
            norm(2, 0)
            ple(nc, dr, cst, 0, xn, h)
            dump("h2", h)
        if upto >= 6:
            norm(0, 1)
            bias_lines(nc, dr, cst)
            with ExitStack() as c0:
                o = c0.enter_context(nc.sbuf_tensor("att_o", [P, H, T], F32))
                with ExitStack() as c1:
                    qk = c1.enter_context(nc.sbuf_tensor("qk", [P, 2 * H, T], F32))
                    v = c1.enter_context(nc.sbuf_tensor("att_v", [P, NT, D], F32))
                    linear(nc, "inqk", dr["w_in_qk"], DC, 2 * H, xn, "act", to_buffer(qk))
                    linear_by_token(nc, "incv", dr["w_in_v"], D, xn, v, P, NT)
                    headnorm(nc, "qn", qk[:, 0:H, :], H, cst["ones2"], CHD, cst["qk_norm"][:, 0:1], cst["eps"])
                    headnorm(nc, "kn", qk[:, H:2 * H, :], H, cst["ones2"], CHD, cst["qk_norm"][:, 1:2], cst["eps"])
                    with Stage(nc, "kvo") as st:
                        with st.block() as block:

                            @block.sync
                            def _(sp):
                                store(sp, dr, dr["out_k"], qk[:, H:2 * H, :])
                                store(sp, dr, dr["out_v"][:, 0:4, :], v[:, 0:4, :])
                                store(sp, dr, dr["out_v"][0:NB * TS, 4, :], v[0:NB * TS, 4, :])
                                sp.wait_ge(dr["stored"], 16 * dr["n_stored"])

                    attention(nc, dr, cst, qk, v, o)
                headnorm(nc, "sub", o, H, cst["ones"], P, cst["subln"], cst["eps"])
                dump("o", o)
                linear(nc, "outc", dr["w_out_c"], DC, DC, o, "dve", add_to(h))
            dump("h3", h)
        if upto >= 7:
            norm(1, 1)
            peer(nc, dr, cst, 1, xn, h)
            dump("h4", h)
            norm(2, 1)
            ple(nc, dr, cst, 1, xn, h)
        with nc.Block() as block:

            @block.sync
            def _(sp):
                store(sp, dr, dr["out_y"], h[:])
                sp.wait_ge(dr["stored"], 16 * dr["n_stored"])



def level_masks():
    m = np.zeros((CH, 7, CH), np.float32)
    s, t = np.meshgrid(np.arange(CH), np.arange(CH), indexing="ij")
    m[:, 0] = s == t
    for n, w in enumerate((32, 16, 8, 4, 2, 1)):
        m[:, n + 1] = (s // (2 * w) == t // (2 * w)) & (s % (2 * w) < w) & (t % (2 * w) >= w)
    return m


def bucket_table():
    hot = np.zeros((33, BW), np.float32)
    for x in range(BW):
        n = 511 - x
        if n < 0:
            hot[32, x] = NEG
            n = 0
        if n < 16:
            b = n
        else:
            b = min(31, 16 + int(math.log(n / 16) / math.log(128 / 16) * 16 + 1e-9))
        hot[b, x] = 1.0
    return hot


def columns(a):
    return np.ascontiguousarray(a.reshape(-1, P).T)


def packed(w):
    i, o = w.shape
    return np.ascontiguousarray(w.reshape(i // P, P, o // P, P).transpose(2, 1, 0, 3)).reshape(o // P, P, i)


def by_rows(w):
    return np.ascontiguousarray(w.reshape(-1, P, w.shape[1]).transpose(1, 0, 2))


def lay_out(z):
    z = {k: np.asarray(v) for k, v in z.items()}
    d = {}
    x = np.concatenate([z["x_prompt"].reshape(TP, D), z["x_sample"].reshape(NB * TS, D)])
    d["xT"] = np.ascontiguousarray(x.T.reshape(DC, P, T).transpose(1, 0, 2))
    p = np.concatenate([z["p_prompt"].reshape(2, TP, -1), z["p_sample"].reshape(2, NB * TS, -1)], axis=1)
    d["pT"] = np.ascontiguousarray(p.transpose(0, 2, 1).reshape(2, 2, P, T).transpose(0, 2, 1, 3))
    d["small"] = np.concatenate([
        columns(z["norm_mix"]), columns(z["norm_ffn"]), columns(z["norm_ple"]),
        columns(z["s5_d"]), columns(z["s5_glu_b"]), columns(z["hgrn_norm"]),
        columns(z["c_q_norm"]), columns(z["c_k_norm"]), columns(z["c_subln"])], axis=1)
    w = z["w_in_ab"][0]
    names = ["u", "q", "f", "i", "g"]
    for n, name in enumerate(names):
        part = w[:, n * 512:(n + 1) * 512]
        d[f"w_in_{name}"] = by_rows(part) if name == "i" else packed(part)
    d["w_out_ab"] = packed(z["w_out_ab"][0])
    d["w_glu"] = packed(z["s5_glu_w"][0])
    d["w_in_qk"] = packed(z["w_in_c"][0][:, :2 * D])
    d["w_in_v"] = by_rows(z["w_in_c"][0][:, 2 * D:])
    d["w_out_c"] = packed(z["w_out_c"][0])
    d["w_peer_q"] = np.stack([packed(z["peer_wq"][i]) for i in range(2)])
    d["w_ple_g"] = np.stack([packed(z["ple_gate"][i]) for i in range(2)])
    d["w_ple_p"] = np.stack([packed(z["ple_proj"][i]) for i in range(2)])
    d["peer_keys"] = np.ascontiguousarray(z["peer_keys"].reshape(2, 16, P, P).transpose(0, 3, 1, 2))
    u = z["peer_u"].reshape(2, P, NJB, JB, DC, P)
    d["peer_ut"] = np.ascontiguousarray(u.transpose(0, 2, 5, 4, 3, 1)).reshape(2, NJB, P, DC * JB * P)
    v = z["peer_v"].reshape(2, P, NJB, JB * D)
    d["peer_v"] = np.ascontiguousarray(v.transpose(0, 2, 1, 3))
    ldt = np.repeat(z["s5_log_dt"].reshape(16, 2), 64, axis=1)
    d["s5_par"] = np.ascontiguousarray(np.stack(
        [z["s5_a_re"].reshape(16, P), z["s5_a_im"].reshape(16, P), ldt]).transpose(2, 0, 1))
    b = np.zeros((P, 2, 16, P), np.float32)
    c = np.zeros((P, 2, 16, P), np.float32)
    for r, (bn, cn) in enumerate((("s5_b_re", "s5_c_re"), ("s5_b_im", "s5_c_im"))):
        for g in range(32):
            rows, cols = slice(64 * (g % 2), 64 * (g % 2) + 64), slice(16 * (g % 8), 16 * (g % 8) + 16)
            b[rows, r, g // 2, cols] = z[bn][0, g]
            c[rows, r, g // 2, cols] = z[cn][0, g].T
    d["s5_b"], d["s5_c"] = b, c
    h0 = np.stack([z["state_s5_re"][0], z["state_s5_im"][0]])
    d["s5_h0"] = np.ascontiguousarray(h0.reshape(2, NB, 16, P).transpose(3, 0, 2, 1))
    d["hgrn_lb"] = np.ascontiguousarray(z["hgrn_lower_bounds"].reshape(2, BH, P).transpose(2, 1, 0))
    d["hgrn_s0"] = np.ascontiguousarray(z["state_hgrn"][0].transpose(2, 0, 1, 3))
    lam = np.stack([z["c_lam_q1"][0], z["c_lam_q2"][0], z["c_lam_k1"][0], z["c_lam_k2"][0]])
    d["c_lam"] = np.ascontiguousarray(np.broadcast_to(lam, (P, 4, CHD)))
    d["rel_bias"] = np.concatenate([z["rel_bias"], np.ones((1, H), np.float32)])
    d["pages"] = np.ascontiguousarray(np.broadcast_to(z["page_table"].reshape(1, -1), (P, 16))).astype(np.int32)
    d["cache_k"] = z["cache_k"][0].reshape(-1, D)
    d["cache_v"] = z["cache_v"][0].reshape(-1, D)
    d["ident"] = np.eye(P, dtype=np.float32)
    d["ones2"] = np.kron(np.eye(2), np.ones((64, 64))).astype(np.float32)
    d["iota"] = np.broadcast_to(np.arange(P, dtype=np.float32), (P, P)).copy()
    d["part"] = np.arange(P, dtype=np.float32)[:, None].copy()
    second = (np.arange(P) // TS) % 2
    d["map_rows"] = np.stack([1 - second, second], axis=1).astype(np.float32)
    d["level_mask"] = level_masks()
    d["seq_mask"] = (np.arange(CH)[:, None] // TS == np.arange(NB)[None]).astype(np.float32)
    d["bucket_hot"] = bucket_table()
    return d


OUTPUTS = {
    "out_y": (P, DC, T), "out_s5": (P, 2, 16, 1 + NB), "out_hgrn_p": (P, BH, P), "out_hgrn_s": (P, NB, BH, P),
    "out_k": (P, H, T), "out_v": (P, NT, D),
}


def declare(nc, arrays):
    dr = {}
    for name, a in arrays.items():
        dr[name] = nc.dram_tensor(f"{name}_dram", a.shape, mybir.dt.from_np(a.dtype), kind="ExternalInput").ap()
    for name, shape in OUTPUTS.items():
        dr[name] = nc.dram_tensor(name, shape, F32, kind="ExternalOutput").ap()
    dr["gates"] = nc.dram_tensor("gates", (NTB, P, P * TB), F32, kind="Internal").ap()
    dr["activities"] = nc.dram_tensor("activities", (NJB, P, JB * T), F32, kind="Internal").ap()
    rows = nc.dram_tensor("bias_rows", (H, P, BW), F32, kind="Internal")
    dr["bias_rows"] = rows.ap()
    dr["bias_skew"] = bass.AP(rows, P - 1, [[P * BW, H], [BW - 1, P], [1, TP]])
    dr["bias_past"] = [bass.AP(rows, n * P * BW + PAST - 1, [[BW - 1, TS], [1, PAST + TS]]) for n in range(H)]
    return dr


def gather_outputs(r):
    y = r["out_y"].transpose(2, 1, 0).reshape(T, D)
    s5e = r["out_s5"].transpose(1, 3, 2, 0).reshape(2, 1 + NB, 32, 64)
    k = r["out_k"].transpose(2, 1, 0)
    v = r["out_v"].transpose(1, 0, 2).reshape(TPAD, H, P)
    hs = r["out_hgrn_s"].transpose(1, 2, 0, 3)
    c = np.ascontiguousarray
    return (c(y[:TP]).reshape(1, TP, D), c(y[TP:]).reshape(NB, TS, D),
            c(s5e[0, :1])[None], c(s5e[1, :1])[None], c(r["out_hgrn_p"].transpose(1, 0, 2))[None, None],
            c(k[:TP])[None, None], c(v[:TP])[None, None],
            c(s5e[0, 1:])[None], c(s5e[1, 1:])[None], c(hs)[None],
            c(k[TP:]).reshape(1, NB, TS, H, P), c(v[TP:T]).reshape(1, NB, TS, H, P))


def kernel(**inputs):
    import concourse.bacc as _bacc
    from concourse.bass_utils import run_bass_kernel_spmd as _run

    arrays = lay_out(inputs)
    nc = _bacc.Bacc("TRN2", target_bir_lowering=False, num_devices=1)
    program(nc, declare(nc, arrays))
    r = _run(nc, [{f"{name}_dram": a for name, a in arrays.items()}], core_ids=[0])
    return gather_outputs(r.results[0])
```

```python
import math
from contextlib import ExitStack

import concourse.bass as bass
import concourse.mybir as mybir
import numpy as np

P = 128
D = 1024
DC = D // P
TP = 512
NB, TS = 8, 8
T = TP + NB * TS
HALF = T // 2
TPAD = 640
NT = TPAD // P
EPS = 1e-6
NEG = -1e30

F32 = mybir.dt.float32
F32R = mybir.dt.float32r
U32 = mybir.dt.uint32
I32 = mybir.dt.int32
ALU = mybir.AluOpType
ACT = mybir.ActivationFunctionType
AX = mybir.AxisListType.X

S5_TILES = 16
SEG = TS + 1
L5 = TP + NB * SEG
BH = 4
CH = 64
NCH = TP // CH
CHD = 64
H = 8
PAST = 256
PAGE = 128
LAM_INIT = 0.8 - 0.6 * math.exp(-0.3 * 1)
BW = 640
PH = 8
PK = 16
TB = 32
NTB = T // TB
JB = 4
NJB = P // JB
UK = 2
SEL_UNITS = 3
N_SEL = (SEL_UNITS * NT - 1) * UK
N_STORED = (N_SEL + NTB * UK) // JB
BIG_ROUND = 1.5 * 2.0 ** 23
HIGH, REST = 0, 1
PRODUCTS = ((HIGH, HIGH), (HIGH, REST), (REST, HIGH))


class Stage:

    def __init__(self, nc, name):
        self.nc, self.name, self.sems = nc, name, []
        self.ctx = ExitStack()

    def __enter__(self):
        self.ctx.__enter__()
        return self

    def __exit__(self, *exc):
        self.ctx.__exit__(*exc)
        if exc[0] is None and self.sems:
            self.nc.clear_and_free_semaphores(self.sems)
            self.nc.all_engine_barrier()

    def sem(self, name):
        self.sems.append(self.nc.alloc_semaphore(f"{self.name}_{name}"))
        return self.sems[-1]

    def sb(self, name, shape, dt=F32):
        return self.ctx.enter_context(self.nc.sbuf_tensor(f"{self.name}_{name}", shape, dt))

    def ps(self, name, shape, dt=F32):
        return self.ctx.enter_context(self.nc.psum_tensor(f"{self.name}_{name}", shape, dt))

    def block(self):
        return self.nc.Block()


def store(eng, dr, dst, src):
    dr["n_stored"] += 1
    return eng.dma_start(dst, src).then_inc(dr["stored"], 16)


def wait_apart(eng, sem, value, column):
    eng.wait_ge(sem, value)
    eng.tensor_tensor(column, column, column, ALU.mult)


def halves(ap, n=T):
    return ap.rearrange("p (a n) -> p a n", a=2)


def at(ap, i):
    return ap[:, bass.ds(i, 1)].rearrange("p a n -> p (a n)")


def grouped(eng, count, size, body):
    for k in range(size):
        body(0, k, True)
    if count > size:
        with eng.Fori(1, count // size) as i:
            for k in range(size):
                body(i, k, False)


def paired(eng, count, body):
    grouped(eng, count, 2, body)


def looped(eng, count, body):
    body(0, True)
    with eng.Fori(1, count) as t:
        body(t, False)


def take_high(dve, high, x):
    return dve.tensor_copy(high.bitcast(F32R), x)


def take_high_act(act, high, x):
    return act.activation(high.bitcast(F32R), x, ACT.Copy)


def leave_rest(eng, rest, x, high):
    return eng.tensor_tensor(rest.bitcast(F32R), x, high, ALU.subtract)


def split_on(dve, parts, x, n):
    for c in range(n):
        take_high(dve, parts[:, HIGH, c, :], x[:, c, :])
        dve.drain()
        yield leave_rest(dve, parts[:, REST, c, :], x[:, c, :], parts[:, HIGH, c, :])


def multiply_split(pe, out, weights, moving, n, start, stop):
    for m, (wp, xp) in enumerate(PRODUCTS):
        for a in range(n):
            last = pe.matmul(out(a), weights(wp).bitcast(F32R), moving(xp, a).bitcast(F32R),
                             start=start and m == 0, stop=stop and m == len(PRODUCTS) - 1)
    return last


class Linear:

    K = 4

    def __init__(self, nc, name, w_dram, n_in, n_out):
        self.w_dram, self.n_in, self.n_out = w_dram, n_in, n_out
        self.st = Stage(nc, name)
        self.started = False

    def __enter__(self):
        st, K = self.st.__enter__(), self.K
        self.w = st.sb("w", [P, K, self.n_in * P])
        self.w_high = st.sb("w_high", [P, K, self.n_in * P])
        self.w_rest = st.sb("w_rest", [P, K, self.n_in * P])
        self.w_landed = [st.sem(f"w_landed{k}") for k in range(K)]
        self.multiplied = st.sem("multiplied")
        return self

    def __exit__(self, *exc):
        self.st.__exit__(*exc)

    def _load(self, sp, n, k, first):
        src = self.w_dram[bass.ds(n, 1)]
        if not first:
            sp.wait_ge(self.multiplied, n - self.K + 1)
        sp.dma_start(self.w[:, k, :], src.rearrange("a p n -> p (a n)")).then_inc(self.w_landed[k], 16)

    def start(self, sp):
        self.started = True
        for k in range(self.K):
            self._load(sp, k, k, True)

    def run(self, rhs, evac_on, evac, is_split=True, x_landed=None):
        st, K, n_in, n_out = self.st, self.K, self.n_in, self.n_out
        w, w_high, w_rest = self.w, self.w_high, self.w_rest
        w_landed, multiplied = self.w_landed, self.multiplied
        x = rhs if is_split else st.sb("x", [P, 2, n_in, T])
        acc = st.ps("acc", [P, 2, 2, 512])
        high_ready = st.sem("high_ready")
        rest_ready = st.sem("rest_ready")
        x_ready = st.sem("x_ready")
        evacuated = st.sem("evacuated")
        with st.block() as block:

            @block.sync
            def _(sp):
                if not self.started:
                    self.start(sp)
                if n_out > K:
                    with sp.Fori(1, n_out // K) as i:
                        for k in range(K):
                            self._load(sp, sp.snap(i * K + k), k, False)

            def evacuate(eng, n, k):
                eng.wait_ge(multiplied, n + 1)
                evac(eng, n, acc[:, k % 2, :, 0:HALF]).then_inc(evacuated, 1)

            @block.vector
            def _(dve):
                def one(i, k, first):
                    dve.wait_ge(w_landed[k], i * 16 + 16)
                    take_high(dve, w_high[:, k, :], w[:, k, :]).then_inc(high_ready, 1)
                    if first and k == 0 and not is_split:
                        if x_landed:
                            dve.wait_ge(x_landed, 16)
                        for last in split_on(dve, x, rhs, n_in):
                            last.then_inc(x_ready, 1)
                    if evac_on == "dve" and not (first and k < 2):
                        evacuate(dve, i * K + k - 2, k)

                grouped(dve, n_out, K, one)
                if evac_on == "dve":
                    for n in (n_out - 2, n_out - 1):
                        evacuate(dve, n, n % 2)

            @block.gpsimd
            def _(pool):
                def one(i, k, first):
                    pool.wait_ge(high_ready, i * K + k + 1)
                    leave_rest(pool, w_rest[:, k, :], w[:, k, :], w_high[:, k, :]).then_inc(rest_ready, 1)

                grouped(pool, n_out, K, one)

            @block.tensor
            def _(pe):
                def multiply(i, k, first):
                    pe.wait_ge(rest_ready, i * K + k + 1)
                    if not (first and k < 2):
                        pe.wait_ge(evacuated, i * K + k - 1)
                    for c in range(n_in):
                        if first and k == 0 and not is_split:
                            pe.wait_ge(x_ready, c + 1)
                        last = multiply_split(
                            pe, lambda a: acc[:, k % 2, a, 0:HALF],
                            lambda part: (w_high, w_rest)[part][:, k, c * P:(c + 1) * P],
                            lambda part, a: x[:, part, c, a * HALF:(a + 1) * HALF], 2, c == 0, c == n_in - 1)
                    last.then_inc(multiplied, 1)

                grouped(pe, n_out, K, multiply)

            if evac_on == "act":

                @block.scalar
                def _(act):
                    grouped(act, n_out, K, lambda i, k, first: evacuate(act, i * K + k, k))


def linear(nc, name, w_dram, n_in, n_out, rhs, evac_on, evac, is_split=True):
    with Linear(nc, name, w_dram, n_in, n_out) as lin:
        lin.run(rhs, evac_on, evac, is_split)


def to_buffer(buf, first=0, func=ACT.Copy):
    def evac(eng, o, res):
        return eng.activation(halves(at(buf, o + first)), res, func)
    return evac


def add_to(buf):
    def evac(eng, o, res):
        dst = halves(at(buf, o))
        return eng.tensor_tensor(dst, dst, res, ALU.add)
    return evac


def rmsnorm(nc, name, x, out, whole, gain, ones, eps, meanwhile):
    with Stage(nc, name) as st:
        sq = st.sb("sq", [P, DC, T])
        if whole is None:
            whole = sq
        rstd = st.sb("rstd", [P, T])
        tot = st.ps("tot", [P, 2, 512])
        squared = st.sem("squared")
        summed = st.sem("summed")
        rooted = st.sem("rooted")
        high_ready = st.sem("high_ready")
        with st.block() as block:

            @block.sync
            def _(sp):
                if meanwhile:
                    meanwhile(sp)

            @block.scalar
            def _(act):
                for c in range(DC):
                    act.activation(sq[:, c, :], x[:, c, :], ACT.Square).then_inc(squared, 1)
                act.wait_ge(summed, 1)
                act.activation(halves(rstd[:]), tot[:, :, 0:HALF], ACT.Sqrt, bias=eps, scale=1.0 / D)\
                   .then_inc(rooted, 1)

            @block.tensor
            def _(pe):
                for c in range(DC):
                    pe.wait_ge(squared, c + 1)
                    for a in range(2):
                        last = pe.matmul(tot[:, a, 0:HALF], ones, sq[:, c, a * HALF:(a + 1) * HALF],
                                         start=(c == 0), stop=(c == DC - 1))
                last.then_inc(summed, 1)

            @block.vector
            def _(dve):
                dve.wait_ge(rooted, 1)
                dve.reciprocal(rstd[:], rstd[:])
                dve.drain()
                for c in range(DC):
                    dve.scalar_tensor_tensor(out=whole[:, c, :], in0=x[:, c, :], scalar=gain[:, c:c + 1],
                                             in1=rstd[:], op0=ALU.mult, op1=ALU.mult)
                    dve.drain()
                    take_high(dve, out[:, HIGH, c, :], whole[:, c, :]).then_inc(high_ready, 1)

            @block.gpsimd
            def _(pool):
                for c in range(DC):
                    pool.wait_ge(high_ready, c + 1)
                    leave_rest(pool, out[:, REST, c, :], whole[:, c, :], out[:, HIGH, c, :])


def headnorm(nc, name, buf, n, per, ident, gain, eps, meanwhile=None):
    rows, size = n * per, P // per
    with Stage(nc, name) as st:
        sq = st.sb("sq", [P, 2, T])
        collect = st.sb("collect", [P, 2 * rows])
        spread = st.sb("spread", [rows, rows * size])
        rstd = st.sb("rstd", [rows, T])
        rstd_parts = st.sb("rstd_parts", [rows, 2, T])
        tot = st.ps("tot", [rows, 2, 512])
        wide = st.ps("wide", [P, 2, 2, 512])
        masks_ready = st.sem("masks_ready")
        squared = st.sem("squared")
        summed = st.sem("summed")
        rooted = st.sem("rooted")
        inverted = st.sem("inverted")
        widened = st.sem("widened")
        scaled = st.sem("scaled")
        with st.block() as block:

            @block.sync
            def _(sp):
                if meanwhile:
                    meanwhile(sp)

            @block.scalar
            def _(act):
                for c in range(n):
                    if c >= 2:
                        act.wait_ge(summed, c - 1)
                    act.activation(sq[:, c % 2, :], buf[:, c, :], ACT.Square).then_inc(squared, 1)
                act.wait_ge(summed, n)
                act.activation(halves(rstd[:]), tot[:, :, 0:HALF], ACT.Sqrt, bias=eps[0:rows, :], scale=1.0 / size)\
                   .then_inc(rooted, 1)

            @block.tensor
            def _(pe):
                pe.wait_ge(masks_ready, 1)
                for c in range(n):
                    pe.wait_ge(squared, c + 1)
                    for a in range(2):
                        last = pe.matmul(tot[:, a, 0:HALF], collect[:, rows - c * per:2 * rows - c * per],
                                         sq[:, c % 2, a * HALF:(a + 1) * HALF], start=(c == 0), stop=(c == n - 1))
                    last.then_inc(summed, 1)
                pe.wait_ge(inverted, 1)
                for c in range(n):
                    if c >= 2:
                        pe.wait_ge(scaled, c - 1)
                    for part in (HIGH, REST):
                        for a in range(2):
                            last = pe.matmul(wide[:, c % 2, a, 0:HALF], spread[:, c * P:(c + 1) * P].bitcast(F32R),
                                             rstd_parts[:, part, a * HALF:(a + 1) * HALF].bitcast(F32R),
                                             start=(part == HIGH), stop=(part == REST))
                    last.then_inc(widened, 1)

            @block.vector
            def _(dve):
                dve.memset(collect[:], 0.0)
                dve.drain()
                for k in range(per):
                    dve.memset(collect[k * size:(k + 1) * size, rows + k:rows + k + 1], 1.0)
                dve.tensor_copy(spread[:].bitcast(F32R).rearrange("r (s m) -> r s m", m=size),
                                ident[0:rows, 0:rows].unsqueeze(2).to_broadcast([rows, rows, size]))
                dve.drain().then_inc(masks_ready, 1)
                dve.wait_ge(rooted, 1)
                dve.reciprocal(rstd[:], rstd[:])
                dve.drain()
                take_high(dve, rstd_parts[:, HIGH, :], rstd[:])
                dve.drain()
                leave_rest(dve, rstd_parts[:, REST, :], rstd[:], rstd_parts[:, HIGH, :]).then_inc(inverted, 1)
                for c in range(n):
                    dve.wait_ge(widened, c + 1)
                    chunk = halves(buf[:, c, :])
                    dve.scalar_tensor_tensor(out=chunk, in0=chunk, scalar=gain(c), in1=wide[:, c % 2, :, 0:HALF],
                                             op0=ALU.mult, op1=ALU.mult).then_inc(scaled, 1)


def linear_by_token(nc, name, w_dram, n_cols, x, out, tile, n_tiles):
    n_half = n_cols // 512
    with Stage(nc, name) as st:
        w = st.sb("w", [P, DC, n_cols])
        w_split = st.sb("w_split", [P, 2, DC, n_cols])
        acc = st.ps("acc", [P, 2, n_half, 512])
        w_landed = [st.sem(f"w_landed{c}") for c in range(DC)]
        w_ready = st.sem("w_ready")
        multiplied = st.sem("multiplied")
        evacuated = st.sem("evacuated")
        rows = [min(tile, T - t * tile) for t in range(n_tiles)]
        with st.block() as block:

            @block.sync
            def _(sp):
                for c in range(DC):
                    sp.dma_start(w[:, c, :], w_dram[:, c, :]).then_inc(w_landed[c], 16)

            @block.vector
            def _(dve):
                for c in range(DC):
                    dve.wait_ge(w_landed[c], 16)
                    for last in split_on(dve, w_split[:, :, c:c + 1, :], w[:, c:c + 1, :], 1):
                        last.then_inc(w_ready, 1)

            @block.tensor
            def _(pe):
                for t, m in enumerate(rows):
                    if t >= 2:
                        pe.wait_ge(evacuated, t - 1)
                    for c in range(DC):
                        if t == 0:
                            pe.wait_ge(w_ready, c + 1)
                        last = multiply_split(
                            pe, lambda a: acc[0:m, t % 2, a, :],
                            lambda part: x[:, part, c, t * tile:t * tile + m],
                            lambda part, a: w_split[:, part, c, a * 512:(a + 1) * 512],
                            n_half, c == 0, c == DC - 1)
                    last.then_inc(multiplied, 1)

            @block.scalar
            def _(act):
                for t, m in enumerate(rows):
                    act.wait_ge(multiplied, t + 1)
                    act.activation(out[0:m, t, :].rearrange("p (a n) -> p a n", a=n_half),
                                   acc[0:m, t % 2, :, :], ACT.Copy).then_inc(evacuated, 1)



def s5(nc, dr, cst, u, cat):
    with ExitStack() as outer:
        def sb(name, shape):
            return outer.enter_context(nc.sbuf_tensor(f"s5_{name}", shape, F32))

        ct = sb("ct", [P, 2, S5_TILES, P])
        bt = sb("bt", [P, 2, S5_TILES, P])
        mag = sb("mag", [P, S5_TILES])
        h0 = sb("h0", [P, 2, S5_TILES, NB])
        ends = sb("ends", [P, 2, S5_TILES, 1 + NB])
        rot1 = sb("rot1", [P, 2, S5_TILES])
        with Stage(nc, "s5b") as st:
            braw = st.sb("braw", [P, 2, S5_TILES, P])
            bb = st.sb("bb", [P, 2, 4, P])
            par = st.sb("par", [P, 3, S5_TILES])
            dt = st.sb("dt", [P, S5_TILES])
            ang = st.sb("ang", [P, 2, S5_TILES])
            rnd = st.sb("rnd", [P, 2, S5_TILES])
            lbre = st.sb("lbre", [P, 2, S5_TILES])
            den = st.sb("den", [P, S5_TILES])
            tmp = st.sb("tmp", [P, S5_TILES])
            coef = st.sb("coef", [P, 2, S5_TILES])
            bp = st.sb("bp", [P, 4, P])
            tr = st.ps("tr", [P, 2, 2, 4, P])
            landed = st.sem("landed")
            b_landed = st.sem("b_landed")
            c_landed = st.sem("c_landed")
            dt_ready = st.sem("dt_ready")
            arg_ready = st.sem("arg_ready")
            trig_ready = st.sem("trig_ready")
            bb_ready = st.sem("bb_ready")
            turned = st.sem("turned")
            copied = st.sem("copied")
            with st.block() as block:

                @block.sync
                def _(sp):
                    sp.dma_start(par[:], dr["s5_par"]).then_inc(landed, 16)
                    sp.dma_start(braw[:], dr["s5_b"]).then_inc(b_landed, 16)
                    sp.dma_start(ct[:], dr["s5_c"]).then_inc(c_landed, 16)
                    sp.dma_start(h0[:], dr["s5_h0"]).then_inc(landed, 16)
                    sp.wait_ge(landed, 32)
                @block.scalar
                def _(act):
                    act.wait_ge(landed, 32)
                    act.activation(dt[:], par[:, 2, :], ACT.Exp).then_inc(dt_ready, 1)
                    act.wait_ge(arg_ready, 1)
                    act.activation(mag[:], mag[:], ACT.Exp)
                    act.activation(rot1[:], ang[:], ACT.Sin).then_inc(trig_ready, 1)
                    for q in range(4):
                        for r in range(2):
                            act.wait_ge(turned, 2 * q + r + 1)
                            act.activation(bt[:, r, 4 * q:4 * q + 4, :], tr[:, q % 2, r, :, :], ACT.Copy)\
                               .then_inc(copied, 1)

                @block.vector
                def _(dve):
                    are, aim = par[:, 0, :], par[:, 1, :]
                    dve.wait_ge(dt_ready, 1)
                    dve.tensor_tensor(mag[:], are, dt[:], ALU.mult)
                    dve.tensor_tensor(ang[:, 1, :], aim, dt[:], ALU.mult)
                    dve.drain()
                    dve.tensor_scalar(ang[:, 0, :], ang[:, 1, :], math.pi / 2, None, ALU.add)
                    dve.drain()
                    dve.tensor_scalar(rnd[:], ang[:], 1.0 / (2 * math.pi), BIG_ROUND, ALU.mult, ALU.add)
                    dve.drain()
                    dve.tensor_scalar(rnd[:], rnd[:], BIG_ROUND, None, ALU.subtract)
                    dve.drain()
                    two_pi_hi = 6.28125
                    dve.scalar_tensor_tensor(out=ang[:], in0=rnd[:], scalar=-two_pi_hi, in1=ang[:],
                                             op0=ALU.mult, op1=ALU.add)
                    dve.drain()
                    dve.scalar_tensor_tensor(out=ang[:], in0=rnd[:], scalar=-(2 * math.pi - two_pi_hi),
                                             in1=ang[:], op0=ALU.mult, op1=ALU.add)
                    dve.drain()
                    dve.tensor_scalar(ang[:], ang[:], 3.1415925, -3.1415925, ALU.min, ALU.max)
                    dve.tensor_tensor(den[:], are, are, ALU.mult)
                    dve.tensor_tensor(tmp[:], aim, aim, ALU.mult)
                    dve.drain()
                    dve.tensor_tensor(den[:], den[:], tmp[:], ALU.add).then_inc(arg_ready, 1)
                    dve.drain()
                    dve.reciprocal(den[:], den[:])
                    dve.wait_ge(trig_ready, 1)
                    for r in range(2):
                        dve.tensor_tensor(lbre[:, r, :], rot1[:, r, :], mag[:], ALU.mult)
                    dve.drain()
                    dve.tensor_scalar(lbre[:, 0, :], lbre[:, 0, :], 1.0, None, ALU.subtract)
                    dve.drain()
                    dve.tensor_tensor(coef[:, 0, :], lbre[:, 0, :], are, ALU.mult)
                    dve.tensor_tensor(tmp[:], lbre[:, 1, :], aim, ALU.mult)
                    dve.tensor_tensor(coef[:, 1, :], lbre[:, 1, :], are, ALU.mult)
                    dve.tensor_tensor(dt[:], lbre[:, 0, :], aim, ALU.mult)
                    dve.drain()
                    dve.tensor_tensor(coef[:, 0, :], coef[:, 0, :], tmp[:], ALU.add)
                    dve.tensor_tensor(coef[:, 1, :], coef[:, 1, :], dt[:], ALU.subtract)
                    dve.drain()
                    for r in range(2):
                        dve.tensor_tensor(coef[:, r, :], coef[:, r, :], den[:], ALU.mult)
                    dve.wait_ge(b_landed, 16)
                    dve.wait_ge(c_landed, 16)
                    dve.drain()
                    dve.tensor_scalar(ct[:, 1, :, :], ct[:, 1, :, :], -1.0, None, ALU.mult)
                    for q in range(4):
                        s = slice(4 * q, 4 * q + 4)
                        cr = coef[:, 0, s].unsqueeze(2).to_broadcast([P, 4, P])
                        ci = coef[:, 1, s].unsqueeze(2).to_broadcast([P, 4, P])
                        if q:
                            dve.wait_ge(turned, 2 * q)
                        dve.tensor_tensor(bb[:, 0, :, :], braw[:, 0, s, :], cr, ALU.mult)
                        dve.tensor_tensor(bp[:], braw[:, 1, s, :], ci, ALU.mult)
                        dve.drain()
                        dve.tensor_tensor(bb[:, 0, :, :], bb[:, 0, :, :], bp[:], ALU.subtract)
                        dve.drain()
                        dve.tensor_tensor(bb[:, 1, :, :], braw[:, 1, s, :], cr, ALU.mult)
                        dve.tensor_tensor(bp[:], braw[:, 0, s, :], ci, ALU.mult)
                        dve.drain()
                        dve.tensor_tensor(bb[:, 1, :, :], bb[:, 1, :, :], bp[:], ALU.add).then_inc(bb_ready, 1)

                @block.tensor
                def _(pe):
                    for q in range(4):
                        pe.wait_ge(bb_ready, q + 1)
                        if q >= 2:
                            pe.wait_ge(copied, 2 * (q - 1))
                        for r in range(2):
                            for j in range(4):
                                last = pe.transpose(tr[:, q % 2, r, j, :], bb[:, r, j, :], cst["ident"])
                            last.then_inc(turned, 1)

        tables = ExitStack()
        rot = tables.enter_context(nc.sbuf_tensor("s5_rot", [P, 2, S5_TILES, L5], F32))
        with Stage(nc, "s5p") as st:
            t = [st.sb(f"t{k}", [P, S5_TILES * TP // 4]) for k in range(2)]
            wk = st.sb("wk", [P, 2, S5_TILES])
            wt = st.sb("wt", [P, 3, S5_TILES])
            with st.block() as block:

                @block.vector
                def _(dve):
                    dve.memset(rot[:, 0, :, 0:1], 1.0)
                    dve.memset(rot[:, 1, :, 0:1], 0.0)
                    dve.tensor_copy(wk[:], rot1[:])
                    dve.drain()
                    k = 1
                    while k < TP:
                        tiles = min(S5_TILES, S5_TILES * TP // 4 // k)
                        t0, t1 = (x[:, 0:tiles * k].rearrange("p (s n) -> p s n", n=k) for x in t)
                        for s0 in range(0, S5_TILES, tiles):
                            some = slice(s0, s0 + tiles)
                            c, s = rot[:, 0, some, 0:k], rot[:, 1, some, 0:k]
                            nc_, ns = rot[:, 0, some, k:2 * k], rot[:, 1, some, k:2 * k]
                            wr = wk[:, 0, some].unsqueeze(2).to_broadcast([P, tiles, k])
                            wi = wk[:, 1, some].unsqueeze(2).to_broadcast([P, tiles, k])
                            dve.tensor_tensor(t0, s, wi, ALU.mult)
                            dve.tensor_tensor(t1, s, wr, ALU.mult)
                            dve.tensor_tensor(nc_, c, wr, ALU.mult)
                            dve.tensor_tensor(ns, c, wi, ALU.mult)
                            dve.drain()
                            dve.tensor_tensor(nc_, nc_, t0, ALU.subtract)
                            dve.tensor_tensor(ns, ns, t1, ALU.add)
                            dve.drain()
                        dve.tensor_tensor(wt[:, 0, :], wk[:, 0, :], wk[:, 0, :], ALU.mult)
                        dve.tensor_tensor(wt[:, 1, :], wk[:, 1, :], wk[:, 1, :], ALU.mult)
                        dve.tensor_tensor(wt[:, 2, :], wk[:, 0, :], wk[:, 1, :], ALU.mult)
                        dve.drain()
                        dve.tensor_tensor(wk[:, 0, :], wt[:, 0, :], wt[:, 1, :], ALU.subtract)
                        dve.tensor_scalar(wk[:, 1, :], wt[:, 2, :], 2.0, None, ALU.mult)
                        dve.drain()
                        k *= 2
                    for r in range(2):
                        for b in range(NB):
                            dve.tensor_copy(rot[:, r, :, TP + SEG * b:TP + SEG * (b + 1)], rot[:, r, :, 0:SEG])

        y = cat[:, 0:4, :]
        with Stage(nc, "s5s") as st:
            x = st.sb("x", [P, 2, 2, L5])
            g = st.sb("g", [P, 2, L5])
            v = st.sb("v", [P, 2, L5])
            hh = st.sb("hh", [P, 2, 2, L5])
            g_im = st.sb("g_im", [P, 2, L5])
            im_ready = st.sem("im_ready")
            ends_kept = st.sem("ends_kept")
            free = cat[:, 4:8, :].rearrange("p c n -> p (c n)")
            decay = free[:, 0:2 * L5].rearrange("p (r n) -> p r n", r=2)
            t_im = free[:, 2 * L5:3 * L5]
            bu = st.ps("bu", [P, 2, 2, 512])
            cy = st.ps("cy", [P, 2, 2, 512])
            bu_ready = st.sem("bu_ready")
            x_ready = st.sem("x_ready")
            x_used = st.sem("x_used")
            h_ready = st.sem("h_ready")
            h_used = st.sem("h_used")
            y_taken = st.sem("y_taken")
            LH = L5 // 2
            with st.block() as block:

                @block.tensor
                def _(pe):
                    def read_in(s):
                        if s:
                            pe.wait_ge(x_ready, s)
                        for r in range(2):
                            for a in range(2):
                                last = pe.matmul(bu[:, r, a, 0:HALF], bt[:, r, s, :],
                                                 u[:, s // 4, a * HALF:(a + 1) * HALF], start=True, stop=True)
                        last.then_inc(bu_ready, 1)

                    def read_out(s):
                        pe.wait_ge(h_ready, s + 1)
                        if s % 4 == 0 and s >= 8:
                            pe.wait_ge(y_taken, s // 4 - 1)
                        for r in range(2):
                            for a in range(2):
                                last = pe.matmul(cy[:, (s // 4) % 2, a, 0:LH], ct[:, r, s, :],
                                                 hh[:, s % 2, r, a * LH:(a + 1) * LH],
                                                 start=(s % 4 == 0 and r == 0), stop=(s % 4 == 3 and r == 1))
                        last.then_inc(h_used, 1)

                    read_in(0)
                    for s in range(S5_TILES):
                        if s + 1 < S5_TILES:
                            read_in(s + 1)
                        read_out(s)

                @block.scalar
                def _(act):
                    def keep_ends(s):
                        act.wait_ge(h_ready, s + 1)
                        for r in range(2):
                            act.activation(ends[:, r, s, 0:1], hh[:, s % 2, r, TP - 1:TP], ACT.Copy)
                            last = act.activation(ends[:, r, s, 1:1 + NB].unsqueeze(2),
                                                  hh[:, s % 2, r, TP:L5].rearrange("p (b e) -> p b e", e=SEG)[:, :, TS:SEG],
                                                  ACT.Copy)
                        last.then_inc(ends_kept, 1)

                    for s in range(S5_TILES):
                        k = s % 2
                        if s >= 2:
                            act.wait_ge(x_used, s - 1)
                        act.activation(decay[:, k, :], cst["seg_mask"], ACT.Copy, scale=mag[:, s:s + 1])
                        for r in range(2):
                            act.activation(x[:, k, r, TP:L5].rearrange("p (b e) -> p b e", e=SEG)[:, :, 0:1],
                                           h0[:, r, s, :].unsqueeze(2), ACT.Copy)
                        act.wait_ge(bu_ready, s + 1)
                        for r in range(2):
                            act.activation(x[:, k, r, 0:HALF], bu[:, r, 0, 0:HALF], ACT.Copy)
                            act.activation(x[:, k, r, HALF:TP], bu[:, r, 1, 0:TP - HALF], ACT.Copy)
                            last = act.activation(
                                x[:, k, r, TP:L5].rearrange("p (b e) -> p b e", e=SEG)[:, :, 1:SEG],
                                bu[:, r, 1, TP - HALF:HALF].rearrange("p (b e) -> p b e", e=TS), ACT.Copy)
                        last.then_inc(x_ready, 1)
                        if s >= 2:
                            keep_ends(s - 2)
                    keep_ends(S5_TILES - 2)
                    keep_ends(S5_TILES - 1)

                @block.gpsimd
                def _(pool):
                    for s in range(S5_TILES):
                        k = s % 2
                        pool.wait_ge(x_ready, s + 1)
                        if s >= 2:
                            pool.wait_ge(x_used, s - 1)
                        pool.tensor_tensor(g_im[:, k, :], x[:, k, 1, :], rot[:, 0, s, :], ALU.mult)
                        pool.tensor_tensor(t_im, x[:, k, 0, :], rot[:, 1, s, :], ALU.mult)
                        pool.drain()
                        pool.tensor_tensor(g_im[:, k, :], g_im[:, k, :], t_im, ALU.subtract).then_inc(im_ready, 1)
                        pool.drain()

                @block.vector
                def _(dve):
                    def take_y(q):
                        dve.wait_ge(h_used, 4 * q + 4)
                        res = cy[:, q % 2, :, :]
                        uq, yq, dq = u[:, q, :], y[:, q, :], cst["s5_d"][:, q:q + 1]
                        dve.scalar_tensor_tensor(out=yq[:, 0:LH], in0=uq[:, 0:LH], scalar=dq,
                                                 in1=res[:, 0, 0:LH], op0=ALU.mult, op1=ALU.add)
                        dve.scalar_tensor_tensor(out=yq[:, LH:TP], in0=uq[:, LH:TP], scalar=dq,
                                                 in1=res[:, 1, 0:TP - LH], op0=ALU.mult, op1=ALU.add)
                        dve.scalar_tensor_tensor(
                            out=yq[:, TP:T].rearrange("p (b e) -> p b e", e=TS),
                            in0=uq[:, TP:T].rearrange("p (b e) -> p b e", e=TS), scalar=dq,
                            in1=res[:, 1, TP - LH:LH].rearrange("p (b e) -> p b e", e=SEG)[:, :, 1:SEG],
                            op0=ALU.mult, op1=ALU.add).then_inc(y_taken, 1)

                    for s in range(S5_TILES):
                        k = s % 2
                        c, sn = rot[:, 0, s, :], rot[:, 1, s, :]
                        dve.wait_ge(x_ready, s + 1)
                        xr, xi = x[:, k, 0, :], x[:, k, 1, :]
                        gr, gi, vr, vi = g[:, 0, :], g[:, 1, :], v[:, 0, :], v[:, 1, :]
                        dve.tensor_tensor(gr, xr, c, ALU.mult)
                        dve.tensor_tensor(vr, xi, sn, ALU.mult)
                        dve.drain()
                        dve.tensor_tensor(gr, gr, vr, ALU.add)
                        dve.drain()
                        dve.tensor_tensor_scan(vr, decay[:, k, :], gr, 0.0, ALU.mult, ALU.add)
                        dve.wait_ge(im_ready, s + 1)
                        dve.tensor_tensor_scan(vi, decay[:, k, :], g_im[:, k, :], 0.0, ALU.mult, ALU.add)\
                           .then_inc(x_used, 1)
                        dve.drain()
                        if s >= 2:
                            dve.wait_ge(h_used, s - 1)
                            dve.wait_ge(ends_kept, s - 1)
                        hr, hi = hh[:, k, 0, :], hh[:, k, 1, :]
                        dve.tensor_tensor(hr, vr, c, ALU.mult)
                        dve.tensor_tensor(gr, vi, sn, ALU.mult)
                        dve.tensor_tensor(hi, vi, c, ALU.mult)
                        dve.tensor_tensor(gi, vr, sn, ALU.mult)
                        dve.drain()
                        dve.tensor_tensor(hr, hr, gr, ALU.subtract)
                        dve.tensor_tensor(hi, hi, gi, ALU.add).then_inc(h_ready, 1)
                        dve.drain()
                        if s % 4 == 3 and s > 3:
                            take_y(s // 4 - 1)
                    take_y(3)

        tables.close()
        with Stage(nc, "s5g") as st:
            yg = st.sb("yg", [P, 4, T])
            lin = st.ctx.enter_context(Linear(nc, "glu", dr["w_glu"], 4, 4))
            with st.block() as block:

                @block.scalar
                def _(act):
                    act.activation(yg[:], y, ACT.Gelu_apprx_tanh)

                @block.sync
                def _(sp):
                    lin.start(sp)
                    store(sp, dr, dr["out_s5"], ends[:])
                    sp.wait_ge(dr["stored"], 16 * dr["n_stored"])

            def gate(eng, o, res):
                return eng.activation(halves(at(y, o)), res, ACT.Sigmoid, bias=cst["s5_glu_b"][:, bass.ds(o, 1)])

            lin.run(yg, "act", gate, is_split=False)
            with st.block() as block:

                @block.vector
                def _(dve):
                    dve.tensor_tensor(y, yg[:], y, ALU.mult)



def hgrn(nc, dr, cst, q, f, g, v, cat):
    NC9 = NCH + 1
    with Stage(nc, "hg") as st:
        k = st.sb("k", [P, BH, T])
        b = st.sb("b", [P, BH, T])
        e = st.sb("e", [P, BH, T])
        x = st.sb("x", [P, BH, T])
        e_of = [e, f]
        x_of = [x, st.sb("x_odd", [P, BH, T])]
        A = st.sb("A", [CH, BH, NC9, CH])
        part = st.sb("part", [CH, 2, NC9, CH])
        lbs = st.sb("lbs", [P, BH, 2])
        lb = st.sb("lb", [P, BH])
        sumlb = st.sb("sumlb", [P, BH])
        omlb = st.sb("omlb", [P, BH])
        lb_in = st.sem("lb_in")
        lb_exp = st.sem("lb_exp")
        lb_max = st.sem("lb_max")
        sig = st.sem("sig")
        f_ready = st.sem("f_ready")
        logged = st.sem("logged")
        d_ready = st.sem("d_ready")
        e_ready = st.sem("e_ready")
        x_ready = st.sem("x_ready")
        scored = st.sem("scored")
        taken = st.sem("taken")
        sps = st.ps("sps", [CH, 2, 2, 512])
        flat = lambda t: t[:].rearrange("p h n -> p (h n)")
        LEVELS = [32, 16, 8, 4, 2, 1]

        def spans(buf, m):
            if m >= 8:
                return buf[:, :, 0:TP].rearrange("p h (a m) -> p h a m", m=2 * m)
            return flat(buf).rearrange("p (a m) -> p a m", m=2 * m)

        def part_of(ap, lo, hi):
            return ap[:, :, :, lo:hi] if len(ap.shape) == 4 else ap[:, :, lo:hi]

        with st.block() as block:

            @block.sync
            def _(sp):
                sp.dma_start(lbs[:], dr["hgrn_lb"]).then_inc(lb_in, 16)
                sp.wait_ge(lb_in, 16)

            @block.scalar
            def _(act):
                act.wait_ge(lb_max, 1)
                act.activation(lbs[:], lbs[:], ACT.Exp).then_inc(lb_exp, 1)
                act.activation(f[:], f[:], ACT.Sigmoid).then_inc(sig, 1)
                act.activation(g[:], g[:], ACT.Silu)
                act.wait_ge(f_ready, 1)
                act.activation(f[:], f[:], ACT.Ln).then_inc(logged, 1)
                for n, m in enumerate(LEVELS):
                    act.wait_ge(d_ready, n + 1)
                    second, former = (part_of(spans(e_of[n % 2], m), lo, lo + m) for lo in (m, 0))
                    act.activation(second, second, ACT.Exp)
                    act.activation(former, former, ACT.Exp, scale=-1.0).then_inc(e_ready, 1)

            @block.vector
            def _(dve):
                dve.wait_ge(lb_in, 16)
                dve.tensor_tensor(sumlb[:], lbs[:, :, 0], lbs[:, :, 1], ALU.max)
                dve.drain()
                dve.tensor_tensor(lbs[:], lbs[:], sumlb[:].unsqueeze(2).to_broadcast([P, BH, 2]), ALU.subtract)\
                   .then_inc(lb_max, 1)
                dve.wait_ge(lb_exp, 1)
                dve.tensor_tensor(sumlb[:], lbs[:, :, 0], lbs[:, :, 1], ALU.add)
                dve.drain()
                dve.reciprocal(sumlb[:], sumlb[:])
                dve.drain()
                dve.tensor_tensor(lb[:], lbs[:, :, 0], sumlb[:], ALU.mult)
                dve.drain()
                dve.tensor_scalar(omlb[:], lb[:], -1.0, 1.0, ALU.mult, ALU.add)
                dve.drain()
                dve.wait_ge(sig, 1)
                for h in range(BH):
                    dve.tensor_scalar(f[:, h, :], f[:, h, :], omlb[:, h:h + 1], lb[:, h:h + 1], ALU.mult, ALU.add)
                dve.drain()
                dve.tensor_scalar(k[:], f[:], -1.0, 1.0, ALU.mult, ALU.add).then_inc(f_ready, 1)
                dve.drain()
                dve.wait_ge(logged, 1)
                dve.tensor_tensor_scan(flat(b), cst["chunk_mask"], flat(f), 0.0, ALU.mult, ALU.add)
                dve.drain()

                def collect(n, h):
                    i = n * BH + h
                    dve.wait_ge(scored, i + 1)
                    mask = cst["level_mask"][:, n, :]
                    lots = [(0, NCH, 0)] + ([] if 0 < n <= 3 else [(NCH, 1, 1)])
                    for c0, cn, bank in lots:
                        src = sps[:, i % 2, bank, 0:cn * CH].rearrange("p (c t) -> p c t", t=CH)
                        mk = mask.unsqueeze(1).to_broadcast([CH, cn, CH])
                        dst = A[:, h, c0:c0 + cn, :]
                        if n == 0:
                            last = dve.tensor_tensor(dst, src, mk, ALU.mult)
                        else:
                            last = dve.tensor_tensor(part[:, i % 2, c0:c0 + cn, :], src, mk, ALU.mult)
                    last.then_inc(taken, 1)
                    dve.drain()
                    if n:
                        hi = lots[-1][0] + lots[-1][1]
                        dve.tensor_tensor(A[:, h, 0:hi, :], A[:, h, 0:hi, :], part[:, i % 2, 0:hi, :], ALU.add)

                def distances(n):
                    m = LEVELS[n]
                    ref = part_of(spans(b, m), m - 1, m)
                    dve.tensor_tensor(spans(e_of[n % 2], m), spans(b, m), ref.to_broadcast(spans(b, m).shape),
                                      ALU.subtract).then_inc(d_ready, 1)

                def decay(n):
                    m, ex, xx = LEVELS[n], e_of[n % 2], x_of[n % 2]
                    dve.wait_ge(e_ready, n + 1)
                    if n >= 2:
                        dve.wait_ge(scored, BH * n)
                    dve.tensor_tensor(part_of(spans(xx, m), m, 2 * m), part_of(spans(ex, m), m, 2 * m),
                                      part_of(spans(q, m), m, 2 * m), ALU.mult)
                    dve.tensor_tensor(part_of(spans(xx, m), 0, m), part_of(spans(ex, m), 0, m),
                                      part_of(spans(k, m), 0, m), ALU.mult).then_inc(x_ready, 1)

                distances(0)
                collect(0, 0)
                collect(0, 1)
                decay(0)
                collect(0, 2)
                collect(0, 3)
                for n in range(len(LEVELS)):
                    more = n + 1 < len(LEVELS)
                    if more:
                        distances(n + 1)
                    collect(n + 1, 0)
                    collect(n + 1, 1)
                    if more:
                        decay(n + 1)
                    collect(n + 1, 2)
                    collect(n + 1, 3)

            @block.tensor
            def _(pe):
                def score(n, h, left, right, chunks):
                    i = n * BH + h
                    if i >= 2:
                        pe.wait_ge(taken, i - 1)
                    for c in range(chunks):
                        s = slice(c * CH, (c + 1) * CH)
                        last = pe.matmul(sps[:, i % 2, c // NCH, (c % NCH) * CH:(c % NCH + 1) * CH],
                                         left[:, h, s], right[:, h, s], start=True, stop=True)
                    last.then_inc(scored, 1)

                pe.wait_ge(f_ready, 1)
                for h in range(BH):
                    score(0, h, k, q, NC9)
                for n, m in enumerate(LEVELS):
                    pe.wait_ge(x_ready, n + 1)
                    for h in range(BH):
                        score(n + 1, h, x_of[n % 2], x_of[n % 2], NCH if m >= 8 else NC9)

        S = st.sb("S", [P, BH, P])
        S0 = st.sb("S0", [P, NB, BH, P])
        vm = st.sb("vm", [CH, 2, NB, P])
        kt = st.sb("kt", [CH, 2, BH, P])
        o_in = st.ps("o_in", [P, 2, 512])
        kps = st.ps("kps", [P, 1, 512])
        eb_ready = st.sem("eb_ready")
        dk_ready = st.sem("dk_ready")
        dk_exp = st.sem("dk_exp")
        kd_ready = st.sem("kd_ready")
        turned = st.sem("turned")
        kt_ready = st.sem("kt_ready")
        s_done = st.sem("s_done")
        dS_ready = st.sem("dS_ready")
        o_ready = st.sem("o_ready")
        o_taken = st.sem("o_taken")
        s0_in = st.sem("s0_in")
        vm_ready = st.sem("vm_ready")
        d = x_of[1]
        dps = st.ps("dps", [P, 1, 512])
        vm_used = [st.sem("dS_taken0"), st.sem("dS_taken1")]
        with st.block() as block:

            @block.sync
            def _(sp):
                sp.dma_start(S0[:], dr["hgrn_s0"]).then_inc(s0_in, 16)
                sp.wait_ge(s_done, NCH)
                store(sp, dr, dr["out_hgrn_p"], S[:])
                sp.wait_ge(s_done, NCH + BH)
                store(sp, dr, dr["out_hgrn_s"], S0[:])
                sp.wait_ge(dr["stored"], 16 * dr["n_stored"])

            @block.scalar
            def _(act):
                act.activation(e[:], b[:], ACT.Exp).then_inc(eb_ready, 1)
                act.wait_ge(dk_ready, 1)
                act.activation(d[:], d[:], ACT.Exp).then_inc(dk_exp, 1)
                for c in range(NC9):
                    act.wait_ge(turned, c + 1)
                    if c >= 2:
                        act.wait_ge(dS_ready, c - 1)
                    act.activation(kt[:, c % 2, :, :], kps[0:CH, 0, :].rearrange("p (h n) -> p h n", h=BH), ACT.Copy)\
                       .then_inc(kt_ready, 1)
                    act.wait_ge(o_ready, c + 1)
                    act.activation(cat[:, 4:8, c * CH:(c + 1) * CH],
                                   o_in[:, c % 2, 0:BH * CH].rearrange("p (h n) -> p h n", h=BH), ACT.Copy)\
                       .then_inc(o_taken, 1)

            @block.vector
            def _(dve):
                last = b[:, :, 0:TP].rearrange("p h (c t) -> p h c t", t=CH)
                dve.tensor_tensor(d[:, :, 0:TP].rearrange("p h (c t) -> p h c t", t=CH),
                                  last[:, :, :, CH - 1:CH].to_broadcast([P, BH, NCH, CH]), last, ALU.subtract)
                last = b[:, :, TP:T].rearrange("p h (c t) -> p h c t", t=TS)
                dve.tensor_tensor(d[:, :, TP:T].rearrange("p h (c t) -> p h c t", t=TS),
                                  last[:, :, :, TS - 1:TS].to_broadcast([P, BH, NB, TS]), last, ALU.subtract)\
                   .then_inc(dk_ready, 1)
                dve.wait_ge(eb_ready, 1)
                dve.tensor_tensor(x[:], q[:], e[:], ALU.mult)
                dve.wait_ge(dk_exp, 1)
                dve.tensor_tensor(k[:], k[:], d[:], ALU.mult).then_inc(kd_ready, 1)
                for c in range(NCH):
                    dve.wait_ge(dS_ready, c + 1)
                    if c:
                        dve.wait_ge(o_ready, c + 1)
                    new = dps[:, 0, :].rearrange("p (h n) -> p h n", h=BH)
                    for h in range(BH):
                        if c == 0:
                            op = dve.tensor_copy(S[:, h, :], new[:, h, :])
                        else:
                            op = dve.scalar_tensor_tensor(
                                out=S[:, h, :], in0=S[:, h, :], scalar=e[:, h, (c + 1) * CH - 1:(c + 1) * CH],
                                in1=new[:, h, :], op0=ALU.mult, op1=ALU.add)
                    op.then_inc(s_done, 1)
                dve.wait_ge(s0_in, 16)
                for h in range(BH):
                    if h >= 2:
                        dve.wait_ge(dS_ready, NCH + 2 * (h - 1))
                    dve.tensor_tensor(vm[:, h % 2, :, :],
                                      v[:, NCH, h * P:(h + 1) * P].unsqueeze(1).to_broadcast([CH, NB, P]),
                                      cst["seq_mask"].unsqueeze(2).to_broadcast([CH, NB, P]), ALU.mult)\
                       .then_inc(vm_ready, 1)
                    if h == 0:
                        dve.wait_ge(o_ready, NC9)
                    ebl = e[:, h, TP:T].rearrange("p (b t) -> p b t", t=TS)[:, :, TS - 1:TS]
                    dve.tensor_tensor(S0[:, :, h, :], S0[:, :, h, :], ebl.to_broadcast([P, NB, P]), ALU.mult)
                    dve.drain()
                    for a in range(2):
                        dve.wait_ge(dS_ready, NCH + 2 * h + a + 1)
                        dst = S0[:, 4 * a:4 * a + 4, h, :]
                        op = dve.tensor_tensor(dst, dst, dps[:, 0, :].rearrange("p (b n) -> p b n", n=P), ALU.add)
                        op.then_inc(vm_used[a], 1)
                    dve.drain().then_inc(s_done, 1)

            @block.tensor
            def _(pe):
                pe.wait_ge(kd_ready, 1)
                pe.wait_ge(s0_in, 16)
                for c in range(NC9):
                    cols = slice(c * CH, (c + 1) * CH)
                    if c:
                        pe.wait_ge(kt_ready, c)
                    for h in range(BH):
                        last_t = pe.transpose(kps[0:CH, 0, h * P:(h + 1) * P], k[:, h, cols], cst["ident"])
                    last_t.then_inc(turned, 1)
                    if c >= 2:
                        pe.wait_ge(o_taken, c - 1)
                    if c:
                        pe.wait_ge(s_done, c)
                    for h in range(BH):
                        o = o_in[:, c % 2, h * CH:(h + 1) * CH]
                        last_o = pe.matmul(o, v[:, c, h * P:(h + 1) * P], A[:, h, c, :], start=True,
                                           stop=(c in (0, NCH)))
                        if 0 < c < NCH:
                            last_o = pe.matmul(o, S[:, h, :], x[:, h, cols], start=False, stop=True)
                        if c == NCH:
                            for bb in range(NB):
                                last_o = pe.matmul(o[:, bb * TS:(bb + 1) * TS], S0[:, bb, h, :],
                                                   x[:, h, TP + bb * TS:TP + (bb + 1) * TS],
                                                   start=False, stop=True, skip_group_check=True)
                    last_o.then_inc(o_ready, 1)
                    pe.wait_ge(kt_ready, c + 1)
                    if c < NCH:
                        for h in range(BH):
                            last_s = pe.matmul(dps[:, 0, h * P:(h + 1) * P], kt[:, c % 2, h, :],
                                               v[:, c, h * P:(h + 1) * P], start=True, stop=True)
                        last_s.then_inc(dS_ready, 1)
                for h in range(BH):
                    pe.wait_ge(vm_ready, h + 1)
                    for a in range(2):
                        if a:
                            pe.wait_ge(vm_used[0], h + 1)
                        elif h:
                            pe.wait_ge(vm_used[1], h)
                        pe.matmul(dps[:, 0, :], kt[:, NCH % 2, h, :],
                                  vm[:, h % 2, 4 * a:4 * a + 4, :].rearrange("p b n -> p (b n)"),
                                  start=True, stop=True).then_inc(dS_ready, 1)

    headnorm(nc, "hgn", cat[:, 4:8, :], BH, 1, cst["ident"], lambda c: cst["hgrn_norm"], cst["eps"])
    with Stage(nc, "hgg") as st:
        with st.block() as block:

            @block.vector
            def _(dve):
                dve.tensor_tensor(cat[:, 4:8, :], cat[:, 4:8, :], g[:], ALU.mult)



class Activities:

    def __init__(self, st, dr, layer, x, first_key, bufs, split):
        self.x, self.key0, self.bufs, self.split = x, first_key, bufs, split
        self.src = dr["peer_ut"][layer]
        self.dst = dr["activities"]
        self.ut = st.sb("ut", [P, bufs, UK, DC * P])
        self.s = st.sb("s", [P, bufs, UK, T])
        self.ps = st.ps("s_ps", [P, UK, 2, 512])
        self.u_in = [st.sem(f"u_in{k}") for k in range(bufs)]
        self.s_ready = st.sem("s_ready")
        self.gelued = st.sem("gelued")
        self.s_out = [st.sem(f"s_out{k}") for k in range(bufs)]
        self.u_split = st.sem("u_split")
        self.ut_split = st.sb("ut_split", [P, bufs, 2, UK, DC * P]) if split else None

    def _keys(self, sp, u):
        n = self.key0 + u * UK
        return bass.ds(n if isinstance(u, int) else sp.snap(n), UK)

    def load(self, sp, u, k, first):
        src = self.src[self._keys(sp, u)]
        if not first:
            if self.split:
                sp.wait_ge(self.u_split, u - self.bufs + 1)
            else:
                sp.wait_ge(self.s_ready, (u - self.bufs + 1) * UK)
        sp.dma_start(self.ut[:, k, :, :], src.rearrange("j p n -> p j n")).then_inc(self.u_in[k], 16)

    def store(self, sp, u, k):
        dst = self.dst[self._keys(sp, u)]
        sp.wait_ge(self.gelued, (u + 1) * UK)
        sp.dma_start(dst.rearrange("j p n -> p j n"), self.s[:, k, :, :]).then_inc(self.s_out[k], 16)

    def stored(self, sp, counts):
        for k, n in enumerate(counts):
            sp.wait_ge(self.s_out[k], n * 16)

    def split_weights(self, dve, u, i, k, first):
        if not first:
            dve.wait_ge(self.s_ready, (u - self.bufs + 1) * UK)
        dve.wait_ge(self.u_in[k], i * 16 + 16)
        for last in split_on(dve, self.ut_split[:, k].unsqueeze(2).rearrange("p a c j n -> p a c (j n)"),
                             self.ut[:, k].unsqueeze(1).rearrange("p c j n -> p c (j n)"), 1):
            last.then_inc(self.u_split, 1)

    def score(self, pe, u, i, k, j):
        if j == 0:
            if self.split:
                pe.wait_ge(self.u_split, u + 1)
            else:
                pe.wait_ge(self.u_in[k], i * 16 + 16)
        if not (isinstance(u, int) and u == 0):
            pe.wait_ge(self.gelued, u * UK + j + 1 - UK)
        for c in range(DC):
            cols = slice(c * P, (c + 1) * P)
            if self.split:
                last = multiply_split(pe, lambda a: self.ps[:, j, a, 0:HALF],
                                      lambda part: self.ut_split[:, k, part, j, cols],
                                      lambda part, a: self.x[:, part, c, a * HALF:(a + 1) * HALF],
                                      2, c == 0, c == DC - 1)
            else:
                for a in range(2):
                    last = pe.matmul(self.ps[:, j, a, 0:HALF], self.ut[:, k, j, cols],
                                     self.x[:, c, a * HALF:(a + 1) * HALF], start=(c == 0), stop=(c == DC - 1))
        last.then_inc(self.s_ready, 1)

    def gelu(self, act, u, i, k, j, first):
        if not first and j == 0:
            act.wait_ge(self.s_out[k], i * 16)
        act.wait_ge(self.s_ready, u * UK + j + 1)
        act.activation(halves(self.s[:, k, j, :]), self.ps[:, j, :, 0:HALF], ACT.Gelu_apprx_tanh)\
           .then_inc(self.gelued, 1)


def peer(nc, dr, cst, layer, norm, h):
    nm = f"p{layer}"
    with ExitStack() as outer:
        xn = outer.enter_context(nc.sbuf_tensor(f"{nm}_xn", [P, 2, DC, T], F32))
        with ExitStack() as middle:
            sel = middle.enter_context(nc.sbuf_tensor(f"{nm}_sel", [P, 3, TPAD], F32))
            with ExitStack() as inner:
                whole = inner.enter_context(nc.sbuf_tensor(f"{nm}_whole", [P, DC, T], F32))
                q = inner.enter_context(nc.sbuf_tensor(f"{nm}_q", [P, 2 * PH, TPAD], F32))
                with Linear(nc, f"{nm}q", dr["w_peer_q"][layer], DC, 2 * PH) as lin:
                    norm(1, layer, xn, whole, lin.start)
                    lin.run(xn, "act", lambda eng, o, res: eng.activation(
                        q[:, bass.ds(o, 1), 0:T].rearrange("p a (b n) -> p (a b) n", b=2), res, ACT.Copy))
                select_experts(nc, dr, cst, layer, nm, q, sel, whole)
            spread_gates(nc, dr, cst, layer, nm, sel, xn)
        all_experts(nc, dr, cst, layer, nm, xn, h)


def select_experts(nc, dr, cst, layer, nm, q, sel, x):
    NQ = 2 * PH
    with Stage(nc, f"{nm}s") as st:
        keys = st.sb("keys", [P, NQ, P])
        qs = st.sb("qs", [P, NQ, P])
        work = st.sb("work", [P, NQ, P])
        top = st.sb("top", [P, NQ, PK])
        topi = st.sb("topi", [P, NQ, PK], U32)
        topf = st.sb("topf", [P, NQ, PK])
        cand = st.sb("cand", [P, PH, PK * PK])
        work2 = work[:].rearrange("p (h c) n -> p h (c n)", c=2)
        sv = st.sb("sv", [P, PH, PK])
        pos = st.sb("pos", [P, PH, PK], U32)
        ab = st.sb("ab", [P, 2, PH, PK], U32)
        abf = st.sb("abf", [P, 2, PH, PK])
        eq = cand[:].rearrange("p h (k a) -> p h k a", a=PK)
        res = st.sb("res", [P, 3, PH, PK])
        sm = st.sb("sm", [P, PH])
        sc = st.ps("sc", [P, NQ, P])
        acts = Activities(st, dr, layer, x, 0, SEL_UNITS, False)
        tr = acts.ps[:, 0, 0, 0:3 * P].rearrange("p (n k) -> p n k", n=3)
        keys_in = st.sem("keys_in")
        padded = st.sem("padded")
        staged = st.sem("staged")
        scored = st.sem("scored")
        spare = st.sb("spare", [P, 1])
        sc_read = st.sem("sc_read")
        sv_ready = st.sem("sv_ready")
        gates_exp = st.sem("gates_exp")
        res_ready = st.sem("res_ready")
        turned = st.sem("turned")
        kept = st.sem("kept")

        def units(last):
            return SEL_UNITS - 1 if last else SEL_UNITS

        with st.block() as block:

            @block.sync
            def _(sp):
                sp.dma_start(keys[:], dr["peer_keys"][layer]).then_inc(keys_in, 16)

                def tile(t, first, last=False):
                    for k in range(units(last)):
                        u = t * SEL_UNITS + k
                        acts.load(sp, u, k, first)
                        if not (first and k == 0):
                            acts.store(sp, u - 1, (k - 1) % SEL_UNITS)

                looped(sp, NT - 1, tile)
                tile(NT - 1, False, True)
                acts.store(sp, NT * SEL_UNITS - 2, SEL_UNITS - 2)
                acts.stored(sp, [NT] * (SEL_UNITS - 1) + [NT - 1])

            @block.gpsimd
            def _(pool):
                pool.memset(q[:, :, T:TPAD], 0.0).then_inc(padded, 1)

            @block.scalar
            def _(act):
                act.wait_ge(padded, 1)

                def stage(t):
                    act.activation(qs[:], q[:, :, bass.ds(t * P, P)], ACT.Copy).then_inc(staged, 1)

                def tile(t, first, last=False):
                    for k in range(units(last)):
                        for j in range(UK):
                            acts.gelu(act, t * SEL_UNITS + k, t, k, j, first)
                        if k == 0 and not last:
                            act.wait_ge(scored, t + 1)
                            stage(t + 1)
                    act.wait_ge(sv_ready, t + 1)
                    act.activation(res[:, 2, :, :], sv[:], ACT.Exp).then_inc(gates_exp, 1)
                    act.wait_ge(turned, t + 1)
                    act.activation(sel[:, :, bass.ds(t * P, P)], tr, ACT.Copy).then_inc(kept, 1)

                stage(0)
                looped(act, NT - 1, tile)
                tile(NT - 1, False, True)

            @block.tensor
            def _(pe):
                pe.wait_ge(keys_in, 16)

                def score(t):
                    pe.wait_ge(staged, t + 1)
                    for n in range(NQ):
                        last = pe.matmul(sc[:, n, :], qs[:, n, :], keys[:, n, :], start=True, stop=True)
                    last.then_inc(scored, 1)

                def tile(t, first, last_tile=False):
                    if not first:
                        pe.wait_ge(kept, t)
                    for k in range(units(last_tile)):
                        for j in range(UK):
                            acts.score(pe, t * SEL_UNITS + k, t, k, j)
                    if not last_tile:
                        pe.wait_ge(sc_read, t + 1)
                        score(t + 1)
                    pe.wait_ge(acts.gelued, (t * SEL_UNITS + units(last_tile)) * UK)
                    pe.wait_ge(res_ready, t + 1)
                    for n in range(3):
                        last = pe.transpose(tr[:, n, :], res[:, n, :, :].rearrange("p h k -> p (h k)"), cst["ident"])
                    last.then_inc(turned, 1)

                score(0)
                looped(pe, NT - 1, tile)
                tile(NT - 1, False, True)

            @block.vector
            def _(dve):
                dve.memset(spare[:], 0.0)
                dve.drain()

                def tile(t, first):
                    wait_apart(dve, scored, t + 1, spare[:])
                    for n in range(NQ):
                        dve.max(top[:, n, 0:8], sc[:, n, :])
                    dve.drain()
                    for n in range(NQ):
                        dve.max_index(topi[:, n, 0:8], top[:, n, 0:8], sc[:, n, :])
                        last = dve.match_replace(work[:, n, :], top[:, n, 0:8], sc[:, n, :], -3e38)
                    last.then_inc(sc_read, 1)
                    dve.drain()
                    for n in range(NQ):
                        dve.max(top[:, n, 8:16], work[:, n, :])
                    dve.drain()
                    for n in range(NQ):
                        dve.max_index(topi[:, n, 8:16], top[:, n, 8:16], work[:, n, :])
                    dve.drain()
                    dve.tensor_copy(topf[:], topi[:])
                    pair = top[:].rearrange("p (h c) k -> p h c k", c=2)
                    dve.tensor_tensor(cand[:].rearrange("p h (a b) -> p h a b", b=PK),
                                      pair[:, :, 0, :].unsqueeze(3).to_broadcast([P, PH, PK, PK]),
                                      pair[:, :, 1, :].unsqueeze(2).to_broadcast([P, PH, PK, PK]), ALU.add)
                    dve.drain()
                    for n in range(PH):
                        dve.max(sv[:, n, 0:8], cand[:, n, :])
                    dve.drain()
                    for n in range(PH):
                        dve.max_index(pos[:, n, 0:8], sv[:, n, 0:8], cand[:, n, :])
                        dve.match_replace(work2[:, n, :], sv[:, n, 0:8], cand[:, n, :], -3e38)
                    dve.drain()
                    for n in range(PH):
                        dve.max(sv[:, n, 8:16], work2[:, n, :])
                    dve.drain()
                    for n in range(PH):
                        dve.max_index(pos[:, n, 8:16], sv[:, n, 8:16], work2[:, n, :])
                    dve.drain()
                    if not first:
                        dve.wait_ge(turned, t)
                    dve.tensor_tensor(sm[:].unsqueeze(2), sv[:, :, 0:1], sv[:, :, 0:1], ALU.max)
                    dve.tensor_scalar(ab[:, 0, :, :], pos[:], 4, None, ALU.logical_shift_right)
                    dve.tensor_scalar(ab[:, 1, :, :], pos[:], 15, None, ALU.bitwise_and)
                    dve.drain()
                    dve.tensor_tensor(sv[:], sv[:], sm[:].unsqueeze(2).to_broadcast([P, PH, PK]), ALU.subtract)\
                       .then_inc(sv_ready, 1)
                    dve.tensor_copy(abf[:], ab[:])
                    dve.drain()
                    iota = cst["iota"][:, 0:PK].unsqueeze(1).unsqueeze(1).to_broadcast([P, PH, PK, PK])
                    idx = topf[:].rearrange("p (h c) k -> p h c k", c=2)
                    for c in range(2):
                        dve.tensor_tensor(eq, iota, abf[:, c, :, :].unsqueeze(3).to_broadcast([P, PH, PK, PK]),
                                          ALU.is_equal)
                        dve.drain()
                        dve.tensor_tensor(eq, eq, idx[:, :, c, :].unsqueeze(2).to_broadcast([P, PH, PK, PK]), ALU.mult)
                        dve.drain()
                        dve.tensor_reduce(res[:, c, :, :], eq, AX, ALU.add)
                        dve.drain()
                    dve.wait_ge(gates_exp, t + 1)
                    dve.tensor_reduce(sm[:], res[:, 2, :, :], AX, ALU.add)
                    dve.drain()
                    dve.reciprocal(sm[:], sm[:])
                    dve.drain()
                    dve.tensor_tensor(res[:, 2, :, :], res[:, 2, :, :],
                                      sm[:].unsqueeze(2).to_broadcast([P, PH, PK]), ALU.mult)
                    dve.drain().then_inc(res_ready, 1)

                looped(dve, NT, tile)


def spread_gates(nc, dr, cst, layer, nm, sel, xn):
    NQ4 = TB // 4
    DEPTH = 4
    with Stage(nc, f"{nm}g") as st:
        cols = st.sb("cols", [P, 2, 3, TB])
        cols_p = st.sb("cols_p", [P, TB])
        spare = st.sb("spare", [P, NQ4])
        one_i = st.sb("one_i", [P, DEPTH, 4, P])
        one_j = st.sb("one_j", [P, DEPTH, 4, P])
        grid = st.sb("grid", [P, 2, P, TB])
        gp = st.ps("gp", [P, 2, 4, P])
        acts = Activities(st, dr, layer, xn, N_SEL, 2, True)
        i_ready = st.sem("i_ready")
        j_ready = st.sem("j_ready")
        multiplied = st.sem("multiplied")
        taken = st.sem("taken")
        grid_out = [st.sem(f"grid_out{k}") for k in range(2)]
        with st.block() as block:

            def hot_j(eng, c, r, w):
                return eng.tensor_scalar(one_j[:, r % DEPTH, w, :], cst["iota"], c[:, 4 * r + w:4 * r + w + 1],
                                         None, ALU.is_equal)

            @block.vector
            def _(dve):
                def batch(i, k, first):
                    tb = i * 2 + k
                    acts.split_weights(dve, tb, i, k, first)
                    dve.tensor_copy(cols[:, k, :, :], sel[:, :, bass.ds(tb * TB, TB)])
                    dve.drain()
                    for r in range(NQ4):
                        if not (first and k == 0 and r < DEPTH):
                            dve.wait_ge(multiplied, tb * NQ4 + r + 1 - DEPTH)
                        for w in range(4):
                            dve.tensor_scalar(one_i[:, r % DEPTH, w, :], cst["iota"],
                                              cols[:, k, 0, 4 * r + w:4 * r + w + 1],
                                              cols[:, k, 2, 4 * r + w:4 * r + w + 1], ALU.is_equal, ALU.mult)
                        for w in range(2):
                            last = hot_j(dve, cols[:, k, 1, :], r, w)
                        last.then_inc(i_ready, 1)

                paired(dve, NTB, batch)

            @block.gpsimd
            def _(pool):
                def batch(i, k, first):
                    tb = i * 2 + k
                    if first and k == 0:
                        pool.memset(spare[:], 0.0)
                    pool.tensor_copy(cols_p[:], sel[:, 1, bass.ds(tb * TB, TB)])
                    pool.drain()
                    for r in range(NQ4):
                        if not (first and k == 0 and r < DEPTH):
                            wait_apart(pool, multiplied, tb * NQ4 + r + 1 - DEPTH, spare[:, r:r + 1])
                        for w in range(2, 4):
                            last = hot_j(pool, cols_p, r, w)
                        last.then_inc(j_ready, 1)
                    pool.drain()

                paired(pool, NTB, batch)

            @block.tensor
            def _(pe):
                def batch(i, k, first):
                    tb = i * 2 + k
                    for r in range(NQ4):
                        if r % (NQ4 // UK) == 0:
                            acts.score(pe, tb, i, k, r // (NQ4 // UK))
                        n = tb * NQ4 + r
                        pe.wait_ge(i_ready, n + 1)
                        pe.wait_ge(j_ready, n + 1)
                        if not (first and k == 0 and r < 2):
                            pe.wait_ge(taken, n - 1)
                        for w in range(4):
                            last = pe.matmul(gp[:, r % 2, w, :], one_i[:, r % DEPTH, w, :], one_j[:, r % DEPTH, w, :],
                                             start=True, stop=True)
                        last.then_inc(multiplied, 1)

                paired(pe, NTB, batch)

            @block.scalar
            def _(act):
                def batch(i, k, first):
                    tb = i * 2 + k
                    for r in range(NQ4):
                        if r % (NQ4 // UK) == 0:
                            acts.gelu(act, tb, i, k, r // (NQ4 // UK), first)
                        if r == 0 and not first:
                            act.wait_ge(grid_out[k], i * 16)
                        act.wait_ge(multiplied, tb * NQ4 + r + 1)
                        act.activation(grid[:, k, :, 4 * r:4 * r + 4].rearrange("p j w -> p w j"), gp[:, r % 2, :, :],
                                       ACT.Copy).then_inc(taken, 1)

                paired(act, NTB, batch)

            @block.sync
            def _(sp):
                def grid_store(i, k, first):
                    tb = i * 2 + k
                    dst = dr["gates"][bass.ds(tb if first else sp.snap(tb), 1)]
                    sp.wait_ge(taken, tb * NQ4 + NQ4)
                    sp.dma_start(dst.rearrange("a p n -> p (a n)"), grid[:, k, :, :].rearrange("p j w -> p (j w)"))\
                      .then_inc(grid_out[k], 16)

                def batch(i, k, first):
                    tb = i * 2 + k
                    acts.load(sp, tb, k, first)
                    if k:
                        acts.store(sp, tb - 1, 0)
                        grid_store(i, 0, first)
                    elif not first:
                        acts.store(sp, tb - 1, 1)
                        grid_store(i - 1, 1, first)

                paired(sp, NTB, batch)
                acts.store(sp, NTB - 1, 1)
                grid_store(NTB // 2 - 1, 1, True)
                acts.stored(sp, [NTB // 2, NTB // 2])
                for k in range(2):
                    sp.wait_ge(grid_out[k], NTB // 2 * 16)


def all_experts(nc, dr, cst, layer, nm, xn, h):
    S = N_STORED
    with Stage(nc, f"{nm}e") as st:
        UR, VR = 2, DC // 2
        ut = st.sb("ut", [P, 2, JB, DC * P])
        u_parts = st.sb("u_parts", [P, UR, 2, DC * P])
        vt = st.sb("vt", [P, 2, JB, D])
        v_parts = st.sb("v_parts", [P, VR, 2, JB * P])
        act_s = st.sb("act_s", [P, JB, T])
        gt = st.sb("gt", [P, NTB, JB * TB])
        w = st.sb("w", [P, 2, 2, JB, T])
        s_ps = st.ps("s_ps", [P, 2, 2, 512])
        y_ps = st.ps("y_ps", [P, 2, 2, 512])
        u_in = [st.sem(f"u_in{k}") for k in range(2)]
        s_in = [st.sem(f"s_in{k}") for k in range(2)]
        v_in = [[st.sem(f"v_in{k}{a}") for a in range(2)] for k in range(2)]
        g_in = st.sem("g_in")
        u_high_ready = st.sem("u_high_ready")
        u_split = st.sem("u_split")
        v_high_ready = st.sem("v_high_ready")
        v_split = st.sem("v_split")
        s_ready = st.sem("s_ready")
        gelued = st.sem("gelued")
        gated = st.sem("gated")
        w_ready = st.sem("w_ready")
        y_ready = st.sem("y_ready")
        y_added = st.sem("y_added")
        assert S % 2 == 0

        def activities(k):
            return ut[:, k, :, :].rearrange("p j n -> p (j n)")[:, 0:JB * T].rearrange("p (j n) -> p j n", j=JB)

        def v_piece(k, c):
            return vt[:, k, :, c * P:(c + 1) * P]

        def v_part(c, part):
            return v_parts[:, c % VR, part, :].rearrange("p (j n) -> p j n", j=JB)

        with st.block() as block:

            @block.sync
            def _(sp):
                def load_gates(gs):
                    sp.dma_start(gt[:], gs.rearrange("b p n -> p b n")).then_inc(g_in, 16)

                def load(n, k, i, first, fresh):
                    static = isinstance(n, int)
                    m = n if static else sp.snap(n)
                    key = n * JB if static else sp.snap(n * JB)
                    us, ss = dr["peer_ut"][layer][bass.ds(key, JB)], dr["activities"][bass.ds(key, JB)]
                    vs = dr["peer_v"][layer][bass.ds(m, 1)].rearrange("a p (j d) -> p (a j) d", j=JB)
                    gs = dr["gates"][:, :, bass.ds(key * TB, JB * TB)]
                    if fresh:
                        if static and n < S + 2:
                            sp.wait_ge(w_ready, (n - 1) * JB)
                        else:
                            sp.wait_ge(u_split, (n - S - 1) * JB)
                        sp.dma_start(ut[:, k, :, :], us.rearrange("j p n -> p j n")).then_inc(u_in[k], 16)
                    else:
                        if not first:
                            sp.wait_ge(w_ready, (n - 1) * JB)
                        sp.dma_start(activities(k), ss.rearrange("j p n -> p j n")).then_inc(s_in[k], 16)
                    if first and k == 0:
                        load_gates(gs)
                    for a in range(2):
                        if not first:
                            sp.wait_ge(v_split, (n - 2) * DC + (a + 1) * DC // 2)
                        cols = slice(a * D // 2, (a + 1) * D // 2)
                        sp.dma_start(vt[:, k, :, cols], vs[:, :, cols]).then_inc(v_in[k][a], 16)
                    if not (first and k == 0):
                        sp.wait_ge(gated, n * JB)
                        load_gates(gs)

                def pair(i, first, fresh):
                    for k in range(2):
                        load(i * 2 + k, k, i, first, fresh)

                pair(0, True, False)
                with sp.Fori(1, S // 2) as i:
                    pair(i, False, False)
                pair(S // 2, False, True)
                with sp.Fori(S // 2 + 1, NJB // 2) as i:
                    pair(i, False, True)

            @block.tensor
            def _(pe):
                def score(n, k):
                    for j in range(JB):
                        m = (n - S) * JB + j
                        pe.wait_ge(u_split, m + 1)
                        if not (isinstance(n, int) and m < 2):
                            pe.wait_ge(gelued, m - 1)
                        for c in range(DC):
                            last = multiply_split(
                                pe, lambda a: s_ps[:, j % 2, a, 0:HALF],
                                lambda part: u_parts[:, j % UR, part, c * P:(c + 1) * P],
                                lambda part, a: xn[:, part, c, a * HALF:(a + 1) * HALF], 2, c == 0, c == DC - 1)
                        last.then_inc(s_ready, 1)

                def combine(n, k):
                    pe.wait_ge(w_ready, n * JB + JB)
                    for c in range(DC):
                        pe.wait_ge(v_split, n * DC + c + 1)
                        if not (isinstance(n, int) and n == 0 and c < 2):
                            pe.wait_ge(y_added, n * DC + c - 1)
                        for j in range(JB):
                            last = multiply_split(
                                pe, lambda a: y_ps[:, c % 2, a, 0:HALF],
                                lambda part: v_part(c, part)[:, j, :],
                                lambda part, a: w[:, k, part, j, a * HALF:(a + 1) * HALF], 2, j == 0, j == JB - 1)
                        last.then_inc(y_ready, 1)

                combine(0, 0)
                with pe.Fori(1, S // 2) as i:
                    combine(i * 2 - 1, 1)
                    combine(i * 2, 0)

                def both(i):
                    score(i * 2, 0)
                    combine(i * 2 - 1, 1)
                    score(i * 2 + 1, 1)
                    combine(i * 2, 0)

                both(S // 2)
                with pe.Fori(S // 2 + 1, NJB // 2) as i:
                    both(i)
                combine(NJB - 1, 1)

            def v_ahead(n, k, c):
                return (n, k, c + VR) if c < VR else (n + 1, 1 - k, c - VR)

            def u_ahead(n, k, j):
                return (n, k, j + UR) if j < UR else (n + 1, 1 - k, j - UR)

            @block.scalar
            def _(act):
                def v_high(n, k, c):
                    if c % (DC // 2) == 0:
                        act.wait_ge(v_in[k][c // (DC // 2)], (n - k) * 8 + 16)
                    take_high_act(act, v_part(c, HIGH), v_piece(k, c)).then_inc(v_high_ready, 1)

                def u_high(n, k, j):
                    if j == 0:
                        act.wait_ge(u_in[k], (n - k - S) * 8 + 16)
                    take_high_act(act, u_parts[:, j % UR, HIGH, :], ut[:, k, j, :]).then_inc(u_high_ready, 1)

                def gelus(n, k, last=False):
                    for j in range(JB):
                        if not (isinstance(n, int) and n == S):
                            act.wait_ge(w_ready, (n - 1) * JB + j + 1)
                        act.wait_ge(s_ready, (n - S) * JB + j + 1)
                        act.activation(halves(act_s[:, j, :]), s_ps[:, j % 2, :, 0:HALF],
                                       ACT.Gelu_apprx_tanh).then_inc(gelued, 1)
                        if not (last and j >= UR):
                            u_high(*u_ahead(n, k, j))

                def follow(n, k, last=False):
                    for c in range(DC):
                        if not (last and c >= VR):
                            act.wait_ge(y_ready, n * DC + c + 1)
                            v_high(*v_ahead(n, k, c))

                for c in range(VR):
                    v_high(0, 0, c)
                follow(0, 0)
                with act.Fori(1, S // 2 - 1) as i:
                    follow(i * 2 - 1, 1)
                    follow(i * 2, 0)
                follow(S - 3, 1)
                for j in range(UR):
                    u_high(S, 0, j)
                follow(S - 2, 0)

                def both(i):
                    gelus(i * 2, 0)
                    follow(i * 2 - 1, 1)
                    gelus(i * 2 + 1, 1)
                    follow(i * 2, 0)

                both(S // 2)
                with act.Fori(S // 2 + 1, NJB // 2 - 1) as i:
                    both(i)
                gelus(NJB - 2, 0)
                follow(NJB - 3, 1)
                gelus(NJB - 1, 1, True)
                follow(NJB - 2, 0)
                follow(NJB - 1, 1, True)

            @block.gpsimd
            def _(pool):
                def v_rest(n, k, c):
                    pool.wait_ge(v_high_ready, n * DC + c + 1)
                    leave_rest(pool, v_part(c, REST), v_piece(k, c), v_part(c, HIGH)).then_inc(v_split, 1)

                def u_rest(n, k, j):
                    pool.wait_ge(u_high_ready, (n - S) * JB + j + 1)
                    leave_rest(pool, u_parts[:, j % UR, REST, :], ut[:, k, j, :], u_parts[:, j % UR, HIGH, :])\
                        .then_inc(u_split, 1)

                def u_rests(n, k, last=False):
                    for j in range(JB):
                        if not (last and j >= UR):
                            u_rest(*u_ahead(n, k, j))

                def follow(n, k, last=False):
                    for c in range(DC):
                        if not (last and c >= VR):
                            v_rest(*v_ahead(n, k, c))

                for c in range(VR):
                    v_rest(0, 0, c)
                follow(0, 0)
                with pool.Fori(1, S // 2 - 1) as i:
                    follow(i * 2 - 1, 1)
                    follow(i * 2, 0)
                follow(S - 3, 1)
                for j in range(UR):
                    u_rest(S, 0, j)
                follow(S - 2, 0)

                def both(i):
                    u_rests(i * 2, 0)
                    follow(i * 2 - 1, 1)
                    u_rests(i * 2 + 1, 1)
                    follow(i * 2, 0)

                both(S // 2)
                with pool.Fori(S // 2 + 1, NJB // 2 - 1) as i:
                    both(i)
                u_rests(NJB - 2, 0)
                follow(NJB - 3, 1)
                u_rests(NJB - 1, 1, True)
                follow(NJB - 2, 0)
                follow(NJB - 1, 1, True)

            @block.vector
            def _(dve):
                def gate(j):
                    return gt[:].rearrange("p b (j n) -> p j b n", j=JB)[:, j]

                def weigh(n, k, i, j, fresh):
                    high, rest = w[:, k, HIGH, j, :], w[:, k, REST, j, :]
                    if j == 0:
                        dve.wait_ge(g_in, n * 16 + 16)
                    if fresh:
                        dve.wait_ge(gelued, (n - S) * JB + j + 1)
                        a = act_s[:, j, :]
                    else:
                        if j == 0:
                            dve.wait_ge(s_in[k], i * 16 + 16)
                        a = activities(k)[:, j, :]
                    by_batch = a.rearrange("p (b n) -> p b n", n=TB)
                    dve.tensor_tensor(by_batch, by_batch, gate(j), ALU.mult).then_inc(gated, 1)
                    dve.drain()
                    take_high(dve, high, a)
                    dve.drain()
                    leave_rest(dve, rest, a, high).then_inc(w_ready, 1)

                def add(n, c):
                    dve.wait_ge(y_ready, n * DC + c + 1)
                    dst = halves(h[:, c, :])
                    dve.tensor_tensor(dst, dst, y_ps[:, c % 2, :, 0:HALF], ALU.add).then_inc(y_added, 1)

                def step(n, k, i, fresh):
                    for c in range(DC):
                        add(n - 1, c)
                        if c < JB:
                            weigh(n, k, i, c, fresh)
                    dve.drain()

                for j in range(JB):
                    weigh(0, 0, 0, j, False)
                with dve.Fori(1, S // 2) as i:
                    step(i * 2 - 1, 1, i - 1, False)
                    step(i * 2, 0, i, False)
                step(S - 1, 1, S // 2 - 1, False)
                with dve.Fori(S // 2, NJB // 2) as i:
                    step(i * 2, 0, i, True)
                    step(i * 2 + 1, 1, i, True)
                for c in range(DC):
                    add(NJB - 1, c)



def ple(nc, dr, cst, layer, norm, h):
    with ExitStack() as ctx:
        xn = ctx.enter_context(nc.sbuf_tensor(f"ple{layer}_xn", [P, 2, DC, T], F32))
        gate = ctx.enter_context(nc.sbuf_tensor(f"ple{layer}_gate", [P, DC, T], F32))
        emb = ctx.enter_context(nc.sbuf_tensor(f"ple{layer}_emb", [P, 2, T], F32))
        early = ctx.enter_context(Stage(nc, f"ple{layer}i"))
        landed = early.sem("landed")
        gating = ctx.enter_context(Linear(nc, f"ple{layer}g", dr["w_ple_g"][layer], DC, DC))
        proj = ctx.enter_context(Linear(nc, f"ple{layer}p", dr["w_ple_p"][layer], 2, DC))

        def loads(sp):
            gating.start(sp)
            sp.dma_start(emb[:], dr["pT"][layer]).then_inc(landed, 16)
            proj.start(sp)

        norm(2, layer, xn, meanwhile=loads)
        gating.run(xn, "act", to_buffer(gate, func=ACT.Sigmoid))

        def evac(eng, o, res):
            buf = halves(at(gate, o))
            eng.tensor_tensor(buf, buf, res, ALU.mult)
            eng.drain()
            dst = at(h, o)
            return eng.tensor_tensor(dst, dst, at(gate, o), ALU.add)

        proj.run(emb, "dve", evac, is_split=False, x_landed=landed)



def bias_lines(nc, dr, cst):
    with Stage(nc, "bl") as st:
        rb = st.sb("rb", [33, H])
        rep = st.sb("rep", [33, H, P])
        hot = st.sb("hot", [33, BW])
        line = st.sb("line", [P, 2, BW])
        ps = st.ps("ps", [P, 2, 2, 512])
        landed = st.sem("landed")
        spread = st.sem("spread")
        multiplied = st.sem("multiplied")
        copied = st.sem("copied")
        written = [st.sem(f"written{k}") for k in range(2)]
        with st.block() as block:

            @block.sync
            def _(sp):
                sp.dma_start(rb[:], dr["rel_bias"]).then_inc(landed, 16)
                sp.dma_start(hot[:], dr["bucket_hot"]).then_inc(landed, 16)
                for n in range(H):
                    sp.wait_ge(copied, n + 1)
                    sp.dma_start(dr["bias_rows"][n], line[:, n % 2, :]).then_inc(written[n % 2], 16)
                for k in range(2):
                    sp.wait_ge(written[k], 16 * H // 2)

            @block.vector
            def _(dve):
                dve.wait_ge(landed, 32)
                dve.tensor_copy(rep[:], rb[:].unsqueeze(2).to_broadcast([33, H, P])).then_inc(spread, 1)

            @block.tensor
            def _(pe):
                pe.wait_ge(spread, 1)
                for n in range(H):
                    if n >= 2:
                        pe.wait_ge(copied, n - 1)
                    for a in range(2):
                        last = pe.matmul(ps[:, n % 2, a, 0:BW // 2], rep[:, n, :], hot[:, a * BW // 2:(a + 1) * BW // 2],
                                         start=True, stop=True)
                    last.then_inc(multiplied, 1)

            @block.scalar
            def _(act):
                for n in range(H):
                    act.wait_ge(multiplied, n + 1)
                    if n >= 2:
                        act.wait_ge(written[n % 2], 16 * (n // 2))
                    act.activation(line[:, n % 2, :].rearrange("p (a n) -> p a n", a=2), ps[:, n % 2, :, 0:BW // 2], ACT.Copy)\
                       .then_inc(copied, 1)


def attention(nc, dr, cst, qk, v, out):
    with ExitStack() as outer:
        lam = outer.enter_context(nc.sbuf_tensor("at_lam", [P, 4], F32))
        with Stage(nc, "al") as st:
            lv = st.sb("lv", [P, 4, CHD])
            pr = st.sb("pr", [P, 2, CHD])
            s2 = st.sb("s2", [P, 2])
            landed = st.sem("landed")
            summed = st.sem("summed")
            exped = st.sem("exped")
            with st.block() as block:

                @block.sync
                def _(sp):
                    sp.dma_start(lv[:], dr["c_lam"]).then_inc(landed, 16)
                    sp.wait_ge(landed, 16)

                @block.vector
                def _(dve):
                    dve.wait_ge(landed, 16)
                    dve.tensor_tensor(pr[:], lv[:, 0:2, :], lv[:, 2:4, :], ALU.mult)
                    dve.drain()
                    dve.tensor_reduce(s2[:], pr[:], AX, ALU.add).then_inc(summed, 1)
                    dve.wait_ge(exped, 1)
                    dve.tensor_tensor(lam[:, 0:1], s2[:, 0:1], s2[:, 1:2], ALU.subtract)
                    dve.drain()
                    dve.tensor_scalar(lam[:, 0:1], lam[:, 0:1], LAM_INIT, None, ALU.add)
                    dve.drain()
                    dve.tensor_scalar(lam[:, 1:2], lam[:, 0:1], -1.0, None, ALU.mult)
                    dve.drain()
                    dve.scalar_tensor_tensor(out=lam[:, 2:3], in0=cst["map_rows"][:, 1:2], scalar=lam[:, 1:2],
                                             in1=cst["map_rows"][:, 0:1], op0=ALU.mult, op1=ALU.add)

                @block.scalar
                def _(act):
                    act.wait_ge(summed, 1)
                    act.activation(s2[:], s2[:], ACT.Exp).then_inc(exped, 1)

        prompt_attention(nc, dr, cst, qk, v, out, lam)
        sample_attention(nc, dr, cst, qk, v, out, lam)


def prompt_attention(nc, dr, cst, qk, v, out, lam):
    NQB = TP // P

    def after(n, k, qb):
        return (n, k, qb + 1) if qb + 1 < NQB else (n + 1, 1 - k, 0)

    def before(n, k, qb):
        return (n, k, qb - 1) if qb else (n - 1, 1 - k, NQB - 1)

    def early(m, least):
        return isinstance(m, int) and m < least

    def steps(eng, start, stride, end):
        def head(n, k):
            for qb in range(NQB):
                here = (n, k, qb)
                static = isinstance(n, int)
                last = static and n == H - 1 and qb == NQB - 1
                stride(here, None if last else after(*here),
                       None if static and n == 0 and qb == 0 else before(*here))

        start(0, 0, 0)
        head(0, 0)
        head(1, 1)
        with eng.Fori(1, H // 2 - 1) as i:
            for k in range(2):
                head(i * 2 + k, k)
        head(H - 2, 0)
        head(H - 1, 1)
        end(H - 1, 1, NQB - 1)

    with Stage(nc, "pa") as st:
        qs = st.sb("qs", [P, 2, TP])
        ks = st.sb("ks", [P, 2, TP])
        vs = st.sb("vs", [P, 2, NQB, P])
        bias = st.sb("bias", [P, 2, TP])
        sc = st.sb("sc", [P, 2, 2, TP])
        mx = st.sb("mx", [P, 2, 2])
        sm = st.sb("sm", [P, 2, 2])
        a = st.sb("a", [P, 2, TP])
        at_ = st.sb("at", [P, 2, TP])
        s_ps = st.ps("s_ps", [P, 2, 2, 512])
        t_ps = st.ps("t_ps", [P, 2, 512])
        o_ps = st.ps("o_ps", [P, 2, 512])
        bias_in = [st.sem(f"bias_in{k}") for k in range(2)]
        staged = st.sem("staged")
        scored = st.sem("scored")
        sc_read = st.sem("sc_read")
        mx_ready = st.sem("mx_ready")
        exped = st.sem("exped")
        a_ready = st.sem("a_ready")
        turned = st.sem("turned")
        at_ready = st.sem("at_ready")
        o_ready = st.sem("o_ready")
        o_taken = st.sem("o_taken")
        with st.block() as block:

            @block.sync
            def _(sp):
                def load(i, k, first):
                    n = i * 2 + k
                    src = dr["bias_skew"][bass.ds(n if first else sp.snap(n), 1)]
                    if not first:
                        sp.wait_ge(sc_read, (n - 1) * NQB)
                    sp.dma_start(bias[:, k, :], src.rearrange("a p n -> p (a n)")).then_inc(bias_in[k], 16)

                for k in range(2):
                    load(0, k, True)
                store(sp, dr, dr["out_k"], qk[:, H:2 * H, :])
                store(sp, dr, dr["out_v"][:, 0:TP // P, :], v[:, 0:TP // P, :])
                store(sp, dr, dr["out_v"][0:NB * TS, TP // P, :], v[0:NB * TS, TP // P, :])
                with sp.Fori(1, H // 2) as i:
                    for k in range(2):
                        load(i, k, False)

            @block.gpsimd
            def _(pool):
                def stage(i, k, first):
                    n = i * 2 + k
                    if not first:
                        pool.wait_ge(o_ready, (n - 1) * NQB)
                    pool.tensor_copy(qs[:, k, :], qk[:, bass.ds(n, 1), 0:TP].rearrange("p a n -> p (a n)"))
                    pool.tensor_copy(ks[:, k, :], qk[:, bass.ds(n + H, 1), 0:TP].rearrange("p a n -> p (a n)"))
                    pool.tensor_copy(vs[:, k, :, :], v[:, 0:NQB, bass.ds(n * P, P)]).then_inc(staged, 1)

                paired(pool, H, stage)

            @block.tensor
            def _(pe):
                def score(n, k, qb):
                    m = n * NQB + qb
                    if qb == 0:
                        pe.wait_ge(staged, n + 1)
                    if not early(m, 2):
                        pe.wait_ge(sc_read, m - 1)
                    for c in range(2):
                        rows = slice(c * CHD, (c + 1) * CHD)
                        last = pe.matmul(s_ps[:, qb % 2, c, 0:(qb + 1) * P], qs[rows, k, qb * P:(qb + 1) * P],
                                         ks[rows, k, 0:(qb + 1) * P], start=True, stop=True)
                    last.then_inc(scored, 1)

                def turn(n, k, qb):
                    m = n * NQB + qb
                    pe.wait_ge(a_ready, m + 1)
                    if not early(m, 2):
                        pe.wait_ge(at_ready, m - 1)
                    for kb in range(qb + 1):
                        last = pe.transpose(t_ps[:, qb % 2, kb * P:(kb + 1) * P], a[:, qb % 2, kb * P:(kb + 1) * P],
                                            cst["ident"])
                    last.then_inc(turned, 1)

                def combine(n, k, qb):
                    m = n * NQB + qb
                    pe.wait_ge(at_ready, m + 1)
                    if not early(m, 2):
                        pe.wait_ge(o_taken, m - 1)
                    for kb in range(qb + 1):
                        last = pe.matmul(o_ps[:, qb % 2, 0:P], vs[:, k, kb, :], at_[:, qb % 2, kb * P:(kb + 1) * P],
                                         start=(kb == 0), stop=(kb == qb))
                    last.then_inc(o_ready, 1)

                def start(n, k, qb):
                    score(n, k, qb)
                    score(*after(n, k, qb))

                def stride(here, nxt, prev):
                    if nxt and not (isinstance(nxt[0], int) and nxt[0] == H - 1 and nxt[2] == NQB - 1):
                        score(*after(*nxt))
                    turn(*here)
                    if prev:
                        combine(*prev)

                steps(pe, start, stride, combine)

            @block.vector
            def _(dve):
                def read_scores(n, k, qb):
                    m = n * NQB + qb
                    w, z = (qb + 1) * P, qb % 2
                    if qb == 0:
                        dve.wait_ge(bias_in[k], (n - k) * 8 + 16)
                    dve.wait_ge(scored, m + 1)
                    for c in range(2):
                        last = dve.scalar_tensor_tensor(out=sc[:, z, c, 0:w], in0=s_ps[:, z, c, 0:w], scalar=CHD ** -0.5,
                                                        in1=bias[:, k, TP - w:TP], op0=ALU.mult, op1=ALU.add)
                    last.then_inc(sc_read, 1)
                    dve.drain()
                    dve.tensor_reduce(mx[:, z, :], sc[:, z, :, 0:w], AX, ALU.max, negate=True).then_inc(mx_ready, 1)

                def mix_maps(n, k, qb):
                    m = n * NQB + qb
                    w, z = (qb + 1) * P, qb % 2
                    dve.wait_ge(exped, m + 1)
                    dve.reciprocal(sm[:, z, :], sm[:, z, :])
                    dve.drain()
                    dve.tensor_scalar(sm[:, z, 1:2], sm[:, z, 1:2], lam[:, 1:2], None, ALU.mult)
                    if not early(m, 2):
                        dve.wait_ge(turned, m - 1)
                    dve.tensor_scalar(a[:, z, 0:w], sc[:, z, 0, 0:w], sm[:, z, 0:1], None, ALU.mult)
                    dve.drain()
                    dve.scalar_tensor_tensor(out=a[:, z, 0:w], in0=sc[:, z, 1, 0:w], scalar=sm[:, z, 1:2],
                                             in1=a[:, z, 0:w], op0=ALU.mult, op1=ALU.add).then_inc(a_ready, 1)

                def stride(here, nxt, prev):
                    if nxt:
                        read_scores(*nxt)
                    mix_maps(*here)
                    dve.drain()

                steps(dve, read_scores, stride, lambda n, k, qb: None)

            @block.scalar
            def _(act):
                def exponentiate(n, k, qb):
                    w, z = (qb + 1) * P, qb % 2
                    act.wait_ge(mx_ready, n * NQB + qb + 1)
                    for c in range(2):
                        last = act.activation(sc[:, z, c, 0:w], sc[:, z, c, 0:w], ACT.Exp,
                                              bias=mx[:, z, c:c + 1], accum_out=sm[:, z, c:c + 1])
                    last.then_inc(exped, 1)

                def keep_turned(n, k, qb):
                    m = n * NQB + qb
                    act.wait_ge(turned, m + 1)
                    if not early(m, 2):
                        act.wait_ge(o_ready, m - 1)
                    act.activation(at_[:, qb % 2, 0:(qb + 1) * P], t_ps[:, qb % 2, 0:(qb + 1) * P], ACT.Copy)\
                       .then_inc(at_ready, 1)

                def keep_output(n, k, qb):
                    act.wait_ge(o_ready, n * NQB + qb + 1)
                    act.activation(out[:, bass.ds(n, 1), qb * P:(qb + 1) * P].rearrange("p a n -> p (a n)"),
                                   o_ps[:, qb % 2, 0:P], ACT.Copy).then_inc(o_taken, 1)

                def stride(here, nxt, prev):
                    if nxt:
                        exponentiate(*nxt)
                    keep_turned(*here)
                    if prev:
                        keep_output(*prev)

                steps(act, exponentiate, stride, keep_output)


def sample_attention(nc, dr, cst, qk, v, out, lam):
    NP = PAST // PAGE
    with Stage(nc, "sa") as st:
        pages = st.sb("pages", [P, NB * NP], I32)
        pagef = st.sb("pagef", [P, NB * NP])
        rows = st.sb("rows", [P, NB * NP], U32)
        kc = st.sb("kc", [P, 2, NP, D])
        vc = st.sb("vc", [P, 2, NP, D])
        kt = st.sb("kt", [P, 2, H, PAST])
        qd = st.sb("qd", [P, H * (P + 16)])
        bpast = st.sb("bpast", [P, PAST + TS])
        bnew = st.sb("bnew", [P, NB * (NB * TS + TS)])
        sc = st.sb("sc", [P, PAST + NB * TS])
        mx = st.sb("mx", [P, 1])
        sm = st.sb("sm", [P, 1])
        a = st.sb("a", [P, PAST + NB * TS])
        at_ = st.sb("at", [P, 3, P])
        osb = st.sb("osb", [P, H, 2, TS])
        k_ps = st.ps("k_ps", [P, 2, 4, P])
        s_ps = st.ps("s_ps", [P, 2, 512])
        t_ps = st.ps("t_ps", [P, 3, P])
        o_ps = st.ps("o_ps", [P, H, 2, TS])
        landed = st.sem("landed")
        rows_ready = st.sem("rows_ready")
        qd_zero = st.sem("qd_zero")
        qd_ready = st.sem("qd_ready")
        k_turned = st.sem("k_turned")
        kt_ready = st.sem("kt_ready")
        scored = st.sem("scored")
        mx_ready = st.sem("mx_ready")
        exped = st.sem("exped")
        a_ready = st.sem("a_ready")
        turned = st.sem("turned")
        at_ready = st.sem("at_ready")
        o_ready = st.sem("o_ready")
        o_copied = st.sem("o_copied")
        o_taken = st.sem("o_taken")
        NG = NP * H // 4
        with st.block() as block:

            @block.sync
            def _(sp):
                sp.dma_start(pages[:], dr["pages"]).then_inc(landed, 16)
                for n in range(H):
                    for c in range(2):
                        sp.dma_start(bpast[n * 16 + c * TS:n * 16 + (c + 1) * TS, :], dr["bias_past"][n])\
                          .then_inc(landed, 16)
                sp.wait_ge(landed, 16 * (1 + 2 * H))
                sp.wait_ge(dr["stored"], 16 * dr["n_stored"])

            @block.gpsimd
            def _(pool):
                pool.memset(qd[:], 0.0).then_inc(qd_zero, 1)
                pool.memset(bnew[:], NEG).then_inc(qd_zero, 1)
                pool.wait_ge(rows_ready, 1)

                def fetch(b, dst, src, arrived):
                    for g in range(NP):
                        pool.indirect_dma_start(
                            dst[:, b % 2, g, :], None, dr[src],
                            bass.IndirectOffsetOnAxis(ap=rows[:, b * NP + g:b * NP + g + 1], axis=0))\
                            .then_inc(arrived[b % 2], 16)

                for b in range(NB + 1):
                    if b < NB:
                        if b >= 2:
                            pool.wait_ge(k_turned, (b - 1) * NG)
                        fetch(b, kc, "cache_k", dr["k_in"])
                    if b >= 1:
                        if b >= 3:
                            pool.wait_ge(o_ready, b - 2)
                        fetch(b - 1, vc, "cache_v", dr["v_in"])

            @block.vector
            def _(dve):
                dve.wait_ge(landed, 16 * (1 + 2 * H))
                dve.tensor_copy(pagef[:], pages[:])
                dve.drain()
                dve.tensor_scalar(pagef[:], pagef[:], float(PAGE), cst["part"], ALU.mult, ALU.add)
                dve.drain()
                dve.tensor_copy(rows[:], pagef[:]).then_inc(rows_ready, 1)
                dve.wait_ge(qd_zero, 2)
                dve.tensor_copy(
                    bnew[:].rearrange("p (b n) -> p b n", b=NB)[:, :, 0:TS],
                    bpast[:, PAST:PAST + TS].unsqueeze(1).to_broadcast([P, NB, TS]))
                dve.drain()

                def spread_queries(b):
                    for c in range(2):
                        r = slice(c * CHD, (c + 1) * CHD)
                        last = dve.tensor_copy(
                            qd[r, :].rearrange("p (h n) -> p h n", h=H)[:, :, c * TS:(c + 1) * TS],
                            qk[r, 0:H, TP + b * TS:TP + (b + 1) * TS])
                    last.then_inc(qd_ready, 1)

                spread_queries(0)
                for b in range(NB):
                    dve.wait_ge(scored, b + 1)
                    dve.scalar_tensor_tensor(out=sc[:, 0:PAST], in0=s_ps[:, 0, 0:PAST], scalar=CHD ** -0.5,
                                             in1=bpast[:, 0:PAST], op0=ALU.mult, op1=ALU.add)
                    dve.scalar_tensor_tensor(out=sc[:, PAST:], in0=s_ps[:, 1, 0:NB * TS], scalar=CHD ** -0.5,
                                             in1=bnew[:, b * NB * TS:(b + 1) * NB * TS], op0=ALU.mult, op1=ALU.add)
                    dve.drain()
                    dve.tensor_reduce(mx[:], sc[:], AX, ALU.max, negate=True).then_inc(mx_ready, 1)
                    if b + 1 < NB:
                        spread_queries(b + 1)
                    dve.wait_ge(exped, b + 1)
                    dve.reciprocal(sm[:], sm[:])
                    dve.drain()
                    dve.tensor_scalar(sm[:], sm[:], lam[:, 2:3], None, ALU.mult)
                    dve.drain()
                    dve.tensor_scalar(a[:], sc[:], sm[:], None, ALU.mult).then_inc(a_ready, 1)
                    dve.wait_ge(o_copied, b + 1)
                    dve.tensor_tensor(out[:, :, TP + b * TS:TP + (b + 1) * TS], osb[:, :, 0, :], osb[:, :, 1, :], ALU.add)\
                       .then_inc(o_taken, 1)

            @block.scalar
            def _(act):
                def keep_keys(b):
                    for g in range(NG):
                        act.wait_ge(k_turned, b * NG + g + 1)
                        if b >= 2 and g == 0:
                            act.wait_ge(scored, b - 1)
                        page, h0 = g // 2, (g % 2) * 4
                        act.activation(kt[:, b % 2, h0:h0 + 4, page * PAGE:(page + 1) * PAGE], k_ps[:, g % 2, :, :],
                                       ACT.Copy).then_inc(kt_ready, 1)

                keep_keys(0)
                for b in range(NB):
                    act.wait_ge(mx_ready, b + 1)
                    act.activation(sc[:], sc[:], ACT.Exp, bias=mx[:], accum_out=sm[:]).then_inc(exped, 1)
                    if b + 1 < NB:
                        keep_keys(b + 1)
                    act.wait_ge(turned, b + 1)
                    act.activation(at_[:, 0:2, :], t_ps[:, 0:2, :], ACT.Copy)
                    act.activation(at_[0:NB * TS, 2, :], t_ps[0:NB * TS, 2, :], ACT.Copy).then_inc(at_ready, 1)
                    act.wait_ge(o_ready, b + 1)
                    if b:
                        act.wait_ge(o_taken, b)
                    act.activation(osb[:], o_ps[:], ACT.Copy).then_inc(o_copied, 1)

            @block.tensor
            def _(pe):
                NK = NB * TS

                def turn_keys(b):
                    pe.wait_ge(dr["k_in"][b % 2], 16 * NP * (b // 2 + 1))
                    for g in range(NG):
                        n = b * NG + g
                        if n >= 2:
                            pe.wait_ge(kt_ready, n - 1)
                        for j in range(4):
                            hh = (g % 2) * 4 + j
                            last = pe.transpose(k_ps[:, g % 2, j, :], kc[:, b % 2, g // 2, hh * P:(hh + 1) * P], cst["ident"])
                        last.then_inc(k_turned, 1)

                turn_keys(0)
                for b in range(NB):
                    pe.wait_ge(kt_ready, (b + 1) * NG)
                    pe.wait_ge(qd_ready, b + 1)
                    if b:
                        pe.wait_ge(a_ready, b)
                    for n in range(H):
                        pe.matmul(s_ps[:, 0, 0:PAST], qd[:, n * P:(n + 1) * P], kt[:, b % 2, n, :],
                                  start=(n == 0), stop=(n == H - 1))
                    for n in range(H):
                        last = pe.matmul(s_ps[:, 1, 0:NK], qd[:, n * P:(n + 1) * P], qk[:, H + n, TP:T],
                                         start=(n == 0), stop=(n == H - 1))
                    last.then_inc(scored, 1)
                    if b + 1 < NB:
                        turn_keys(b + 1)
                    pe.wait_ge(a_ready, b + 1)
                    for n in range(2):
                        pe.transpose(t_ps[:, n, :], a[:, n * P:(n + 1) * P], cst["ident"])
                    pe.transpose(t_ps[0:NK, 2, :], a[:, PAST:PAST + NK], cst["ident"]).then_inc(turned, 1)
                    pe.wait_ge(at_ready, b + 1)
                    pe.wait_ge(dr["v_in"][b % 2], 16 * NP * (b // 2 + 1))
                    if b:
                        pe.wait_ge(o_copied, b)
                    for n in range(H):
                        cols = slice(n * 16, (n + 1) * 16)
                        o = o_ps[:, n, :, :].rearrange("p c t -> p (c t)")
                        for g in range(NP):
                            pe.matmul(o, vc[:, b % 2, g, n * P:(n + 1) * P], at_[:, g, cols], start=(g == 0), stop=False)
                        last = pe.matmul(o, v[0:NK, TP // P, n * P:(n + 1) * P], at_[0:NK, 2, cols], start=False, stop=True)
                    last.then_inc(o_ready, 1)



CONST_COLS = dict(gains=48, s5_d=4, s5_glu_b=4, hgrn_norm=1, qk_norm=2, subln=1)


def program(nc, dr, upto=99, dumps=None):
    with ExitStack() as ctx:
        def sb(name, shape, dt=F32):
            return ctx.enter_context(nc.sbuf_tensor(name, shape, dt))

        h = sb("h", [P, DC, T])
        small = sb("small", [P, sum(CONST_COLS.values())])
        ident = sb("ident", [P, P])
        ones = sb("ones", [P, P])
        iota = sb("iota", [P, P])
        part = sb("part", [P, 1])
        map_rows = sb("map_rows", [P, 2])
        eps = sb("eps", [P, 1])
        cst = dict(ident=ident[:], ones=ones[:], iota=iota[:], part=part[:], eps=eps[:],
                   map_rows=map_rows[:])
        col = 0
        for name, n in CONST_COLS.items():
            cst[name] = small[:, col:col + n]
            col += n
        dr["stored"] = nc.alloc_semaphore("stored")
        dr["n_stored"] = 0
        dr["k_in"] = [nc.alloc_semaphore(f"k_in{k}") for k in range(2)]
        dr["v_in"] = [nc.alloc_semaphore(f"v_in{k}") for k in range(2)]

        with Stage(nc, "init") as st:
            landed = st.sem("landed")
            with st.block() as block:

                @block.sync
                def _(sp):
                    sp.dma_start(h[:], dr["xT"]).then_inc(landed, 16)
                    for dst, src in ((small, "small"), (ident, "ident"), (map_rows, "map_rows"),
                                     (iota, "iota"), (part, "part")):
                        sp.dma_start(dst[:], dr[src]).then_inc(landed, 16)
                    sp.wait_ge(landed, 6 * 16)

                @block.vector
                def _(dve):
                    dve.memset(ones[:], 1.0)
                    dve.memset(eps[:], EPS)
                    dve.wait_ge(landed, 6 * 16)
                    dve.tensor_scalar(cst["subln"], cst["subln"], 1.0 - LAM_INIT, None, ALU.mult)

        def gain(kind, layer):
            n = (kind * 2 + layer) * DC
            return cst["gains"][:, n:n + DC]

        def norm(kind, layer, out, whole=None, meanwhile=None):
            rmsnorm(nc, f"n{kind}{layer}", h, out, whole, gain(kind, layer), cst["ones"], cst["eps"], meanwhile)

        def parts(ctx, name):
            return ctx.enter_context(nc.sbuf_tensor(name, [P, 2, DC, T], F32))

        def dump(name, buf):
            if dumps is not None and name in dumps:
                with Stage(nc, "d" + name) as st:
                    with st.block() as block:

                        @block.sync
                        def _(sp):
                            store(sp, dr, dumps[name], buf[:])
                            sp.wait_ge(dr["stored"], 16 * dr["n_stored"])

        if upto >= 1:
            with ExitStack() as c0:
                whole = c0.enter_context(nc.sbuf_tensor("xn_whole", [P, DC, T], F32))
                cat = c0.enter_context(nc.sbuf_tensor("cat", [P, DC, T], F32))
                with ExitStack() as c1:
                    u = c1.enter_context(nc.sbuf_tensor("u", [P, 4, T], F32))
                    seg = c1.enter_context(nc.sbuf_tensor("seg_mask", [P, L5], F32))
                    cst["seg_mask"] = seg[:]
                    with Stage(nc, "seg") as st:
                        with st.block() as block:

                            @block.vector
                            def _(dve):
                                dve.memset(seg[:], 1.0)
                                dve.drain()
                                dve.memset(seg[:, TP:L5].rearrange("p (b e) -> p b e", e=SEG)[:, :, 0:1], 0.0)

                    with ExitStack() as c2:
                        xn = parts(c2, "xn_s5")
                        with Linear(nc, "inu", dr["w_in_u"], DC, 4) as lin:
                            norm(0, 0, xn, whole, lin.start)
                            lin.run(xn, "act", to_buffer(u))
                    s5(nc, dr, cst, u, cat)
                with ExitStack() as c1:
                    qfg = c1.enter_context(nc.sbuf_tensor("hg_qfg", [P, 3 * BH, T], F32))
                    q, f, g = [qfg[:, n * BH:(n + 1) * BH, :] for n in range(3)]
                    v = c1.enter_context(nc.sbuf_tensor("hg_v", [CH, NCH + 1, BH * P], F32))
                    chunk_mask = c1.enter_context(nc.sbuf_tensor("chunk_mask", [P, BH * T], F32))
                    level_mask = c1.enter_context(nc.sbuf_tensor("level_mask", [CH, 7, CH], F32))
                    seq_mask = c1.enter_context(nc.sbuf_tensor("seq_mask", [CH, NB], F32))
                    cst.update(chunk_mask=chunk_mask[:], level_mask=level_mask[:], seq_mask=seq_mask[:])
                    with ExitStack() as c2:
                        xn = parts(c2, "xn_hgrn")
                        with Stage(nc, "hgm") as st:
                            landed = st.sem("landed")
                            high_ready = st.sem("high_ready")
                            with st.block() as block:

                                @block.sync
                                def _(sp):
                                    sp.dma_start(level_mask[:], dr["level_mask"]).then_inc(landed, 16)
                                    sp.dma_start(seq_mask[:], dr["seq_mask"]).then_inc(landed, 16)
                                    sp.wait_ge(landed, 32)

                                @block.vector
                                def _(dve):
                                    for c in range(DC):
                                        take_high(dve, xn[:, HIGH, c, :], whole[:, c, :]).then_inc(high_ready, 1)
                                    dve.memset(chunk_mask[:], 1.0)
                                    dve.drain()
                                    m = chunk_mask[:].rearrange("p (h n) -> p h n", h=BH)
                                    for cols, n in ((slice(0, TP), CH), (slice(TP, T), TS)):
                                        starts = m[:, :, cols].rearrange("p h (c t) -> p h c t", t=n)[:, :, :, 0:1]
                                        dve.memset(starts, 0.0)

                                @block.gpsimd
                                def _(pool):
                                    for c in range(DC):
                                        pool.wait_ge(high_ready, c + 1)
                                        leave_rest(pool, xn[:, REST, c, :], whole[:, c, :], xn[:, HIGH, c, :])

                        linear(nc, "inqfg", dr["w_in_qfg"], DC, 3 * BH, xn, "act", to_buffer(qfg))
                        linear_by_token(nc, "inv", dr["w_in_i"], BH * P, xn, v, CH, NCH + 1)
                    if upto >= 2:
                        hgrn(nc, dr, cst, q, f, g, v, cat)
                if upto >= 2:
                    dump("cat", cat)
                if upto >= 3:
                    linear(nc, "outab", dr["w_out_ab"], DC, DC, cat, "dve", add_to(h), is_split=False)
        dump("h0", h)
        if upto >= 4:
            peer(nc, dr, cst, 0, norm, h)
            dump("h1", h)
        if upto >= 5:
            ple(nc, dr, cst, 0, norm, h)
            dump("h2", h)
        if upto >= 6:
            bias_lines(nc, dr, cst)
            with ExitStack() as c0:
                o = c0.enter_context(nc.sbuf_tensor("att_o", [P, H, T], F32))
                with ExitStack() as c1:
                    qk = c1.enter_context(nc.sbuf_tensor("qk", [P, 2 * H, T], F32))
                    v = c1.enter_context(nc.sbuf_tensor("att_v", [P, NT, D], F32))
                    with ExitStack() as c2:
                        xn = parts(c2, "xn_att")
                        with Linear(nc, "inqk", dr["w_in_qk"], DC, 2 * H) as lin:
                            norm(0, 1, xn, meanwhile=lin.start)
                            lin.run(xn, "act", to_buffer(qk))
                        for a in range(2):
                            cols = slice(a * D // 2, (a + 1) * D // 2)
                            linear_by_token(nc, f"incv{a}", dr["w_in_v"][:, :, cols], D // 2, xn, v[:, :, cols], P, NT)
                    headnorm(nc, "qkn", qk, 2 * H, 2, cst["ident"],
                             lambda c: cst["qk_norm"][:, c // H:c // H + 1], cst["eps"])
                    attention(nc, dr, cst, qk, v, o)
                with Linear(nc, "outc", dr["w_out_c"], DC, DC) as lin:
                    headnorm(nc, "sub", o, H, 1, cst["ident"], lambda c: cst["subln"], cst["eps"], lin.start)
                    lin.run(o, "dve", add_to(h), is_split=False)
            dump("h3", h)
        if upto >= 7:
            peer(nc, dr, cst, 1, norm, h)
            dump("h4", h)
            ple(nc, dr, cst, 1, norm, h)
        with nc.Block() as block:

            @block.sync
            def _(sp):
                store(sp, dr, dr["out_y"], h[:])
                sp.wait_ge(dr["stored"], 16 * dr["n_stored"])



def level_masks():
    m = np.zeros((CH, 7, CH), np.float32)
    s, t = np.meshgrid(np.arange(CH), np.arange(CH), indexing="ij")
    m[:, 0] = s == t
    for n, w in enumerate((32, 16, 8, 4, 2, 1)):
        m[:, n + 1] = (s // (2 * w) == t // (2 * w)) & (s % (2 * w) < w) & (t % (2 * w) >= w)
    return m


def bucket_table():
    hot = np.zeros((33, BW), np.float32)
    for x in range(BW):
        n = 511 - x
        if n < 0:
            hot[32, x] = NEG
            n = 0
        if n < 16:
            b = n
        else:
            b = min(31, 16 + int(math.log(n / 16) / math.log(128 / 16) * 16 + 1e-9))
        hot[b, x] = 1.0
    return hot


def columns(a):
    return np.ascontiguousarray(a.reshape(-1, P).T)


def packed(w):
    i, o = w.shape
    return np.ascontiguousarray(w.reshape(i // P, P, o // P, P).transpose(2, 1, 0, 3)).reshape(o // P, P, i)


def by_rows(w):
    return np.ascontiguousarray(w.reshape(-1, P, w.shape[1]).transpose(1, 0, 2))


def lay_out(z):
    z = {k: np.asarray(v) for k, v in z.items()}
    d = {}
    x = np.concatenate([z["x_prompt"].reshape(TP, D), z["x_sample"].reshape(NB * TS, D)])
    d["xT"] = np.ascontiguousarray(x.T.reshape(DC, P, T).transpose(1, 0, 2))
    p = np.concatenate([z["p_prompt"].reshape(2, TP, -1), z["p_sample"].reshape(2, NB * TS, -1)], axis=1)
    d["pT"] = np.ascontiguousarray(p.transpose(0, 2, 1).reshape(2, 2, P, T).transpose(0, 2, 1, 3))
    d["small"] = np.concatenate([
        columns(z["norm_mix"]), columns(z["norm_ffn"]), columns(z["norm_ple"]),
        columns(z["s5_d"]), columns(z["s5_glu_b"]), columns(z["hgrn_norm"]),
        columns(z["c_q_norm"]), columns(z["c_k_norm"]), columns(z["c_subln"])], axis=1)
    w = dict(zip("uqfig", np.split(z["w_in_ab"][0], 5, axis=1)))
    d["w_in_u"] = packed(w["u"])
    d["w_in_qfg"] = np.concatenate([packed(w[n]) for n in "qfg"])
    d["w_in_i"] = by_rows(w["i"])
    d["w_out_ab"] = packed(z["w_out_ab"][0])
    d["w_glu"] = packed(z["s5_glu_w"][0])
    d["w_in_qk"] = packed(z["w_in_c"][0][:, :2 * D])
    d["w_in_v"] = by_rows(z["w_in_c"][0][:, 2 * D:])
    d["w_out_c"] = packed(z["w_out_c"][0])
    d["w_peer_q"] = np.stack([packed(z["peer_wq"][i]) for i in range(2)])
    d["w_ple_g"] = np.stack([packed(z["ple_gate"][i]) for i in range(2)])
    d["w_ple_p"] = np.stack([packed(z["ple_proj"][i]) for i in range(2)])
    d["peer_keys"] = np.ascontiguousarray(z["peer_keys"].reshape(2, 16, P, P).transpose(0, 3, 1, 2))
    u = z["peer_u"].reshape(2, P, P, DC, P)
    d["peer_ut"] = np.ascontiguousarray(u.transpose(0, 2, 4, 3, 1)).reshape(2, P, P, DC * P)
    v = z["peer_v"].reshape(2, P, NJB, JB * D)
    d["peer_v"] = np.ascontiguousarray(v.transpose(0, 2, 1, 3))
    ldt = np.repeat(z["s5_log_dt"].reshape(16, 2), 64, axis=1)
    d["s5_par"] = np.ascontiguousarray(np.stack(
        [z["s5_a_re"].reshape(16, P), z["s5_a_im"].reshape(16, P), ldt]).transpose(2, 0, 1))
    b = np.zeros((P, 2, 16, P), np.float32)
    c = np.zeros((P, 2, 16, P), np.float32)
    for r, (bn, cn) in enumerate((("s5_b_re", "s5_c_re"), ("s5_b_im", "s5_c_im"))):
        for g in range(32):
            rows, cols = slice(64 * (g % 2), 64 * (g % 2) + 64), slice(16 * (g % 8), 16 * (g % 8) + 16)
            b[rows, r, g // 2, cols] = z[bn][0, g]
            c[rows, r, g // 2, cols] = z[cn][0, g].T
    d["s5_b"], d["s5_c"] = b, c
    h0 = np.stack([z["state_s5_re"][0], z["state_s5_im"][0]])
    d["s5_h0"] = np.ascontiguousarray(h0.reshape(2, NB, 16, P).transpose(3, 0, 2, 1))
    d["hgrn_lb"] = np.ascontiguousarray(z["hgrn_lower_bounds"].reshape(2, BH, P).transpose(2, 1, 0))
    d["hgrn_s0"] = np.ascontiguousarray(z["state_hgrn"][0].transpose(2, 0, 1, 3))
    lam = np.stack([z["c_lam_q1"][0], z["c_lam_q2"][0], z["c_lam_k1"][0], z["c_lam_k2"][0]])
    d["c_lam"] = np.ascontiguousarray(np.broadcast_to(lam, (P, 4, CHD)))
    d["rel_bias"] = np.concatenate([z["rel_bias"], np.ones((1, H), np.float32)])
    d["pages"] = np.ascontiguousarray(np.broadcast_to(z["page_table"].reshape(1, -1), (P, 16))).astype(np.int32)
    d["cache_k"] = z["cache_k"][0].reshape(-1, D)
    d["cache_v"] = z["cache_v"][0].reshape(-1, D)
    d["ident"] = np.eye(P, dtype=np.float32)
    d["iota"] = np.broadcast_to(np.arange(P, dtype=np.float32), (P, P)).copy()
    d["part"] = np.arange(P, dtype=np.float32)[:, None].copy()
    second = (np.arange(P) // TS) % 2
    d["map_rows"] = np.stack([1 - second, second], axis=1).astype(np.float32)
    d["level_mask"] = level_masks()
    d["seq_mask"] = (np.arange(CH)[:, None] // TS == np.arange(NB)[None]).astype(np.float32)
    d["bucket_hot"] = bucket_table()
    return d


OUTPUTS = {
    "out_y": (P, DC, T), "out_s5": (P, 2, 16, 1 + NB), "out_hgrn_p": (P, BH, P), "out_hgrn_s": (P, NB, BH, P),
    "out_k": (P, H, T), "out_v": (P, NT, D),
}


def declare(nc, arrays):
    dr = {}
    for name, a in arrays.items():
        dr[name] = nc.dram_tensor(f"{name}_dram", a.shape, mybir.dt.from_np(a.dtype), kind="ExternalInput").ap()
    for name, shape in OUTPUTS.items():
        dr[name] = nc.dram_tensor(name, shape, F32, kind="ExternalOutput").ap()
    dr["gates"] = nc.dram_tensor("gates", (NTB, P, P * TB), F32, kind="Internal").ap()
    dr["activities"] = nc.dram_tensor("activities", (P, P, T), F32, kind="Internal").ap()
    rows = nc.dram_tensor("bias_rows", (H, P, BW), F32, kind="Internal")
    dr["bias_rows"] = rows.ap()
    dr["bias_skew"] = bass.AP(rows, P - 1, [[P * BW, H], [BW - 1, P], [1, TP]])
    dr["bias_past"] = [bass.AP(rows, n * P * BW + PAST - 1, [[BW - 1, TS], [1, PAST + TS]]) for n in range(H)]
    return dr


def gather_outputs(r):
    y = r["out_y"].transpose(2, 1, 0).reshape(T, D)
    s5e = r["out_s5"].transpose(1, 3, 2, 0).reshape(2, 1 + NB, 32, 64)
    k = r["out_k"].transpose(2, 1, 0)
    v = r["out_v"].transpose(1, 0, 2).reshape(TPAD, H, P)
    hs = r["out_hgrn_s"].transpose(1, 2, 0, 3)
    c = np.ascontiguousarray
    return (c(y[:TP]).reshape(1, TP, D), c(y[TP:]).reshape(NB, TS, D),
            c(s5e[0, :1])[None], c(s5e[1, :1])[None], c(r["out_hgrn_p"].transpose(1, 0, 2))[None, None],
            c(k[:TP])[None, None], c(v[:TP])[None, None],
            c(s5e[0, 1:])[None], c(s5e[1, 1:])[None], c(hs)[None],
            c(k[TP:]).reshape(1, NB, TS, H, P), c(v[TP:T]).reshape(1, NB, TS, H, P))


def kernel(**inputs):
    import concourse.bacc as _bacc
    from concourse.bass_utils import run_bass_kernel_spmd as _run

    arrays = lay_out(inputs)
    nc = _bacc.Bacc("TRN2", target_bir_lowering=False, num_devices=1)
    program(nc, declare(nc, arrays))
    r = _run(nc, [{f"{name}_dram": a for name, a in arrays.items()}], core_ids=[0])
    return gather_outputs(r.results[0])
```
